# Optimizing a Trainium2 kernel written in Bass

```python
import math
import jax, jax.numpy as jnp
from jax import lax
import numpy as np

D_MODEL = 1024
BATCH = 1
SEQ = 1024
DEPTH = 2

GRID_W = 64
CTX_LEN = 256
N_MIXERS = 4
ATT_HEADS = 8
ATT_DK = 64
ATT_DV = 2 * ATT_DK
ATT_QK_WIDTH = ATT_HEADS * 2 * ATT_DK
ATT_WIDTH = ATT_HEADS * ATT_DV
Q_BLOCK = 128
ROPE_BASE = 10000.0
CONF_WIDTH = D_MODEL
CONF_KW = 31
SC_WIDTH = D_MODEL
SC_KW = 3
POOL_WIDTH = D_MODEL
POOL_WINDOWS = (2, 4, 8, 16)
POOL_GROUP = POOL_WIDTH // len(POOL_WINDOWS)
DEEPNORM_ALPHA = (2 * DEPTH) ** 0.25
DEEPNORM_BETA = (8 * DEPTH) ** -0.25
LN_EPS = 1e-5

kernel_name = "hybrid_interleaved_diffusion_block"

def _layers_of_kind(kind):
    return len(range(kind, DEPTH, N_MIXERS))

def layer_norm(x, g, b):
    xf = x.astype(jnp.float32)
    mu = jnp.mean(xf, axis=-1, keepdims=True)
    var = jnp.mean(jnp.square(xf - mu), axis=-1, keepdims=True)
    y = (xf - mu) * lax.rsqrt(var + LN_EPS)
    return (y * g.astype(jnp.float32) + b.astype(jnp.float32)).astype(x.dtype)

def rms_norm(x, g):
    xf = x.astype(jnp.float32)
    y = xf * lax.rsqrt(jnp.mean(jnp.square(xf), axis=-1, keepdims=True) + LN_EPS)
    return (y * g.astype(jnp.float32)).astype(x.dtype)

def axial_rope_tables(length, dim):
    half = dim // 2
    inv = 1.0 / (ROPE_BASE ** (jnp.arange(0, half, 2, dtype=jnp.float32) / half))
    t = jnp.arange(length, dtype=jnp.int32)
    row, col = jnp.divmod(t, GRID_W)
    ar = row.astype(jnp.float32)[:, None] * inv[None, :]
    ac = col.astype(jnp.float32)[:, None] * inv[None, :]
    ang = jnp.concatenate([ar, ar, ac, ac], axis=-1)
    return jnp.cos(ang), jnp.sin(ang)

def rotate_half_axial(x):
    x0, x1, x2, x3 = jnp.split(x, 4, axis=-1)
    return jnp.concatenate([-x1, x0, -x3, x2], axis=-1)

def apply_rope(x, cos, sin):
    cos = cos[:, None, None, :].astype(x.dtype)
    sin = sin[:, None, None, :].astype(x.dtype)
    return x * cos + rotate_half_axial(x) * sin

def depthwise_conv_centered(x, w, b=None):
    pad = (w.shape[0] - 1) // 2
    y = lax.conv_general_dilated(x, w[:, None, :], window_strides=(1,), padding=[(pad, pad)],
                                 dimension_numbers=('NWC', 'WIO', 'NWC'),
                                 feature_group_count=x.shape[-1])
    return y if b is None else y + b

def _diff_attend(qb, k_all, v_all, lam):
    s = jnp.einsum('bhmqd,bhmkd->bhmqk', qb, k_all).astype(jnp.float32) * (ATT_DK ** -0.5)
    p = jax.nn.softmax(s, axis=-1)
    a = (p[:, :, 0] - lam * p[:, :, 1]).astype(v_all.dtype)
    return jnp.einsum('bhqk,bhkd->bhqd', a, v_all)

def _diff_head_out(o, z, subln_g, lambda_init, w_out):
    o = rms_norm(o, subln_g) * (1.0 - lambda_init)
    o = o.reshape(o.shape[0], o.shape[1], ATT_WIDTH)
    return (o * jax.nn.silu(z)) @ w_out

def diff_attention_mixer(h, hc, w_in, w_out, lq1, lk1, lq2, lk2, subln_g, lambda_init, cos, sin, with_ctx_queries):
    B, L, _ = h.shape
    Lc = hc.shape[1]
    w_q, w_k, w_v, w_z = jnp.split(w_in, [ATT_QK_WIDTH, 2 * ATT_QK_WIDTH, 2 * ATT_QK_WIDTH + ATT_WIDTH], axis=1)
    q = apply_rope((h @ w_q).reshape(B, L, ATT_HEADS, 2, ATT_DK), cos, sin)
    k = apply_rope((h @ w_k).reshape(B, L, ATT_HEADS, 2, ATT_DK), cos, sin)
    v = (h @ w_v).reshape(B, L, ATT_HEADS, ATT_DV)
    z = h @ w_z
    kc = (hc @ w_k).reshape(B, Lc, ATT_HEADS, 2, ATT_DK)
    vc = (hc @ w_v).reshape(B, Lc, ATT_HEADS, ATT_DV)
    f32 = jnp.float32
    lam = (jnp.exp(jnp.sum(lq1.astype(f32) * lk1.astype(f32)))
           - jnp.exp(jnp.sum(lq2.astype(f32) * lk2.astype(f32))) + lambda_init)

    to_bhmld = lambda t: t.transpose(0, 2, 3, 1, 4)
    k_all = to_bhmld(jnp.concatenate([k, kc], axis=1))
    v_all = jnp.concatenate([v, vc], axis=1).transpose(0, 2, 1, 3)
    nblk = L // Q_BLOCK
    qb = jnp.moveaxis(to_bhmld(q).reshape(B, ATT_HEADS, 2, nblk, Q_BLOCK, ATT_DK), 3, 0)
    o = lax.map(lambda qblk: _diff_attend(qblk, k_all, v_all, lam), qb)
    o = o.transpose(1, 0, 3, 2, 4).reshape(B, L, ATT_HEADS, ATT_DV)
    y = _diff_head_out(o, z, subln_g, lambda_init, w_out)
    if not with_ctx_queries:
        return y, None
    qc = (hc @ w_q).reshape(B, Lc, ATT_HEADS, 2, ATT_DK)
    oc = _diff_attend(to_bhmld(qc), to_bhmld(kc), vc.transpose(0, 2, 1, 3), lam).transpose(0, 2, 1, 3)
    yc = _diff_head_out(oc, hc @ w_z, subln_g, lambda_init, w_out)
    return y, yc

def conformer_conv_mixer(h, w_in, dw_w, dw_b, ln_g, ln_b, w_out):
    a, g, z = jnp.split(h @ w_in, 3, axis=-1)
    y = a * jax.nn.sigmoid(g)
    y = depthwise_conv_centered(y, dw_w, dw_b)
    y = jax.nn.silu(layer_norm(y, ln_g, ln_b))
    return (y * jax.nn.silu(z)) @ w_out

def short_conv_mixer(h, w_in, conv_w, w_out):
    v, bg, cg, z = jnp.split(h @ w_in, 4, axis=-1)
    y = bg * depthwise_conv_centered(cg * v, conv_w)
    return (y * jax.nn.silu(z)) @ w_out

def multiscale_pool_minus_identity(h):
    L = h.shape[1]
    cs = jnp.cumsum(h.astype(jnp.float32), axis=1)
    cs = jnp.concatenate([jnp.zeros_like(cs[:, :1]), cs], axis=1)
    t = jnp.arange(L)
    outs = []
    for g, w in enumerate(POOL_WINDOWS):
        lo = jnp.clip(t - w // 2, 0, L)
        hi = jnp.clip(t + w // 2, 0, L)
        csg = cs[..., g * POOL_GROUP:(g + 1) * POOL_GROUP]
        s = jnp.take(csg, hi, axis=1) - jnp.take(csg, lo, axis=1)
        cnt = (hi - lo).astype(jnp.float32)[None, :, None]
        outs.append(s / cnt - h[..., g * POOL_GROUP:(g + 1) * POOL_GROUP].astype(jnp.float32))
    return jnp.stack(outs, axis=2).astype(h.dtype)

def pool_mixer(h, w_in, w_group, scale, w_out):
    v, z = jnp.split(h @ w_in, 2, axis=-1)
    p = multiscale_pool_minus_identity(v)
    y = jnp.einsum('blgc,gcd->blgd', p, w_group).reshape(v.shape) * scale
    return (y * jax.nn.silu(z)) @ w_out

def setup_inputs(seed: int = 0) -> dict:
    key = jax.random.key(seed)
    ks = iter(jax.random.split(key, 64))
    nrm = lambda shape, s: jax.random.normal(next(ks), shape, jnp.float32) * s
    nA, nB, nC, nD = (_layers_of_kind(k) for k in range(N_MIXERS))
    D = D_MODEL
    return {
        "x": nrm((BATCH, SEQ, D), 1.0),
        "c": nrm((BATCH, D), 1.0),
        "ctx": nrm((BATCH, CTX_LEN, D), 1.0),
        "c_ctx": nrm((D,), 1.0),
        "mod_w": nrm((DEPTH, D, 3 * D), D ** -0.5),
        "mod_b": nrm((DEPTH, 3 * D), 0.02),
        "ln_g": 1.0 + nrm((DEPTH, D), 0.05),
        "ln_b": nrm((DEPTH, D), 0.02),
        "attn_w_in": nrm((nA, D, 2 * ATT_QK_WIDTH + 2 * ATT_WIDTH), D ** -0.5),
        "attn_w_out": nrm((nA, ATT_WIDTH, D), ATT_WIDTH ** -0.5 * DEEPNORM_BETA),
        "attn_lambda_q1": nrm((nA, ATT_DK), 0.1),
        "attn_lambda_k1": nrm((nA, ATT_DK), 0.1),
        "attn_lambda_q2": nrm((nA, ATT_DK), 0.1),
        "attn_lambda_k2": nrm((nA, ATT_DK), 0.1),
        "attn_subln_g": 1.0 + nrm((nA, ATT_DV), 0.05),
        "conf_w_in": nrm((nB, D, 3 * CONF_WIDTH), D ** -0.5),
        "conf_dw_w": nrm((nB, CONF_KW, CONF_WIDTH), CONF_KW ** -0.5),
        "conf_dw_b": nrm((nB, CONF_WIDTH), 0.02),
        "conf_ln_g": 1.0 + nrm((nB, CONF_WIDTH), 0.05),
        "conf_ln_b": nrm((nB, CONF_WIDTH), 0.02),
        "conf_w_out": nrm((nB, CONF_WIDTH, D), CONF_WIDTH ** -0.5 * DEEPNORM_BETA),
        "sc_w_in": nrm((nC, D, 4 * SC_WIDTH), D ** -0.5),
        "sc_conv_w": nrm((nC, SC_KW, SC_WIDTH), SC_KW ** -0.5),
        "sc_w_out": nrm((nC, SC_WIDTH, D), SC_WIDTH ** -0.5 * DEEPNORM_BETA),
        "pool_w_in": nrm((nD, D, 2 * POOL_WIDTH), D ** -0.5),
        "pool_w_group": nrm((nD, len(POOL_WINDOWS), POOL_GROUP, POOL_GROUP), POOL_GROUP ** -0.5),
        "pool_scale": 1.0 + nrm((nD, POOL_WIDTH), 0.1),
        "pool_w_out": nrm((nD, POOL_WIDTH, D), POOL_WIDTH ** -0.5 * DEEPNORM_BETA),
    }

def reference(x, c, ctx, c_ctx, mod_w, mod_b, ln_g, ln_b,
              attn_w_in, attn_w_out, attn_lambda_q1, attn_lambda_k1, attn_lambda_q2, attn_lambda_k2, attn_subln_g,
              conf_w_in, conf_dw_w, conf_dw_b, conf_ln_g, conf_ln_b, conf_w_out,
              sc_w_in, sc_conv_w, sc_w_out,
              pool_w_in, pool_w_group, pool_scale, pool_w_out):
    L = x.shape[1]
    cos, sin = axial_rope_tables(L, ATT_DK)
    last_ctx_reader = max(i for i in range(DEPTH) if i % N_MIXERS == 0)
    silu_c = jax.nn.silu(c)
    silu_cc = jax.nn.silu(c_ctx)

    def seq_mixer(kind, j, s):
        if kind == 1:
            return conformer_conv_mixer(s, conf_w_in[j], conf_dw_w[j], conf_dw_b[j], conf_ln_g[j], conf_ln_b[j], conf_w_out[j])
        if kind == 2:
            return short_conv_mixer(s, sc_w_in[j], sc_conv_w[j], sc_w_out[j])
        return pool_mixer(s, pool_w_in[j], pool_w_group[j], pool_scale[j], pool_w_out[j])

    for i in range(DEPTH):
        kind, j = i % N_MIXERS, i // N_MIXERS
        update_ctx = i < last_ctx_reader
        shift, scale, gate = jnp.split(silu_c @ mod_w[i] + mod_b[i], 3, axis=-1)
        h = x * (1 + scale[:, None, :]) + shift[:, None, :]
        hc, cgate, out_c = None, None, None
        if kind == 0 or update_ctx:
            cshift, cscale, cgate = jnp.split(silu_cc @ mod_w[i] + mod_b[i], 3, axis=-1)
            hc = ctx * (1 + cscale) + cshift
        if kind == 0:
            lambda_init = 0.8 - 0.6 * math.exp(-0.3 * i)
            out, out_c = diff_attention_mixer(h, hc, attn_w_in[j], attn_w_out[j], attn_lambda_q1[j], attn_lambda_k1[j],
                                              attn_lambda_q2[j], attn_lambda_k2[j], attn_subln_g[j], lambda_init,
                                              cos, sin, update_ctx)
        else:
            out = seq_mixer(kind, j, h)
            if update_ctx:
                out_c = seq_mixer(kind, j, hc)
        x = layer_norm(DEEPNORM_ALPHA * x + gate[:, None, :] * out, ln_g[i], ln_b[i])
        if update_ctx:
            ctx = layer_norm(DEEPNORM_ALPHA * ctx + cgate * out_c, ln_g[i], ln_b[i])
    return x


_drawn_inputs = setup_inputs


def setup_inputs(seed=0):
    import zlib

    import numpy as np

    out = dict(_drawn_inputs(seed))
    spreads = {}
    factors = {'mod_b': 5.643,
     'attn_lambda_q1': 200.0,
     'attn_lambda_q2': 45.952,
     'attn_lambda_k2': 23.464,
     'attn_subln_g': 8.0,
     'conf_dw_b': 8.0,
     'conf_ln_g': 8.0,
     'conf_ln_b': 29.984}
    for name, (base, spread) in spreads.items():
        noise = np.random.default_rng([zlib.crc32(name.encode()), seed]).standard_normal(out[name].shape)
        drawn = base * np.exp(spread * noise) if base else spread * noise
        out[name] = __import__('jax').numpy.asarray(drawn.astype(out[name].dtype))
    for name, factor in factors.items():
        out[name] = (out[name] * factor).astype(out[name].dtype)
    return out
```

```python
import math
from contextlib import ExitStack

import concourse.bass as bass
from concourse import mybir

F32 = mybir.dt.float32
F32R = mybir.dt.float32r
ALU = mybir.AluOpType
ACT = mybir.ActivationFunctionType
AX = mybir.AxisListType

P = 128
D = 1024
KT = D // P
L = 1024
LC = 256
LT = L + LC
HEADS = 8
DK = 64
DV = 128
BANK = 512
HALVES = L // BANK
QT = L // P
KEYT = LT // P
CONF_KW = 31
PAD = (CONF_KW - 1) // 2
DEPTH = 2
ALPHA = (2 * DEPTH) ** 0.25
LAMBDA_INIT = 0.8 - 0.6 * math.exp(-0.3 * 0)
EPS = 1e-5
PIECE = KT * P
MASK_HALF_SWAP = list(range(16, 32)) + list(range(16))

V_C, V_CCTX, V_MODB, V_DWB, V_CLNG, V_CLNB, V_SUBG = 0, 8, 16, 64, 72, 80, 88
V_N = 89


def ds(i, n):
    return bass.ds(i, n)


class Memory:

    def __init__(self, nc, stack, tag):
        self.nc, self.stack, self.tag = nc, stack, tag

    def sb(self, name, shape, dt=F32):
        return self.stack.enter_context(self.nc.sbuf_tensor(f"{self.tag}_{name}", shape, dt))

    def psum(self, name, shape):
        return self.stack.enter_context(self.nc.psum_tensor(f"{self.tag}_{name}", shape, F32))

    def sem(self, name):
        return self.stack.enter_context(self.nc.semaphore(f"{self.tag}_{name}"))


def project(nc, io, keep):
    UQK, UZ = 2 * HEADS, HEADS
    UNITS = UQK + UZ
    with ExitStack() as stack:
        m = Memory(nc, stack, "pj")
        work = m.sb("work", [P, KT, LT])
        h_hi = m.sb("h_hi", [P, KT, LT], F32R)
        h_lo = m.sb("h_lo", [P, KT, LT], F32R)
        w_hi = m.sb("w_hi", [P, 4, PIECE], F32R)
        w_lo = m.sb("w_lo", [P, 4, PIECE], F32R)
        stage = m.sb("stage", [P, 2, PIECE])
        mod_tile = m.sb("mod_tile", [P, 2, D])
        acc = m.sb("acc", [P, 2, D])
        cos = m.sb("cos", [P, L])
        sin = m.sb("sin", [P, L])
        silu_c = m.sb("silu_c", [P, 2 * KT])
        mod0 = m.sb("mod0", [P, 2, 2, KT])
        note = m.sb("note", [P, 10])
        low_note = m.sb("low_note", [P, 1])
        ps = m.psum("ps", [P, 8, BANK])

        straight = [work[:, 0, :], work[:, 1, :]]
        turned = work[:, 2, :]
        out_hi = [work[:, 3, :], work[:, 4, :]]
        out_lo = [work[:, 5, :], work[:, 6, :]]

        vec_in, x_in, table_in = m.sem("vec_in"), m.sem("x_in"), m.sem("table_in")
        mod_in = [m.sem("mod_in0"), m.sem("mod_in1")]
        stage_in = [m.sem("stage_in0"), m.sem("stage_in1")]
        silu_done, ones_done = m.sem("silu_done"), m.sem("ones_done")
        mod_acc, mod_sums, mod_ready = m.sem("mod_acc"), m.sem("mod_sums"), m.sem("mod_ready")
        gate_done = m.sem("gate_done")
        h_mod, h_hi_done, h_lo_done = m.sem("h_mod"), m.sem("h_hi_done"), m.sem("h_lo_done")
        w_hi_done, w_lo_done = m.sem("w_hi_done"), m.sem("w_lo_done")
        proj_ready, proj_evac = m.sem("proj_ready"), m.sem("proj_evac")
        swapped, sin_done, cos_done = m.sem("swapped"), m.sem("sin_done"), m.sem("cos_done")
        rope_done, out_hi_done, out_lo_done = m.sem("rope_done"), m.sem("out_hi_done"), m.sem("out_lo_done")
        v_hi_done, v_lo_done = m.sem("v_hi_done"), m.sem("v_lo_done")
        qk_out = [m.sem("qk_out0"), m.sem("qk_out1")]
        z_out = [m.sem("z_out0"), m.sem("z_out1")]
        v_out = [m.sem("v_out0"), m.sem("v_out1")]

        MOD0 = 36
        vcol = keep.vcol
        mod_w = io["mod_w"].rearrange("l d n -> (l d) n")

        with nc.Block() as block:
            @block.sync
            def _(sp):
                sp.dma_start(vcol[:], io["vec"]).then_inc(vec_in, 16)

                def load_mod(slot, rows, cols):
                    sp.dma_start(mod_tile[:, slot, :], mod_w[rows, cols]).then_inc(mod_in[slot], 16)

                for q in range(2):
                    for t in range(KT):
                        n = KT * q + t
                        if n >= 2:
                            sp.wait_ge(mod_acc, 18 * ((n - 2) // KT) + 2 + 2 * ((n - 2) % KT) + 2)
                        load_mod(n % 2, slice(t * P, (t + 1) * P), slice(q * D, (q + 1) * D))
                    if q == 0:
                        for g in range(2):
                            sp.dma_start(stage[:, g, :], io["w_in"][g]).then_inc(stage_in[g], 16)
                sp.dma_start(cos[:], io["rope"][:, 0:L]).then_inc(table_in, 16)
                sp.dma_start(sin[:], io["rope"][:, L:2 * L]).then_inc(table_in, 16)
                sp.wait_ge(w_lo_done, 1)
                sp.dma_start(stage[:, 0, :], io["w_in"][2]).then_inc(stage_in[0], 16)

                def load_piece(g, slot):
                    sp.wait_ge(w_lo_done, g - 1)
                    sp.dma_start(stage[:, slot, :], io["w_in"][ds(g, 1)].rearrange("a p n -> (a p) n")
                                 if not isinstance(g, int) else io["w_in"][g]).then_inc(stage_in[slot], 16)

                for kind, scratch, width in ((0, io["q_hl"], L), (1, io["k_hl"], LT)):
                    with sp.Fori(0, 2) as i:
                        for j in range(4):
                            u = i * 4 + (HEADS * kind + j)
                            load_piece(u + 3, (j + 3) % 2)
                            sp.wait_ge(out_lo_done, u + 2)
                            for part, buf in ((0, out_hi), (1, out_lo)):
                                sp.dma_start(scratch[ds((i * 4 + j) * (2 * P) + part * P, P), :],
                                             buf[j % 2][:, 0:width]).then_inc(qk_out[j % 2], 16)
                with sp.Fori(0, 2) as i:
                    for j in range(4):
                        u = i * 4 + (UQK + j)
                        load_piece(u + 3, (j + 3) % 2)
                        for b in range(4):
                            step = 4 * j + b
                            before = (step - 2 + (1 if step - 2 < 8 else 2) + 1) if step >= 2 else step - 1
                            sp.wait_ge(mod_acc, i * 18 + (MOD0 + before))
                            t = 4 * (j % 2) + b
                            if j < 2:
                                load_mod(b % 2, ds(i * D + t * P, P), slice(2 * D, 3 * D))
                            else:
                                load_mod(b % 2, slice(D + t * P, D + (t + 1) * P), ds(i * D, D))
                        sp.wait_ge(proj_evac, u + 3)
                        sp.dma_start(io["z_s"][ds((i * 4 + j) * P, P), :],
                                     straight[j % 2][:, 0:L]).then_inc(z_out[j % 2], 16)
                load_piece(27, 1)
                for vc in range(2):
                    for tt in range(KEYT):
                        n = KEYT * vc + tt
                        if vc == 0 and tt in (1, 2):
                            load_piece(27 + tt, (27 + tt) % 2)
                        if vc == 1 and tt == 0:
                            load_piece(30, 0)
                            load_piece(31, 1)
                        sp.wait_ge(v_lo_done, n + 3)
                        for part, buf in ((0, out_hi), (1, out_lo)):
                            sp.dma_start(io["v_hl"][part, tt, :, vc * BANK:(vc + 1) * BANK],
                                         buf[n % 2][:, 0:BANK]).then_inc(v_out[n % 2], 16)
                for p in range(2):
                    sp.wait_ge(qk_out[p], 32 + 32 * UQK // 2)
                    sp.wait_ge(z_out[p], 16 + 16 * UZ // 2)
                    sp.wait_ge(v_out[p], 32 * KEYT)

            @block.gpsimd
            def _(pool):
                nc.gpsimd.memset(keep.ones[:], 1.0).then_inc(ones_done, 1)
                nc.gpsimd.memset(keep.eps[:], EPS)
                nc.gpsimd.memset(keep.ident[:], 0.0).then_inc(ones_done, 1)
                pool.wait_ge(ones_done, 2)
                nc.gpsimd.affine_select(out=keep.ident[:], in_=keep.ident[:], compare_op=ALU.not_equal, fill=1.0,
                                        base=0, pattern=[[-1, P]], channel_multiplier=1).then_inc(ones_done, 1)
                for kt in range(KT):
                    pool.wait_ge(h_mod, kt + 1)
                    nc.gpsimd.tensor_copy(h_hi[:, kt, :], work[:, kt, :]).then_inc(h_hi_done, 1)
                pool.wait_ge(table_in, 32)
                with pool.Fori(0, 4) as i:
                    for j in range(4):
                        pool.wait_ge(swapped, i * 4 + (j + 1))
                        nc.gpsimd.tensor_mul(straight[j % 2][:, 0:L], straight[j % 2][:, 0:L],
                                             cos[:]).then_inc(cos_done, 1)

            @block.scalar
            def _(act):
                for kt in range(KT):
                    act.dma_start(work[:, kt, :], io["x_t"][kt]).then_inc(x_in, 16)
                for n in range(DEPTH):
                    act.dma_start(keep.gate[:, n, :], io["mod_b"][n:n + 1, 2 * D:3 * D]
                                  .partition_broadcast(P).rearrange("p a n -> p (a n)")).then_inc(x_in, 16)
                act.wait_ge(vec_in, 16)
                nc.scalar.activation(silu_c[:], vcol[:, 0:2 * KT], ACT.Silu).then_inc(silu_done, 1)
                nc.scalar.activation(note[:, 0:1], vcol[:, 0:1], ACT.Copy).then_inc(proj_evac, 2)
                nc.scalar.activation(note[:, 1:2], vcol[:, 0:1], ACT.Copy).then_inc(out_hi_done, 1)
                for p in range(2):
                    nc.scalar.activation(note[:, 2 + p:3 + p], vcol[:, 0:1], ACT.Copy).then_inc(qk_out[p], 32)
                    nc.scalar.activation(note[:, 8 + p:9 + p], vcol[:, 0:1], ACT.Copy).then_inc(z_out[p], 16)

                def split_piece(g, slot, wslot, loads):
                    act.wait_ge(stage_in[slot], loads * 16)
                    nc.scalar.activation(w_hi[:, wslot, :], stage[:, slot, :], ACT.Copy).then_inc(w_hi_done, 1)

                split_piece(0, 0, 0, 1)
                split_piece(1, 1, 1, 1)
                act.wait_ge(x_in, 16 * (KT + DEPTH))
                act.wait_ge(mod_ready, 4)
                for kt in range(KT):
                    nc.scalar.activation(work[:, kt, 0:L], work[:, kt, 0:L], ACT.Identity,
                                         bias=mod0[:, 0, 0, kt:kt + 1], scale=mod0[:, 1, 0, kt:kt + 1])
                    nc.scalar.activation(work[:, kt, L:LT], work[:, kt, L:LT], ACT.Identity,
                                         bias=mod0[:, 0, 1, kt:kt + 1],
                                         scale=mod0[:, 1, 1, kt:kt + 1]).then_inc(h_mod, 1)
                split_piece(2, 0, 2, 2)
                act.wait_ge(h_lo_done, KT)
                for kind in range(2):
                    with act.Fori(0, 2) as i:
                        for j in range(4):
                            u = i * 4 + (HEADS * kind + j)
                            p = j % 2
                            act.wait_ge(proj_ready, u + 1)
                            act.wait_ge(rope_done, u + 1)
                            if kind == 1:
                                act.wait_ge(out_lo_done, u + 1)
                                nc.scalar.activation(turned[:, L:LT], ps[:, 3 * p + 2, 0:LC], ACT.Copy)
                            nc.scalar.activation(straight[p][:, 0:L].rearrange("p (b n) -> p b n", b=2),
                                                 ps[:, 3 * p:3 * p + 2, :], ACT.Copy,
                                                 scale=DK ** -0.5 if kind == 0 else 1.0).then_inc(proj_evac, 1)
                            act.wait_ge(rope_done, u + 3)
                            act.wait_ge(qk_out[p], i * 64 + 32 * (4 * kind + j // 2 + 1))
                            width = L if kind == 0 else LT
                            nc.scalar.activation(out_hi[p][:, 0:width].bitcast(F32R), turned[:, 0:width],
                                                 ACT.Copy).then_inc(out_hi_done, 1)
                            act.wait_ge(proj_ready, u + 1)
                            split_piece(u + 3, (j + 3) % 2, (j + 3) % 4, i * 2 + (4 * kind + (j + 3) // 2 + 1))
                act.wait_ge(rope_done, 2 + UQK)
                with act.Fori(0, 2) as i:
                    for j in range(4):
                        u = i * 4 + (UQK + j)
                        p = j % 2
                        act.wait_ge(proj_ready, u + 1)
                        act.wait_ge(z_out[p], i * 32 + 16 * (j // 2 + 1))
                        nc.scalar.activation(straight[p][:, 0:L].rearrange("p (b n) -> p b n", b=2),
                                             ps[:, 3 * p:3 * p + 2, :], ACT.Silu).then_inc(proj_evac, 1)
                        split_piece(u + 3, (j + 3) % 2, (j + 3) % 4, i * 2 + (8 + (j + 3) // 2 + 1))
                act.wait_ge(proj_ready, UNITS)
                split_piece(27, 1, 3, 14)
                for p in range(2):
                    act.wait_ge(qk_out[p], 32 + 32 * UQK // 2)
                for vc in range(2):
                    for tt in range(KEYT):
                        n = KEYT * vc + tt
                        act.wait_ge(proj_ready, UNITS + n + 1)
                        if n >= 2:
                            act.wait_ge(v_out[n % 2], 32 * (n // 2))
                        nc.scalar.activation(out_hi[n % 2][:, 0:BANK].bitcast(F32R), ps[:, 3 * (n % 2), :],
                                             ACT.Copy).then_inc(v_hi_done, 1)
                    if vc == 0:
                        for g in range(28, 32):
                            split_piece(g, g % 2, g % 4, g // 2 + 1)

            @block.vector
            def _(dve):
                nc.vector.memset(note[:, 7:8], 0.0).then_inc(rope_done, 2)
                nc.vector.memset(note[:, 6:7], 0.0).then_inc(v_lo_done, 2)
                nc.vector.memset(low_note[:], 0.0).then_inc(out_lo_done, 1)
                dve.wait_ge(silu_done, 1)
                for q in range(2):
                    if q:
                        dve.wait_ge(mod_sums, 1)
                    for a in range(2):
                        nc.vector.memset(acc[:, a, :], 0.0).then_inc(mod_acc, 1)
                    with dve.Fori(0, KT // 2) as i:
                        for b in range(2):
                            dve.wait_ge(mod_in[b], i * 16 + 16 * (4 * q + 1))
                            for a in range(2):
                                dve.wait_ge(mod_acc, i * 4 + (18 * q + 2 + 2 * b + a - 1))
                                nc.vector.scalar_tensor_tensor(
                                    out=acc[:, a, :], in0=mod_tile[:, b, :],
                                    scalar=silu_c[:, ds(i * 2 + (a * KT + b), 1)], in1=acc[:, a, :],
                                    op0=ALU.mult, op1=ALU.add).then_inc(mod_acc, 1)
                dve.wait_ge(mod_sums, 2)
                for a in range(2):
                    nc.vector.tensor_tensor(mod0[:, 0, a, :], ps[:, 7, a * KT:(a + 1) * KT],
                                            vcol[:, V_MODB:V_MODB + KT], ALU.add).then_inc(mod_ready, 1)
                    nc.vector.scalar_tensor_tensor(out=mod0[:, 1, a, :], in0=ps[:, 7, (2 + a) * KT:(3 + a) * KT],
                                                   scalar=1.0, in1=vcol[:, V_MODB + KT:V_MODB + 2 * KT],
                                                   op0=ALU.add, op1=ALU.add).then_inc(mod_ready, 1)

                def low_piece(g, slot, wslot):
                    dve.wait_ge(w_hi_done, g + 1)
                    nc.vector.tensor_sub(w_lo[:, wslot, :], stage[:, slot, :],
                                         w_hi[:, wslot, :].bitcast(F32)).then_inc(w_lo_done, 1)

                low_piece(0, 0, 0)
                low_piece(1, 1, 1)
                for kt in range(KT):
                    dve.wait_ge(h_hi_done, kt + 1)
                    nc.vector.tensor_sub(h_lo[:, kt, :], work[:, kt, :],
                                         h_hi[:, kt, :].bitcast(F32)).then_inc(h_lo_done, 1)
                low_piece(2, 0, 2)
                dve.wait_ge(table_in, 32)
                for kind in range(2):
                    width = L if kind == 0 else LT
                    with dve.Fori(0, 2) as i:
                        for j in range(4):
                            u = i * 4 + (HEADS * kind + j)
                            p = j % 2
                            dve.wait_ge(proj_evac, u + 3)
                            dve.wait_ge(out_hi_done, u + 1)
                            dve.wait_ge(out_lo_done, u + 1)
                            nc.vector.memset(note[:, 5:6], 0.0)
                            nc.vector.stream_shuffle(turned[:, 0:L], straight[p][:, 0:L],
                                                     MASK_HALF_SWAP).then_inc(swapped, 1)
                            dve.wait_ge(swapped, u + 1)
                            nc.vector.tensor_mul(turned[:, 0:L], turned[:, 0:L], sin[:]).then_inc(sin_done, 1)
                            dve.wait_ge(sin_done, u + 1)
                            dve.wait_ge(cos_done, u + 1)
                            nc.vector.tensor_add(turned[:, 0:L], turned[:, 0:L],
                                                 straight[p][:, 0:L]).then_inc(rope_done, 1)
                            dve.wait_ge(out_hi_done, u + 2)
                            dve.wait_ge(rope_done, u + 3)
                            nc.vector.tensor_sub(out_lo[p][:, 0:width].bitcast(F32R), turned[:, 0:width],
                                                 out_hi[p][:, 0:width]).then_inc(out_lo_done, 1)
                            low_piece(u + 3, (j + 3) % 2, (j + 3) % 4)
                with dve.Fori(0, 2) as i:
                    for j in range(4):
                        u = i * 4 + (UQK + j)
                        low_piece(u + 3, (j + 3) % 2, (j + 3) % 4)
                        half = j // 2
                        for b in range(4):
                            step = 4 * j + b
                            pos = step + half
                            if step % 8 == 0:
                                dve.wait_ge(mod_sums, i * 2 + 2)
                                nc.vector.memset(acc[:, half, :], 0.0).then_inc(mod_acc, 1)
                            dve.wait_ge(mod_in[b % 2], i * 128 + 16 * (8 + 2 * j + b // 2 + 1))
                            dve.wait_ge(mod_acc, i * 18 + (MOD0 + pos + 1))
                            t = 4 * (j % 2) + b
                            nc.vector.scalar_tensor_tensor(
                                out=acc[:, half, :], in0=mod_tile[:, b % 2, :], scalar=silu_c[:, t:t + 1],
                                in1=acc[:, half, :], op0=ALU.mult, op1=ALU.add).then_inc(mod_acc, 1)
                    dve.wait_ge(mod_sums, i * 2 + 3)
                    g = keep.gate[:, ds(i, 1), :].rearrange("p a (b n) -> p (a b) n", b=2)
                    nc.vector.tensor_tensor(g, ps[:, 6:8, :], g, ALU.add).then_inc(gate_done, 1)
                    dve.wait_ge(mod_sums, i * 2 + 4)
                    nc.vector.tensor_tensor(keep.mod1[:, ds(i, 1), :].rearrange("p a n -> p (a n)"), ps[:, 7, 0:KT],
                                            vcol[:, ds(i * KT + (V_MODB + 3 * KT), KT)],
                                            ALU.add).then_inc(gate_done, 1)
                low_piece(27, 1, 3)
                dve.wait_ge(gate_done, 4)
                nc.vector.tensor_scalar_add(keep.mod1[:, 1, :], keep.mod1[:, 1, :], 1.0)
                for vc in range(2):
                    for tt in range(KEYT):
                        n = KEYT * vc + tt
                        dve.wait_ge(v_hi_done, n + 1)
                        nc.vector.tensor_sub(out_lo[n % 2][:, 0:BANK].bitcast(F32R), ps[:, 3 * (n % 2), :],
                                             out_hi[n % 2][:, 0:BANK]).then_inc(v_lo_done, 1)
                    if vc == 0:
                        for g in range(28, 32):
                            low_piece(g, g % 2, g % 4)

            @block.tensor
            def _(pe):
                pe.wait_ge(ones_done, 1)
                for q in range(2):
                    pe.wait_ge(mod_acc, 18 * (q + 1))
                    for a in range(2):
                        for j in range(KT):
                            c = (2 * q + a) * KT + j
                            last = nc.tensor.matmul(ps[:, 7, c:c + 1], acc[:, a, j * P:(j + 1) * P],
                                                    keep.ones[:, 0:1], start=True, stop=True)
                    last.then_inc(mod_sums, 1)

                def unit(u, j, context):
                    pe.wait_ge(w_lo_done, u + 1)
                    pe.wait_ge(proj_evac, u + 1)
                    p = j % 2
                    outs = [(3 * p + n, n * BANK, BANK) for n in range(HALVES)]
                    if context:
                        outs.append((3 * p + 2, L, LC))
                    for kt in range(KT):
                        for w, parts in ((w_hi, (h_hi, h_lo)), (w_lo, (h_hi,))):
                            for h in parts:
                                for bank, at, n in outs:
                                    last = nc.tensor.matmul(
                                        ps[:, bank, 0:n], w[:, j, kt * P:(kt + 1) * P], h[:, kt, at:at + n],
                                        start=(kt == 0 and w is w_hi and h is h_hi),
                                        stop=(kt == KT - 1 and w is w_lo))
                    last.then_inc(proj_ready, 1)

                pe.wait_ge(h_lo_done, KT)
                for kind in range(2):
                    with pe.Fori(0, 2) as i:
                        for j in range(4):
                            unit(i * 4 + (HEADS * kind + j), j, kind == 1)
                with pe.Fori(0, 2) as i:
                    for j in range(4):
                        unit(i * 4 + (UQK + j), j, False)
                        if j == 2:
                            pe.wait_ge(mod_acc, i * 18 + (MOD0 + 9))
                            for n in range(2):
                                last = nc.tensor.matmul(ps[:, 6 + n, :], keep.ones[:],
                                                        acc[:, 0, n * BANK:(n + 1) * BANK], start=True, stop=True)
                            last.then_inc(mod_sums, 1)
                    pe.wait_ge(mod_acc, i * 18 + (MOD0 + 18))
                    pe.wait_ge(gate_done, i * 2 + 1)
                    for n in range(KT):
                        last = nc.tensor.matmul(ps[:, 7, n:n + 1], acc[:, 1, n * P:(n + 1) * P],
                                                keep.ones[:, 0:1], start=True, stop=True)
                    last.then_inc(mod_sums, 1)
                with pe.Fori(0, 2) as vc:
                    for tt in range(KEYT):
                        if tt < 2:
                            pe.wait_ge(proj_evac, UNITS + 2)
                        pe.wait_ge(v_lo_done, vc * KEYT + (tt + 1))
                        for kt in range(KT):
                            if tt == 0 and kt % 2 == 0:
                                pe.wait_ge(w_lo_done, vc * 4 + (UNITS + kt // 2 + 1))
                            for h, parts in ((h_hi, (w_hi, w_lo)), (h_lo, (w_hi,))):
                                for w in parts:
                                    last = nc.tensor.matmul(
                                        ps[:, 3 * (tt % 2), :], h[:, kt, tt * P:(tt + 1) * P],
                                        w[:, kt // 2, (kt % 2) * BANK:(kt % 2 + 1) * BANK],
                                        start=(kt == 0 and h is h_hi and w is w_hi),
                                        stop=(kt == KT - 1 and h is h_lo))
                        last.then_inc(proj_ready, 1)


def attend(nc, io, keep):
    KEY_CUTS = [(0, BANK), (BANK, BANK), (2 * BANK, LT - 2 * BANK)]
    ROUNDS = [(0, 4), (4, 4), (8, 2)]
    RMS_SHRINK = 2.0 ** -12
    GROUP = 4
    with ExitStack() as stack:
        m = Memory(nc, stack, "at")
        q_a = m.sb("q_a", [P, 2, 2, L], F32R)
        q_b = m.sb("q_b", [P, 2, 2, L], F32R)
        k_s = m.sb("k_s", [P, 2, 2, LT], F32R)
        v_hi = m.sb("v_hi", [P, 2, KEYT, DV], F32R)
        v_lo = m.sb("v_lo", [P, 2, KEYT, DV], F32R)
        z_s = m.sb("z_s", [P, 2, L])
        prob = m.sb("prob", [P, 2, 2, LT])
        a_hi = m.sb("a_hi", [P, KEYT, GROUP * P], F32R)
        a_lo = m.sb("a_lo", [P, KEYT, GROUP * P], F32R)
        square = m.sb("square", [P, BANK])
        rms = m.sb("rms", [P, BANK])
        eps_small = m.sb("eps_small", [P, 1])
        normed = m.sb("normed", [P, BANK])
        o_hi = m.sb("o_hi", [P, BANK])
        o_lo = m.sb("o_lo", [P, BANK])
        stat = m.sb("stat", [P, 2, 8])
        lam_in = m.sb("lam_in", [P, 4, DK])
        lam = m.sb("lam", [P, 6])
        note = m.sb("note", [P, 10])
        hold_out = m.sb("hold_out", [P, 1])
        mean_w = m.sb("mean_w", [P, P])
        ps = m.psum("ps", [P, 8, BANK])

        lam_loaded, lam_step, lam_exp, lam_ready = (m.sem(n) for n in ("lam_loaded", "lam_step", "lam_exp", "lam_ready"))
        head_in = [m.sem("head_in0"), m.sem("head_in1")]
        s_ready = [m.sem("s_ready0"), m.sem("s_ready1")]
        max_done = [m.sem("max_done0"), m.sem("max_done1")]
        exp_done = [m.sem("exp_done0"), m.sem("exp_done1")]
        inv_done, neg_done, scaled, diff_done = (m.sem(n) for n in ("inv_done", "neg_done", "scaled", "diff_done"))
        t_ready, t_hi_done, t_lo_done = m.sem("t_ready"), m.sem("t_hi_done"), m.sem("t_lo_done")
        pv_ready, sq_done, mean_ready = m.sem("pv_ready"), m.sem("sq_done"), m.sem("mean_ready")
        rms_done, inv_rms_done, normed_done = m.sem("rms_done"), m.sem("inv_rms_done"), m.sem("normed_done")
        gated, o_hi_done, o_lo_done, og_out = (m.sem(n) for n in ("gated", "o_hi_done", "o_lo_done", "og_out"))

        GROUPS = HEADS * QT // GROUP
        IN_HEAD = 16 * 15

        def run(eng, group):
            group(0, 0, False)
            with eng.Fori(0, 3) as i:
                for b in range(4):
                    group(i * 4 + (b + 1), (b + 1) % 4, False)
            for g in range(13, GROUPS):
                group(g, g % 4, g == GROUPS - 1)

        with nc.Block() as block:
            @block.sync
            def _(sp):
                sp.dma_start(lam_in[:], io["lam"].partition_broadcast(P).rearrange("p a b n -> p (a b) n")
                             ).then_inc(lam_loaded, 16)

                def load_head(h, slot):
                    qrow, krow = h * (2 * P), h * (2 * P)
                    for mp in range(2):
                        for part in range(2):
                            top = slice(part * DK, (part + 1) * DK)
                            other = slice((1 - part) * DK, (2 - part) * DK)
                            src = io["q_hl"][ds(qrow + (part * P + mp * DK), DK), :]
                            sp.dma_start(q_a[top, slot, mp, :].bitcast(F32), src).then_inc(head_in[slot], 16)
                            sp.dma_start(q_b[other, slot, mp, :].bitcast(F32), src).then_inc(head_in[slot], 16)
                            src = io["k_hl"][ds(krow + (part * P + mp * DK), DK), :]
                            sp.dma_start(k_s[top, slot, mp, :].bitcast(F32), src).then_inc(head_in[slot], 16)
                    for part, v in ((0, v_hi), (1, v_lo)):
                        src = io["v_hl"][part].rearrange("t p n -> p t n")[:, :, ds(h * DV, DV)]
                        sp.dma_start(v[:, slot, :, :].bitcast(F32), src).then_inc(head_in[slot], 16)
                    sp.dma_start(z_s[:, slot, :], io["z_s"][ds(h * DV, DV), :]).then_inc(head_in[slot], 16)

                load_head(0, 0)
                load_head(1, 1)

                def group(g, gm, last):
                    if gm % 2 == 0 and not (isinstance(g, int) and (g < 2 or g > 12)):
                        sp.wait_ge(mean_ready, g)
                        sp.wait_ge(gated, g)
                        if isinstance(g, int):
                            load_head(g // 2 + 1, 1 - gm // 2)
                        else:
                            load_head(g_half[0], 1 - gm // 2)
                    sp.wait_ge(o_lo_done, g + 2)
                    row, half = (g // 2) * P if isinstance(g, int) else g_half[1], gm % 2
                    for part, buf in ((0, o_hi), (1, o_lo)):
                        at = slice(half * BANK, (half + 1) * BANK)
                        sp.dma_start(io["og_hl"][ds(row + part * D, P), at], buf[:]).then_inc(og_out, 16)

                g_half = [None, None]
                group(0, 0, False)
                with sp.Fori(0, 3) as i:
                    for b in range(4):
                        head = i * 2 + (b + 1) // 2
                        g_half[0], g_half[1] = head + 1, head * P
                        group(i * 4 + (b + 1), (b + 1) % 4, False)
                for g in range(13, GROUPS):
                    group(g, g % 4, g == GROUPS - 1)
                sp.wait_ge(og_out, 32 * GROUPS)

            @block.tensor
            def _(pe):
                def scores(t, slot, tile):
                    for mp in range(2):
                        pe.wait_ge(exp_done[mp], t + 1)
                        for n, (at, w) in enumerate(KEY_CUTS):
                            for first, q in ((True, q_a), (False, q_b)):
                                lastmm = nc.tensor.matmul(
                                    ps[:, 3 * mp + n, 0:w], q[:, slot, mp, tile * P:(tile + 1) * P],
                                    k_s[:, slot, mp, at:at + w], start=first, stop=not first)
                        lastmm.then_inc(s_ready[mp], 1)

                def group(g, gm, last):
                    slot = gm // 2
                    for c in range(GROUP):
                        t = g * GROUP + c
                        if not (last and c == GROUP - 1):
                            nt = (gm * GROUP + c + 1) % (2 * QT)
                            if nt % QT == 0:
                                pe.wait_ge(head_in[nt // QT], head_loads(g))
                            scores(t + 1, nt // QT, nt % QT)
                        pe.wait_ge(diff_done, t + 1)
                        for r, (at, n) in enumerate(ROUNDS):
                            s = 3 * c + r
                            if s == 0:
                                pe.wait_ge(normed_done, g + 1)
                            elif s == 1:
                                pe.wait_ge(rms_done, g + 1)
                            else:
                                pe.wait_ge(t_lo_done, g * 12 + (s - 1))
                            for k in range(n):
                                lastmm = nc.tensor.transpose(ps[:, 6 + s % 2, k * P:(k + 1) * P],
                                                             prob[:, c % 2, 0, (at + k) * P:(at + k + 1) * P],
                                                             keep.ident[:])
                            lastmm.then_inc(t_ready, 1)
                    pe.wait_ge(t_lo_done, g * 12 + 12)
                    for k in range(KEYT):
                        for v, a in ((v_hi, a_hi), (v_hi, a_lo), (v_lo, a_hi)):
                            lastmm = nc.tensor.matmul(ps[:, 6, :], v[:, slot, k, :], a[:, k, :],
                                                      start=(k == 0 and v is v_hi and a is a_hi),
                                                      stop=(k == KEYT - 1 and v is v_lo))
                    lastmm.then_inc(pv_ready, 1)
                    pe.wait_ge(sq_done, g + 1)
                    nc.tensor.matmul(ps[:, 7, :], mean_w[:], square[:], start=True, stop=True).then_inc(mean_ready, 1)

                def head_loads(g):
                    return IN_HEAD * ((g // 2 + 1) // 2 + 1) if isinstance(g, int) else head_count[0]

                head_count = [None]
                pe.wait_ge(head_in[0], IN_HEAD)
                pe.wait_ge(lam_step, 1)
                scores(0, 0, 0)
                group(0, 0, False)
                with pe.Fori(0, 3) as i:
                    for b in range(4):
                        head_count[0] = i * IN_HEAD + IN_HEAD * (1 if b == 0 else 2)
                        group(i * 4 + (b + 1), (b + 1) % 4, False)
                for g in range(13, GROUPS):
                    group(g, g % 4, g == GROUPS - 1)

            @block.gpsimd
            def _(pool):
                nc.gpsimd.memset(eps_small[:], EPS * RMS_SHRINK)
                nc.gpsimd.memset(mean_w[:], 1.0 / DV).then_inc(lam_step, 1)

                def hold():
                    nc.gpsimd.tensor_add(hold_out[:], mean_w[:, 0:1], mean_w[:, 1:2])

                pool.wait_ge(lam_step, 1)

                def scale(t, p):
                    pool.wait_ge(inv_done, t + 1)
                    hold()
                    nc.gpsimd.tensor_scalar(prob[:, p, 0, :], prob[:, p, 0, :], stat[:, p, 4:5], 1.0,
                                            ALU.mult, ALU.mult).then_inc(scaled, 1)

                def finish(g, gm):
                    slot, half = (gm - 1) % 4 // 2, (gm - 1) % 2
                    pool.wait_ge(normed_done, g + 1)
                    nc.gpsimd.tensor_mul(normed[:], normed[:],
                                         z_s[:, slot, half * BANK:(half + 1) * BANK]).then_inc(gated, 1)
                    pool.wait_ge(gated, g)
                    pool.wait_ge(og_out, g * 32)
                    hold()
                    nc.gpsimd.tensor_copy(o_hi[:].bitcast(F32R), normed[:]).then_inc(o_hi_done, 1)
                    pool.wait_ge(o_hi_done, g)
                    nc.gpsimd.tensor_sub(o_lo[:].bitcast(F32R), normed[:], o_hi[:]).then_inc(o_lo_done, 1)

                scale(0, 0)

                def group(g, gm, last):
                    for c in range(GROUP):
                        t = g * GROUP + c
                        if not (last and c == GROUP - 1):
                            scale(t + 1, (c + 1) % 2)
                        if c == 2 and not (isinstance(g, int) and g == 0):
                            finish(g, gm)

                run(pool, group)
                finish(GROUPS, 0)

            @block.scalar
            def _(act):
                for n, s in enumerate((exp_done[0], exp_done[1], rms_done, normed_done)):
                    nc.scalar.activation(note[:, n:n + 1], keep.eps[:], ACT.Copy).then_inc(s, 1)
                nc.scalar.activation(note[:, 4:5], keep.eps[:], ACT.Copy).then_inc(og_out, 32)
                act.wait_ge(lam_step, 5)
                nc.scalar.activation(lam[:, 2:4], lam[:, 0:2], ACT.Exp).then_inc(lam_exp, 1)

                def exponential(t, mp, p, slot_reused):
                    act.wait_ge(max_done[mp], t + 1)
                    if slot_reused is not None:
                        act.wait_ge(t_ready, slot_reused)
                    nc.scalar.activation(prob[:, p, mp, :], ps[:, 3 * mp:3 * mp + 3, :].rearrange("p b n -> p (b n)")[:, 0:LT],
                                         ACT.Exp, bias=stat[:, p, mp:mp + 1],
                                         accum_out=stat[:, p, 2 + mp:3 + mp]).then_inc(exp_done[mp], 1)

                def high(g, c, r):
                    at, n = ROUNDS[r]
                    s = 3 * c + r
                    act.wait_ge(t_ready, g * 12 + (s + 1))
                    nc.scalar.activation(a_hi[:, at:at + n, c * P:(c + 1) * P],
                                         ps[:, 6 + s % 2, 0:n * P].rearrange("p (k q) -> p k q", k=n),
                                         ACT.Copy).then_inc(t_hi_done, 1)

                def finish(g):
                    act.wait_ge(pv_ready, g + 1)
                    nc.scalar.activation(square[:], ps[:, 6, :], ACT.Square).then_inc(sq_done, 1)
                    act.wait_ge(mean_ready, g + 1)
                    nc.scalar.activation(rms[:], ps[:, 7, :], ACT.Sqrt, bias=eps_small[:],
                                         scale=RMS_SHRINK).then_inc(rms_done, 1)

                exponential(0, 0, 0, None)
                exponential(0, 1, 0, None)

                def group(g, gm, last):
                    for c in range(GROUP):
                        t = g * GROUP + c
                        p = (c + 1) % 2
                        nxt = not (last and c == GROUP - 1)
                        reused = None
                        if not (isinstance(g, int) and g == 0 and c == 0):
                            reused = g * 12 + 3 * c
                        if nxt:
                            exponential(t + 1, 0, p, reused)
                        high(g, c, 0)
                        if nxt:
                            exponential(t + 1, 1, p, reused)
                        high(g, c, 1)
                        high(g, c, 2)
                    finish(g)

                run(act, group)

            @block.vector
            def _(dve):
                dve.wait_ge(lam_loaded, 16)
                dve.wait_ge(lam_step, 1)
                for n in range(2):
                    nc.vector.tensor_mul(lam_in[:, 2 * n, :], lam_in[:, 2 * n, :],
                                         lam_in[:, 2 * n + 1, :]).then_inc(lam_step, 1)
                dve.wait_ge(lam_step, 3)
                for n in range(2):
                    nc.vector.tensor_reduce(lam[:, n:n + 1], lam_in[:, 2 * n, :], AX.X, ALU.add).then_inc(lam_step, 1)
                dve.wait_ge(lam_exp, 1)
                nc.vector.tensor_sub(lam[:, 4:5], lam[:, 3:4], lam[:, 2:3]).then_inc(lam_ready, 1)
                dve.wait_ge(lam_ready, 1)
                nc.vector.tensor_scalar_add(lam[:, 5:6], lam[:, 4:5], -LAMBDA_INIT).then_inc(lam_ready, 1)
                dve.wait_ge(lam_ready, 2)

                def maximum(t, mp, p):
                    dve.wait_ge(s_ready[mp], t + 1)
                    nc.vector.tensor_reduce(stat[:, p, mp:mp + 1],
                                            ps[:, 3 * mp:3 * mp + 3, :].rearrange("p b n -> p (b n)")[:, 0:LT],
                                            AX.X, ALU.max, negate=True).then_inc(max_done[mp], 1)

                def inverse(t, p):
                    dve.wait_ge(exp_done[0], t + 2)
                    nc.vector.reciprocal(stat[:, p, 4:5], stat[:, p, 2:3]).then_inc(inv_done, 1)

                def difference(t, p):
                    dve.wait_ge(exp_done[1], t + 2)
                    nc.vector.reciprocal(stat[:, p, 5:6], stat[:, p, 3:4]).then_inc(neg_done, 1)
                    dve.wait_ge(neg_done, t * 2 + 1)
                    nc.vector.tensor_mul(stat[:, p, 6:7], stat[:, p, 5:6], lam[:, 5:6]).then_inc(neg_done, 1)
                    dve.wait_ge(neg_done, t * 2 + 2)
                    dve.wait_ge(scaled, t + 1)
                    nc.vector.scalar_tensor_tensor(out=prob[:, p, 0, :], in0=prob[:, p, 1, :],
                                                   scalar=stat[:, p, 6:7], in1=prob[:, p, 0, :],
                                                   op0=ALU.mult, op1=ALU.add).then_inc(diff_done, 1)

                def low(g, c, r):
                    at, n = ROUNDS[r]
                    s = 3 * c + r
                    dve.wait_ge(t_hi_done, g * 12 + (s + 1))
                    nc.vector.tensor_sub(a_lo[:, at:at + n, c * P:(c + 1) * P],
                                         ps[:, 6 + s % 2, 0:n * P].rearrange("p (k q) -> p k q", k=n),
                                         a_hi[:, at:at + n, c * P:(c + 1) * P].bitcast(F32)).then_inc(t_lo_done, 1)

                def finish(g):
                    dve.wait_ge(rms_done, g + 1)
                    nc.vector.reciprocal(rms[:], rms[:]).then_inc(inv_rms_done, 1)
                    dve.wait_ge(inv_rms_done, g)
                    dve.wait_ge(o_lo_done, g)
                    nc.vector.scalar_tensor_tensor(out=normed[:], in0=ps[:, 6, :], scalar=keep.subln[:],
                                                   in1=rms[:], op0=ALU.mult, op1=ALU.mult).then_inc(normed_done, 1)

                nc.vector.tensor_scalar_mul(keep.subln[:], keep.vcol[:, V_SUBG:V_SUBG + 1],
                                            (1.0 - LAMBDA_INIT) * RMS_SHRINK ** 0.5).then_inc(lam_ready, 1)
                nc.vector.memset(note[:, 6:7], 0.0).then_inc(o_lo_done, 1)
                dve.wait_ge(lam_ready, 3)
                maximum(0, 0, 0)
                maximum(0, 1, 0)
                inverse(0, 0)
                difference(0, 0)

                def group(g, gm, last):
                    for c in range(GROUP):
                        t = g * GROUP + c
                        p = (c + 1) % 2
                        nxt = not (last and c == GROUP - 1)
                        if nxt:
                            maximum(t + 1, 0, p)
                            maximum(t + 1, 1, p)
                            inverse(t + 1, p)
                        if c == 0 and not (isinstance(g, int) and g == 0):
                            finish(g)
                        low(g, c, 0)
                        if nxt and c < GROUP:
                            difference(t + 1, p)
                        low(g, c, 1)
                        low(g, c, 2)

                run(dve, group)
                finish(GROUPS)


def output(nc, io, keep, layer, src, weights, residual, dst, nxt):
    with ExitStack() as stack:
        m = Memory(nc, stack, f"out{layer}")
        w_hi = m.sb("w_hi", [P, KT, D], F32R)
        w_lo = m.sb("w_lo", [P, KT, D], F32R)
        stage = m.sb("stage", [P, 2, D])
        s_hi = m.sb("s_hi", [P, 2, KT, P], F32R)
        s_lo = m.sb("s_lo", [P, 2, KT, P], F32R)
        res = m.sb("res", [P, 2, D])
        row = m.sb("row", [P, 2, D])
        done = m.sb("done", [P, 2, D])
        hf = m.sb("hf", [P, KT, P])
        ln_g = m.sb("ln_g", [P, D])
        ln_b = m.sb("ln_b", [P, D])
        stats = m.sb("stats", [P, 2, 2, 6])
        mv = m.sb("mv", [P, 2, 2])
        rstd = m.sb("rstd", [P, 2])
        note = m.sb("note", [P, 4])
        hold_out = m.sb("hold_out", [P, 1])
        ps = m.psum("ps", [P, 8, BANK])

        names = ("row_in", "w_hi_done", "w_lo_done", "proj_ready", "prod_done", "sum_done", "stats_done", "mv_done",
                 "std_done", "rstd_done", "norm_done", "weighted", "done_ready", "t_ready", "h_done", "h_hi_done",
                 "h_lo_done")
        (row_in, w_hi_done, w_lo_done, proj_ready, prod_done, sum_done, stats_done, mv_done, std_done, rstd_done,
         norm_done, weighted, done_ready, t_ready, h_done, h_hi_done, h_lo_done) = (m.sem(n) for n in names)
        stage_in = [m.sem("stage_in0"), m.sem("stage_in1")]
        src_in = [m.sem("src_in0"), m.sem("src_in1")]
        res_in = [m.sem("res_in0"), m.sem("res_in1")]
        done_out = [m.sem("done_out0"), m.sem("done_out1")]

        def run(eng, tile):
            tile(0, 0, 0)
            with eng.Fori(0, 3) as i:
                tile(i * 2 + 1, i, 1)
                tile(i * 2 + 2, i + 1, 0)
            tile(QT - 1, 3, 1)

        with nc.Block() as block:
            @block.sync
            def _(sp):
                def load_tile(n, p):
                    cols = ds(n * P, P)
                    for part, buf in ((0, s_hi), (1, s_lo)):
                        view = src[part * D:(part + 1) * D, :].rearrange("(k p) t -> p k t", p=P)
                        sp.dma_start(buf[:, p, :, :].bitcast(F32), view[:, :, cols]).then_inc(src_in[p], 16)
                    sp.dma_start(res[:, p, :], residual[ds(n * P, P), :]).then_inc(res_in[p], 16)

                load_tile(0, 0)
                for kt in range(KT):
                    if kt >= 2:
                        sp.wait_ge(w_lo_done, kt - 1)
                    sp.dma_start(stage[:, kt % 2, :], weights[kt * P:(kt + 1) * P, :]).then_inc(stage_in[kt % 2], 16)
                sp.dma_start(ln_g[:], io["ln_g"][layer:layer + 1, :].partition_broadcast(P)
                             .rearrange("p a n -> p (a n)")).then_inc(row_in, 16)
                sp.dma_start(ln_b[:], io["ln_b"][layer:layer + 1, :].partition_broadcast(P)
                             .rearrange("p a n -> p (a n)")).then_inc(row_in, 16)
                load_tile(1, 1)

                def tile(n, k, p):
                    if not (isinstance(n, int) and n == QT - 1):
                        sp.wait_ge(proj_ready, n + 1)
                        sp.wait_ge(sum_done, n + 1)
                        load_tile(n + 2, p)
                    sp.wait_ge(done_ready, n + 3)
                    sp.dma_start(dst[ds(n * P, P), :], done[:, p, :]).then_inc(done_out[p], 16)

                tile(0, 0, 0)
                with sp.Fori(0, 2) as i:
                    tile(i * 2 + 1, None, 1)
                    tile(i * 2 + 2, None, 0)
                tile(5, None, 1)
                for n in (6, 7):
                    sp.wait_ge(done_ready, n + 3)
                    sp.dma_start(dst[n * P:(n + 1) * P, :], done[:, n % 2, :]).then_inc(done_out[n % 2], 16)
                for p in range(2):
                    sp.wait_ge(done_out[p], 16 + 16 * QT // 2)

            @block.tensor
            def _(pe):
                def product(n, k, p):
                    pe.wait_ge(src_in[p], k * 32 + 32)
                    pe.wait_ge(prod_done, n + 1)
                    for kt in range(KT):
                        if isinstance(n, int) and n == 0:
                            pe.wait_ge(w_lo_done, kt + 1)
                        for s, parts in ((s_hi, (w_hi, w_lo)), (s_lo, (w_hi,))):
                            for w in parts:
                                for half in range(2):
                                    last = nc.tensor.matmul(
                                        ps[:, 2 * p + half, :], s[:, p, kt, :],
                                        w[:, kt, half * BANK:(half + 1) * BANK],
                                        start=(kt == 0 and s is s_hi and w is w_hi),
                                        stop=(kt == KT - 1 and s is s_lo))
                    last.then_inc(proj_ready, 1)

                def transposes(n, p):
                    pe.wait_ge(done_ready, n + 3)
                    pe.wait_ge(h_done, n + 1)
                    for kt in range(KT):
                        last = nc.tensor.transpose(ps[:, 4 + 2 * p + kt // 4, (kt % 4) * P:(kt % 4 + 1) * P],
                                                   done[:, p, kt * P:(kt + 1) * P], keep.ident[:])
                    last.then_inc(t_ready, 1)

                def tile(n, k, p):
                    product(n, k, p)
                    if nxt and not (isinstance(n, int) and n == 0):
                        transposes(n - 1, 1 - p)

                run(pe, tile)
                if nxt:
                    transposes(QT - 1, 1)

            @block.scalar
            def _(act):
                nc.scalar.activation(note[:, 0:1], keep.eps[:], ACT.Copy).then_inc(h_done, 2)
                nc.scalar.activation(note[:, 1:2], keep.eps[:], ACT.Copy).then_inc(t_ready, 2)
                for p in range(2):
                    nc.scalar.activation(done[:, p, 0:1], keep.eps[:], ACT.Copy).then_inc(done_out[p], 16)
                for kt in range(KT):
                    act.wait_ge(stage_in[kt % 2], 16 * (kt // 2 + 1))
                    nc.scalar.activation(w_hi[:, kt, :], stage[:, kt % 2, :], ACT.Copy).then_inc(w_hi_done, 1)

                def tile(n, k, p):
                    act.wait_ge(mv_done, n + 1)
                    nc.scalar.activation(rstd[:, p:p + 1], mv[:, p, 1:2], ACT.Sqrt,
                                         bias=keep.eps[:]).then_inc(std_done, 1)
                    if nxt and not (isinstance(n, int) and n == 0):
                        modulate(n - 1, 1 - p)

                def modulate(n, p):
                    act.wait_ge(t_ready, n + 3)
                    act.wait_ge(h_lo_done, n + 1)
                    for kt in range(KT):
                        last = nc.scalar.activation(
                            hf[:, kt, :], ps[:, 4 + 2 * p + kt // 4, (kt % 4) * P:(kt % 4 + 1) * P], ACT.Identity,
                            bias=keep.mod1[:, 0, kt:kt + 1], scale=keep.mod1[:, 1, kt:kt + 1])
                    last.then_inc(h_done, 1)

                run(act, tile)
                if nxt:
                    modulate(QT - 1, 1)

            @block.vector
            def _(dve):
                nc.vector.memset(stats[:, 0, 0, 0:1], 0.0).then_inc(prod_done, 2)
                nc.vector.memset(stats[:, 0, 0, 1:2], 0.0).then_inc(h_lo_done, 1)
                nc.vector.memset(stats[:, 0, 0, 2:3], 0.0).then_inc(done_ready, 2)
                for kt in range(KT):
                    dve.wait_ge(w_hi_done, kt + 1)
                    nc.vector.tensor_sub(w_lo[:, kt, :], stage[:, kt % 2, :],
                                         w_hi[:, kt, :].bitcast(F32)).then_inc(w_lo_done, 1)

                def tile(n, k, p):
                    dve.wait_ge(proj_ready, n + 1)
                    dve.wait_ge(done_ready, n + 1)
                    two = row[:, p, :].rearrange("p (b n) -> p b n", b=2)
                    gate = keep.gate[:, layer, :].rearrange("p (b n) -> p b n", b=2)
                    nc.vector.tensor_tensor(two, ps[:, 2 * p:2 * p + 2, :], gate, ALU.mult).then_inc(prod_done, 1)
                    dve.wait_ge(res_in[p], k * 16 + 16)
                    dve.wait_ge(prod_done, n + 3)
                    nc.vector.scalar_tensor_tensor(out=row[:, p, :], in0=res[:, p, :], scalar=ALPHA, in1=row[:, p, :],
                                                   op0=ALU.mult, op1=ALU.add).then_inc(sum_done, 1)
                    dve.wait_ge(sum_done, n + 1)
                    for half in range(2):
                        nc.vector.bn_stats(stats[:, p, half, :],
                                           row[:, p, half * BANK:(half + 1) * BANK]).then_inc(stats_done, 1)
                    dve.wait_ge(stats_done, n * 2 + 2)
                    nc.vector.memset(note[:, 3:4], 0.0)
                    nc.vector.bn_aggr(mv[:, p, :], stats[:, p, :, :].rearrange("p a b -> p (a b)")).then_inc(mv_done, 1)
                    dve.wait_ge(std_done, n + 1)
                    nc.vector.reciprocal(rstd[:, p:p + 1], rstd[:, p:p + 1]).then_inc(rstd_done, 1)
                    dve.wait_ge(rstd_done, n + 1)
                    nc.vector.tensor_scalar(row[:, p, :], row[:, p, :], mv[:, p, 0:1], rstd[:, p:p + 1],
                                            ALU.subtract, ALU.mult).then_inc(norm_done, 1)
                    if nxt and not (isinstance(n, int) and n == 0):
                        low(n - 1)

                def low(n):
                    dve.wait_ge(h_hi_done, n + 1)
                    nc.vector.tensor_sub(keep.h_lo[:, :, ds(n * P, P)], hf[:],
                                         keep.h_hi[:, :, ds(n * P, P)].bitcast(F32)).then_inc(h_lo_done, 1)

                run(dve, tile)
                if nxt:
                    low(QT - 1)

            @block.gpsimd
            def _(pool):
                pool.wait_ge(row_in, 32)

                def tile(n, k, p):
                    pool.wait_ge(norm_done, n + 1)
                    nc.gpsimd.tensor_mul(row[:, p, :], row[:, p, :], ln_g[:]).then_inc(weighted, 1)
                    pool.wait_ge(weighted, n + 1)
                    pool.wait_ge(done_out[p], k * 16 + 16)
                    if nxt:
                        pool.wait_ge(t_ready, n + 1)
                    nc.gpsimd.tensor_add(done[:, p, :], row[:, p, :], ln_b[:]).then_inc(done_ready, 1)
                    if nxt and not (isinstance(n, int) and n == 0):
                        high(n - 1)

                def high(n):
                    pool.wait_ge(h_done, n + 3)
                    nc.gpsimd.tensor_add(hold_out[:], ln_b[:, 0:1], ln_b[:, 1:2])
                    nc.gpsimd.tensor_copy(keep.h_hi[:, :, ds(n * P, P)], hf[:]).then_inc(h_hi_done, 1)

                run(pool, tile)
                if nxt:
                    high(QT - 1)


def conform(nc, io, keep):
    with ExitStack() as outer:
        mo = Memory(nc, outer, "cf")
        conv = mo.sb("conv", [P, KT, L])
        z_s = mo.sb("z_s", [P, KT, L])
        total = mo.sb("total", [P, L])
        mean_w = mo.sb("mean_w", [P, P])
        ps = mo.psum("ps", [P, 8, BANK])
        with ExitStack() as stack:
            m = Memory(nc, stack, "cg")
            w_hi = m.sb("w_hi", [P, 3, PIECE], F32R)
            w_lo = m.sb("w_lo", [P, 3, PIECE], F32R)
            stage = m.sb("stage", [P, 2, PIECE])
            padded = m.sb("padded", [P, 2, L + 2 * PAD])
            sig = m.sb("sig", [P, L])
            odd = m.sb("odd", [P, L])
            taps = m.sb("taps", [P, KT * CONF_KW])
            note = m.sb("note", [P, 4])
            (tap_in, w_hi_done, w_lo_done, g_ready, a_ready, z_ready, sig_done, glu_done, z_done, conv_step,
             total_done, pad_done) = (m.sem(n) for n in (
                 "tap_in", "w_hi_done", "w_lo_done", "g_ready", "a_ready", "z_ready", "sig_done", "glu_done",
                 "z_done", "conv_step", "total_done", "pad_done"))
            stage_in = [m.sem("stage_in0"), m.sem("stage_in1")]
            STEPS = CONF_KW + 1

            with nc.Block() as block:
                @block.sync
                def _(sp):
                    for g in range(2):
                        sp.dma_start(stage[:, g, :], io["conf_w"][g * P:(g + 1) * P, :]).then_inc(stage_in[g], 16)
                    sp.dma_start(taps[:], io["taps"]).then_inc(tap_in, 16)
                    with sp.Fori(0, 11) as i:
                        for b in range(2):
                            sp.wait_ge(w_lo_done, i * 2 + (b + 1))
                            sp.dma_start(stage[:, b, :],
                                         io["conf_w"][ds(i * (2 * P) + (2 + b) * P, P), :]).then_inc(stage_in[b], 16)

                @block.tensor
                def _(pe):
                    def part(c, kind, ready, free):
                        pe.wait_ge(w_lo_done, c * 3 + (kind + 1))
                        pe.wait_ge(free, c + 1)
                        for kt in range(KT):
                            for w, parts in ((w_hi, (keep.h_hi, keep.h_lo)), (w_lo, (keep.h_hi,))):
                                for h in parts:
                                    for half in range(2):
                                        last = nc.tensor.matmul(
                                            ps[:, 2 * kind + half, :], w[:, kind, kt * P:(kt + 1) * P],
                                            h[:, kt, half * BANK:(half + 1) * BANK],
                                            start=(kt == 0 and w is w_hi and h is keep.h_hi),
                                            stop=(kt == KT - 1 and w is w_lo))
                        last.then_inc(ready, 1)

                    with pe.Fori(0, KT) as c:
                        part(c, 0, g_ready, sig_done)
                        part(c, 1, a_ready, glu_done)
                        part(c, 2, z_ready, z_done)

                @block.scalar
                def _(act):
                    for n, s in enumerate((sig_done, z_done)):
                        nc.scalar.activation(note[:, n:n + 1], keep.eps[:], ACT.Copy).then_inc(s, 1)

                    def split(g, slot, kind, loads):
                        act.wait_ge(stage_in[slot], loads * 16)
                        nc.scalar.activation(w_hi[:, kind, :], stage[:, slot, :], ACT.Copy).then_inc(w_hi_done, 1)

                    def tile(c, n, following):
                        act.wait_ge(g_ready, c + 1)
                        act.wait_ge(glu_done, c + 1)
                        nc.scalar.activation(sig[:].rearrange("p (b n) -> p b n", b=2), ps[:, 0:2, :],
                                             ACT.Sigmoid).then_inc(sig_done, 1)
                        if following:
                            piece(c, n, 0)
                            act.wait_ge(a_ready, c + 1)
                            piece(c, n, 1)
                        act.wait_ge(z_ready, c + 1)
                        nc.scalar.activation(z_s[:, ds(c, 1), :].rearrange("p a (b n) -> p (a b) n", b=2),
                                             ps[:, 4:6, :], ACT.Silu).then_inc(z_done, 1)
                        if following:
                            piece(c, n, 2)

                    def piece(c, n, kind):
                        g = 3 * n + 3 + kind
                        i = (c - n) // 2 if isinstance(c, int) else half_c[0]
                        split(None, g % 2, kind, i * 3 + (g // 2 + 1))

                    half_c = [None]
                    for g in range(3):
                        split(g, g % 2, g, g // 2 + 1)
                    with act.Fori(0, 3) as i:
                        half_c[0] = i
                        tile(i * 2, 0, True)
                        tile(i * 2 + 1, 1, True)
                    tile(6, 0, True)
                    tile(7, 1, False)

                @block.gpsimd
                def _(pool):
                    nc.gpsimd.memset(mean_w[:], 1.0 / D)
                    nc.gpsimd.memset(total[:], 0.0).then_inc(total_done, 1)

                    def low(g, slot, kind):
                        pool.wait_ge(w_hi_done, g + 1)
                        nc.gpsimd.tensor_sub(w_lo[:, kind, :], stage[:, slot, :],
                                             w_hi[:, kind, :].bitcast(F32)).then_inc(w_lo_done, 1)

                    def add_total(c):
                        pool.wait_ge(conv_step, c * STEPS)
                        pool.wait_ge(total_done, c)
                        nc.gpsimd.tensor_add(total[:], total[:],
                                             conv[:, ds(c - 1, 1), :].rearrange("p a n -> p (a n)")
                                             ).then_inc(total_done, 1)

                    for g in range(3):
                        low(g, g % 2, g)

                    def tile(c, n):
                        for kind in range(3):
                            low(c * 3 + (3 + kind), (3 * n + 3 + kind) % 2, kind)
                        if not (isinstance(c, int) and c == 0):
                            add_total(c)

                    tile(0, 0)
                    with pool.Fori(0, 3) as i:
                        tile(i * 2 + 1, 1)
                        tile(i * 2 + 2, 0)
                    add_total(7)
                    add_total(8)

                @block.vector
                def _(dve):
                    nc.vector.memset(padded[:, :, 0:PAD], 0.0)
                    nc.vector.memset(padded[:, :, PAD + L:], 0.0).then_inc(pad_done, 1)
                    nc.vector.memset(odd[:, 0:1], 0.0).then_inc(glu_done, 1)
                    dve.wait_ge(tap_in, 16)
                    dve.wait_ge(pad_done, 1)

                    def tile(c, q):
                        dve.wait_ge(a_ready, c + 1)
                        dve.wait_ge(sig_done, c + 2)
                        nc.vector.tensor_tensor(padded[:, q, PAD:PAD + L].rearrange("p (b n) -> p b n", b=2),
                                                ps[:, 2:4, :], sig[:].rearrange("p (b n) -> p b n", b=2),
                                                ALU.mult).then_inc(glu_done, 1)
                        dve.wait_ge(glu_done, c + 2)
                        even = conv[:, ds(c, 1), :].rearrange("p a n -> p (a n)")

                        def tap(k):
                            return taps[:, ds(c * CONF_KW + k, 1)]

                        nc.vector.tensor_scalar(even, padded[:, q, 0:L], tap(0), keep.vcol[:, ds(c + V_DWB, 1)],
                                                ALU.mult, ALU.add).then_inc(conv_step, 1)
                        nc.vector.tensor_scalar(odd[:], padded[:, q, 1:1 + L], tap(1), None,
                                                ALU.mult).then_inc(conv_step, 1)
                        for k in range(2, CONF_KW):
                            dve.wait_ge(conv_step, c * STEPS + (k - 1))
                            into = even if k % 2 == 0 else odd[:]
                            nc.vector.scalar_tensor_tensor(out=into, in0=padded[:, q, k:k + L], scalar=tap(k),
                                                           in1=into, op0=ALU.mult, op1=ALU.add).then_inc(conv_step, 1)
                        dve.wait_ge(conv_step, c * STEPS + CONF_KW)
                        nc.vector.tensor_add(even, even, odd[:]).then_inc(conv_step, 1)
                        dve.wait_ge(conv_step, c * STEPS + STEPS)

                    with dve.Fori(0, KT // 2) as i:
                        tile(i * 2, 0)
                        tile(i * 2 + 1, 1)

        with ExitStack() as stack:
            m = Memory(nc, stack, "cn")
            square = m.sb("square", [P, 2, L])
            rstd = m.sb("rstd", [P, L])
            y_hi = m.sb("y_hi", [P, 2, L])
            y_lo = m.sb("y_lo", [P, 2, L])
            (mean_ready, centred, sq_done, sq_used, std_done, rstd_done, scaled, act_done, gated, y_hi_done,
             y_lo_done) = (m.sem(n) for n in ("mean_ready", "centred", "sq_done", "sq_used", "std_done", "rstd_done",
                                              "scaled", "act_done", "gated", "y_hi_done", "y_lo_done"))
            y_out = [m.sem("y_out0"), m.sem("y_out1")]

            with nc.Block() as block:
                @block.tensor
                def _(pe):
                    for half in range(2):
                        last = nc.tensor.matmul(ps[:, half, :], mean_w[:], total[:, half * BANK:(half + 1) * BANK],
                                                start=True, stop=True)
                    last.then_inc(mean_ready, 1)
                    for c in range(KT):
                        pe.wait_ge(sq_done, c + 1)
                        for half in range(2):
                            last = nc.tensor.matmul(ps[:, 2 + half, :], mean_w[:],
                                                    square[:, c % 2, half * BANK:(half + 1) * BANK],
                                                    start=c == 0, stop=c == KT - 1)
                        last.then_inc(sq_used, 1)

                @block.vector
                def _(dve):
                    dve.wait_ge(mean_ready, 1)
                    for c in range(KT):
                        two = conv[:, c, :].rearrange("p (b n) -> p b n", b=2)
                        nc.vector.tensor_tensor(two, two, ps[:, 0:2, :], ALU.subtract).then_inc(centred, 1)
                    dve.wait_ge(centred, KT)
                    dve.wait_ge(std_done, 1)
                    nc.vector.reciprocal(rstd[:], rstd[:]).then_inc(rstd_done, 1)
                    dve.wait_ge(rstd_done, 1)

                    def low(c):
                        dve.wait_ge(y_hi_done, c + 1)
                        nc.vector.tensor_sub(y_lo[:, c % 2, :].bitcast(F32R), conv[:, c, :],
                                             y_hi[:, c % 2, :]).then_inc(y_lo_done, 1)

                    for c in range(KT):
                        nc.vector.tensor_mul(conv[:, c, :], conv[:, c, :], rstd[:]).then_inc(scaled, 1)
                        if c >= 3:
                            low(c - 3)
                    for c in range(KT - 3, KT):
                        low(c)

                @block.scalar
                def _(act):
                    for c in range(KT):
                        act.wait_ge(centred, c + 1)
                        if c >= 2:
                            act.wait_ge(sq_used, c - 1)
                        nc.scalar.activation(square[:, c % 2, :], conv[:, c, :], ACT.Square).then_inc(sq_done, 1)
                    act.wait_ge(sq_used, KT)
                    nc.scalar.activation(rstd[:].rearrange("p (b n) -> p b n", b=2), ps[:, 2:4, :], ACT.Sqrt,
                                         bias=keep.eps[:]).then_inc(std_done, 1)

                    def high(c):
                        act.wait_ge(gated, c + 1)
                        if c >= 2:
                            act.wait_ge(y_out[c % 2], 32 * (c // 2))
                        nc.scalar.activation(y_hi[:, c % 2, :].bitcast(F32R), conv[:, c, :],
                                             ACT.Copy).then_inc(y_hi_done, 1)

                    for c in range(KT):
                        act.wait_ge(scaled, c + 1)
                        nc.scalar.activation(conv[:, c, :], conv[:, c, :], ACT.Silu,
                                             scale=keep.vcol[:, V_CLNG + c:V_CLNG + c + 1],
                                             bias=keep.vcol[:, V_CLNB + c:V_CLNB + c + 1]).then_inc(act_done, 1)
                        if c >= 2:
                            high(c - 2)
                    for c in range(KT - 2, KT):
                        high(c)

                @block.gpsimd
                def _(pool):
                    for c in range(KT):
                        pool.wait_ge(act_done, c + 1)
                        nc.gpsimd.tensor_mul(conv[:, c, :], conv[:, c, :], z_s[:, c, :]).then_inc(gated, 1)

                @block.sync
                def _(sp):
                    for c in range(KT):
                        sp.wait_ge(y_lo_done, c + 1)
                        for part, buf in ((0, y_hi), (1, y_lo)):
                            sp.dma_start(io["y_hl"][part * D + c * P:part * D + (c + 1) * P, :],
                                         buf[:, c % 2, :]).then_inc(y_out[c % 2], 16)
                    for p in range(2):
                        sp.wait_ge(y_out[p], 32 * KT // 2)


class Keep:
    pass


def build(nc, io, out):
    with ExitStack() as stack:
        m = Memory(nc, stack, "keep")
        keep = Keep()
        keep.vcol = m.sb("vcol", [P, V_N])
        keep.gate = m.sb("gate", [P, DEPTH, D])
        keep.mod1 = m.sb("mod1", [P, 2, KT])
        keep.ones = m.sb("ones", [P, P])
        keep.ident = m.sb("ident", [P, P])
        keep.eps = m.sb("eps", [P, 1])
        keep.subln = m.sb("subln", [P, 1])
        project(nc, io, keep)
        attend(nc, io, keep)
        keep_h = Memory(nc, stack, "h")
        keep.h_hi = keep_h.sb("hi", [P, KT, L], F32R)
        keep.h_lo = keep_h.sb("lo", [P, KT, L], F32R)
        output(nc, io, keep, 0, io["og_hl"], io["attn_w_out"], io["x"], io["x1"], True)
        conform(nc, io, keep)
        output(nc, io, keep, 1, io["y_hl"], io["conf_w_out"], io["x1"], out, False)


def rope_tables():
    import numpy as np
    half = DK // 2
    inv = (1.0 / (np.float32(10000.0) ** (np.arange(0, half, 2, dtype=np.float32) / half))).astype(np.float32)
    t = np.arange(L)
    ar = (t // 64).astype(np.float32)[:, None] * inv[None, :]
    ac = (t % 64).astype(np.float32)[:, None] * inv[None, :]
    ang = np.concatenate([ar, ar, ac, ac], axis=-1)
    sign = np.where(np.arange(DK) % half < half // 2, -1.0, 1.0).astype(np.float32)
    cos, sin = np.cos(ang), np.sin(ang) * sign
    both = np.concatenate([cos.T, sin.T], axis=1)
    return np.ascontiguousarray(np.concatenate([both, both], axis=0).astype(np.float32))


def kernel(x, c, ctx, c_ctx, mod_w, mod_b, ln_g, ln_b,
           attn_w_in, attn_w_out, attn_lambda_q1, attn_lambda_k1, attn_lambda_q2, attn_lambda_k2, attn_subln_g,
           conf_w_in, conf_dw_w, conf_dw_b, conf_ln_g, conf_ln_b, conf_w_out,
           sc_w_in, sc_conv_w, sc_w_out,
           pool_w_in, pool_w_group, pool_scale, pool_w_out):
    import numpy as np
    import concourse.bacc as bacc
    from concourse.bass_utils import run_bass_kernel_spmd

    a = lambda v: np.asarray(v)
    tokens = np.concatenate([a(x)[0], a(ctx)[0]], axis=0)
    cols = [a(c)[0], a(c_ctx), a(mod_b).reshape(-1), a(conf_dw_b)[0], a(conf_ln_g)[0], a(conf_ln_b)[0],
            a(attn_subln_g)[0]]
    vec = np.concatenate([v.reshape(-1, P) for v in cols], axis=0).T

    def pieces(w):
        n = w.shape[1] // P
        return w.reshape(KT, P, n, P).transpose(2, 1, 0, 3).reshape(n, P, PIECE)

    w_in = a(attn_w_in)[0]
    v_w = w_in[:, 2 * D:3 * D].reshape(4, 2, P, 2, BANK)
    v_w = v_w.transpose(3, 0, 2, 1, 4).reshape(8, P, PIECE)
    w_in = np.concatenate([pieces(w_in[:, :2 * D]), pieces(w_in[:, 3 * D:]), v_w], axis=0)
    conf = pieces(a(conf_w_in)[0]).reshape(3, KT, P, PIECE)
    conf = conf[[1, 0, 2]].transpose(1, 0, 2, 3).reshape(3 * KT * P, PIECE)
    taps = a(conf_dw_w)[0].reshape(CONF_KW, KT, P).transpose(2, 1, 0).reshape(P, KT * CONF_KW)
    arrays = {
        "x": a(x)[0], "x_t": tokens.T.reshape(KT, P, LT), "vec": vec, "mod_w": a(mod_w), "mod_b": a(mod_b),
        "ln_g": a(ln_g), "ln_b": a(ln_b), "w_in": w_in, "attn_w_out": a(attn_w_out)[0],
        "lam": np.stack([a(v)[0] for v in (attn_lambda_q1, attn_lambda_k1, attn_lambda_q2, attn_lambda_k2)])[None],
        "rope": rope_tables(), "conf_w": conf, "taps": taps, "conf_w_out": a(conf_w_out)[0],
    }
    arrays = {k: np.ascontiguousarray(v) for k, v in arrays.items()}
    nc = bacc.Bacc("TRN2", target_bir_lowering=False, num_devices=1)
    io = {k: nc.dram_tensor(f"in_{k}", v.shape, mybir.dt.from_np(v.dtype), kind="ExternalInput").ap()
          for k, v in arrays.items()}
    for name, shape in (("q_hl", (HEADS * 2 * P, L)), ("k_hl", (HEADS * 2 * P, LT)), ("v_hl", (2, KEYT, P, D)),
                        ("z_s", (D, L)), ("og_hl", (2 * D, L)), ("x1", (L, D)), ("y_hl", (2 * D, L))):
        io[name] = nc.dram_tensor(f"scratch_{name}", shape, F32, kind="Internal").ap()
    out = nc.dram_tensor("out", (L, D), F32, kind="ExternalOutput").ap()
    build(nc, io, out)
    r = run_bass_kernel_spmd(nc, [{f"in_{k}": v for k, v in arrays.items()}], core_ids=[0])
    return r.results[0]["out"].reshape(1, L, D)
```

```python
import math
from contextlib import ExitStack

import concourse.bass as bass
from concourse import mybir

F32 = mybir.dt.float32
F32R = mybir.dt.float32r
ALU = mybir.AluOpType
ACT = mybir.ActivationFunctionType
AX = mybir.AxisListType

P = 128
D = 1024
KT = D // P
L = 1024
LC = 256
LT = L + LC
HEADS = 8
DK = 64
DV = 128
BANK = 512
HALVES = L // BANK
QT = L // P
KEYT = LT // P
CONF_KW = 31
PAD = (CONF_KW - 1) // 2
DEPTH = 2
ALPHA = (2 * DEPTH) ** 0.25
LAMBDA_INIT = 0.8 - 0.6 * math.exp(-0.3 * 0)
EPS = 1e-5
PIECE = KT * P
MASK_HALF_SWAP = list(range(16, 32)) + list(range(16))

V_C, V_CCTX, V_MODB, V_DWB, V_CLNG, V_CLNB, V_SUBG = 0, 8, 16, 64, 72, 80, 88
V_N = 89


def ds(i, n):
    return bass.ds(i, n)


class Memory:

    def __init__(self, nc, stack, tag):
        self.nc, self.stack, self.tag = nc, stack, tag

    def sb(self, name, shape, dt=F32):
        return self.stack.enter_context(self.nc.sbuf_tensor(f"{self.tag}_{name}", shape, dt))

    def psum(self, name, shape):
        return self.stack.enter_context(self.nc.psum_tensor(f"{self.tag}_{name}", shape, F32))

    def sem(self, name):
        return self.stack.enter_context(self.nc.semaphore(f"{self.tag}_{name}"))


def project(nc, io, keep):
    UQK, UZ = 2 * HEADS, HEADS
    UNITS = UQK + UZ
    with ExitStack() as stack:
        m = Memory(nc, stack, "pj")
        work = m.sb("work", [P, KT, LT])
        h_hi = m.sb("h_hi", [P, KT, LT], F32R)
        h_lo = m.sb("h_lo", [P, KT, LT], F32R)
        w_hi = m.sb("w_hi", [P, 4, PIECE], F32R)
        w_lo = m.sb("w_lo", [P, 4, PIECE], F32R)
        stage = m.sb("stage", [P, 2, PIECE])
        mod_tile = m.sb("mod_tile", [P, 2, D])
        acc = m.sb("acc", [P, 2, D])
        cos = m.sb("cos", [P, L])
        sin = m.sb("sin", [P, L])
        silu_c = m.sb("silu_c", [P, 2 * KT])
        mod0 = m.sb("mod0", [P, 2, 2, KT])
        note = m.sb("note", [P, 10])
        low_note = m.sb("low_note", [P, 1])
        ps = m.psum("ps", [P, 8, BANK])

        straight = [work[:, 0, :], work[:, 1, :]]
        turned = work[:, 2, :]
        out_hi = [work[:, 3, :], work[:, 4, :]]
        out_lo = [work[:, 5, :], work[:, 6, :]]

        vec_in, x_in, table_in = m.sem("vec_in"), m.sem("x_in"), m.sem("table_in")
        mod_in = [m.sem("mod_in0"), m.sem("mod_in1")]
        stage_in = [m.sem("stage_in0"), m.sem("stage_in1")]
        silu_done, ones_done = m.sem("silu_done"), m.sem("ones_done")
        mod_acc, mod_sums, mod_ready = m.sem("mod_acc"), m.sem("mod_sums"), m.sem("mod_ready")
        gate_done = m.sem("gate_done")
        h_mod, h_hi_done, h_lo_done = m.sem("h_mod"), m.sem("h_hi_done"), m.sem("h_lo_done")
        w_hi_done, w_lo_done = m.sem("w_hi_done"), m.sem("w_lo_done")
        proj_ready, proj_evac = m.sem("proj_ready"), m.sem("proj_evac")
        swapped, sin_done, cos_done = m.sem("swapped"), m.sem("sin_done"), m.sem("cos_done")
        rope_done, out_hi_done, out_lo_done = m.sem("rope_done"), m.sem("out_hi_done"), m.sem("out_lo_done")
        v_hi_done, v_lo_done = m.sem("v_hi_done"), m.sem("v_lo_done")
        qk_out = [m.sem("qk_out0"), m.sem("qk_out1")]
        z_out = [m.sem("z_out0"), m.sem("z_out1")]
        v_out = [m.sem("v_out0"), m.sem("v_out1")]

        MOD0 = 36
        vcol = keep.vcol
        mod_w = io["mod_w"].rearrange("l d n -> (l d) n")

        with nc.Block() as block:
            @block.sync
            def _(sp):
                sp.dma_start(vcol[:], io["vec"]).then_inc(vec_in, 16)

                def load_mod(slot, rows, cols):
                    sp.dma_start(mod_tile[:, slot, :], mod_w[rows, cols]).then_inc(mod_in[slot], 16)

                for q in range(2):
                    for t in range(KT):
                        n = KT * q + t
                        if n >= 2:
                            sp.wait_ge(mod_acc, 18 * ((n - 2) // KT) + 2 + 2 * ((n - 2) % KT) + 2)
                        load_mod(n % 2, slice(t * P, (t + 1) * P), slice(q * D, (q + 1) * D))
                    if q == 0:
                        for g in range(2):
                            sp.dma_start(stage[:, g, :], io["w_in"][g]).then_inc(stage_in[g], 16)
                sp.dma_start(cos[:], io["rope"][:, 0:L]).then_inc(table_in, 16)
                sp.dma_start(sin[:], io["rope"][:, L:2 * L]).then_inc(table_in, 16)
                sp.wait_ge(w_lo_done, 1)
                sp.dma_start(stage[:, 0, :], io["w_in"][2]).then_inc(stage_in[0], 16)

                def load_piece(g, slot):
                    sp.wait_ge(w_lo_done, g - 1)
                    sp.dma_start(stage[:, slot, :], io["w_in"][ds(g, 1)].rearrange("a p n -> (a p) n")
                                 if not isinstance(g, int) else io["w_in"][g]).then_inc(stage_in[slot], 16)

                for kind, scratch, width in ((0, io["q_hl"], L), (1, io["k_hl"], LT)):
                    with sp.Fori(0, 2) as i:
                        for j in range(4):
                            u = i * 4 + (HEADS * kind + j)
                            load_piece(u + 3, (j + 3) % 2)
                            sp.wait_ge(out_lo_done, u + 2)
                            for part, buf in ((0, out_hi), (1, out_lo)):
                                sp.dma_start(scratch[ds((i * 4 + j) * (2 * P) + part * P, P), :],
                                             buf[j % 2][:, 0:width]).then_inc(qk_out[j % 2], 16)
                with sp.Fori(0, 2) as i:
                    for j in range(4):
                        u = i * 4 + (UQK + j)
                        load_piece(u + 3, (j + 3) % 2)
                        for b in range(4):
                            step = 4 * j + b
                            before = (step - 2 + (1 if step - 2 < 8 else 2) + 1) if step >= 2 else step - 1
                            sp.wait_ge(mod_acc, i * 18 + (MOD0 + before))
                            t = 4 * (j % 2) + b
                            if j < 2:
                                load_mod(b % 2, ds(i * D + t * P, P), slice(2 * D, 3 * D))
                            else:
                                load_mod(b % 2, slice(D + t * P, D + (t + 1) * P), ds(i * D, D))
                        sp.wait_ge(proj_evac, u + 3)
                        sp.dma_start(io["z_s"][ds((i * 4 + j) * P, P), :],
                                     straight[j % 2][:, 0:L]).then_inc(z_out[j % 2], 16)
                load_piece(27, 1)
                for vc in range(2):
                    for tt in range(KEYT):
                        n = KEYT * vc + tt
                        if vc == 0 and tt in (1, 2):
                            load_piece(27 + tt, (27 + tt) % 2)
                        if vc == 1 and tt == 0:
                            load_piece(30, 0)
                            load_piece(31, 1)
                        sp.wait_ge(v_lo_done, n + 3)
                        for part, buf in ((0, out_hi), (1, out_lo)):
                            sp.dma_start(io["v_hl"][part, tt, :, vc * BANK:(vc + 1) * BANK],
                                         buf[n % 2][:, 0:BANK]).then_inc(v_out[n % 2], 16)
                for p in range(2):
                    sp.wait_ge(qk_out[p], 32 + 32 * UQK // 2)
                    sp.wait_ge(z_out[p], 16 + 16 * UZ // 2)
                    sp.wait_ge(v_out[p], 32 * KEYT)

            @block.gpsimd
            def _(pool):
                nc.gpsimd.memset(keep.ones[:], 1.0).then_inc(ones_done, 1)
                nc.gpsimd.memset(keep.eps[:], EPS)
                nc.gpsimd.memset(keep.ident[:], 0.0).then_inc(ones_done, 1)
                pool.wait_ge(ones_done, 2)
                nc.gpsimd.affine_select(out=keep.ident[:], in_=keep.ident[:], compare_op=ALU.not_equal, fill=1.0,
                                        base=0, pattern=[[-1, P]], channel_multiplier=1).then_inc(ones_done, 1)
                for kt in range(KT):
                    pool.wait_ge(h_mod, kt + 1)
                    nc.gpsimd.tensor_copy(h_hi[:, kt, :], work[:, kt, :]).then_inc(h_hi_done, 1)
                pool.wait_ge(table_in, 32)
                with pool.Fori(0, 4) as i:
                    for j in range(4):
                        pool.wait_ge(swapped, i * 4 + (j + 1))
                        nc.gpsimd.tensor_mul(straight[j % 2][:, 0:L], straight[j % 2][:, 0:L],
                                             cos[:]).then_inc(cos_done, 1)

            @block.scalar
            def _(act):
                for kt in range(KT):
                    act.dma_start(work[:, kt, :], io["x_t"][kt]).then_inc(x_in, 16)
                for n in range(DEPTH):
                    act.dma_start(keep.gate[:, n, :], io["mod_b"][n:n + 1, 2 * D:3 * D]
                                  .partition_broadcast(P).rearrange("p a n -> p (a n)")).then_inc(x_in, 16)
                act.wait_ge(vec_in, 16)
                nc.scalar.activation(silu_c[:], vcol[:, 0:2 * KT], ACT.Silu).then_inc(silu_done, 1)
                nc.scalar.activation(note[:, 0:1], vcol[:, 0:1], ACT.Copy).then_inc(proj_evac, 2)
                nc.scalar.activation(note[:, 1:2], vcol[:, 0:1], ACT.Copy).then_inc(out_hi_done, 1)
                for p in range(2):
                    nc.scalar.activation(note[:, 2 + p:3 + p], vcol[:, 0:1], ACT.Copy).then_inc(qk_out[p], 32)
                    nc.scalar.activation(note[:, 8 + p:9 + p], vcol[:, 0:1], ACT.Copy).then_inc(z_out[p], 16)

                def split_piece(g, slot, wslot, loads):
                    act.wait_ge(stage_in[slot], loads * 16)
                    nc.scalar.activation(w_hi[:, wslot, :], stage[:, slot, :], ACT.Copy).then_inc(w_hi_done, 1)

                split_piece(0, 0, 0, 1)
                split_piece(1, 1, 1, 1)
                act.wait_ge(x_in, 16 * (KT + DEPTH))
                act.wait_ge(mod_ready, 4)
                for kt in range(KT):
                    nc.scalar.activation(work[:, kt, 0:L], work[:, kt, 0:L], ACT.Identity,
                                         bias=mod0[:, 0, 0, kt:kt + 1], scale=mod0[:, 1, 0, kt:kt + 1])
                    nc.scalar.activation(work[:, kt, L:LT], work[:, kt, L:LT], ACT.Identity,
                                         bias=mod0[:, 0, 1, kt:kt + 1],
                                         scale=mod0[:, 1, 1, kt:kt + 1]).then_inc(h_mod, 1)
                split_piece(2, 0, 2, 2)
                act.wait_ge(h_lo_done, KT)
                for kind in range(2):
                    with act.Fori(0, 2) as i:
                        for j in range(4):
                            u = i * 4 + (HEADS * kind + j)
                            p = j % 2
                            act.wait_ge(proj_ready, u + 1)
                            act.wait_ge(rope_done, u + 1)
                            if kind == 1:
                                act.wait_ge(out_lo_done, u + 1)
                                nc.scalar.activation(turned[:, L:LT], ps[:, 3 * p + 2, 0:LC], ACT.Copy)
                            nc.scalar.activation(straight[p][:, 0:L].rearrange("p (b n) -> p b n", b=2),
                                                 ps[:, 3 * p:3 * p + 2, :], ACT.Copy,
                                                 scale=DK ** -0.5 if kind == 0 else 1.0).then_inc(proj_evac, 1)
                            act.wait_ge(rope_done, u + 3)
                            act.wait_ge(qk_out[p], i * 64 + 32 * (4 * kind + j // 2 + 1))
                            width = L if kind == 0 else LT
                            nc.scalar.activation(out_hi[p][:, 0:width].bitcast(F32R), turned[:, 0:width],
                                                 ACT.Copy).then_inc(out_hi_done, 1)
                            act.wait_ge(proj_ready, u + 1)
                            split_piece(u + 3, (j + 3) % 2, (j + 3) % 4, i * 2 + (4 * kind + (j + 3) // 2 + 1))
                act.wait_ge(rope_done, 2 + UQK)
                with act.Fori(0, 2) as i:
                    for j in range(4):
                        u = i * 4 + (UQK + j)
                        p = j % 2
                        act.wait_ge(proj_ready, u + 1)
                        act.wait_ge(z_out[p], i * 32 + 16 * (j // 2 + 1))
                        nc.scalar.activation(straight[p][:, 0:L].rearrange("p (b n) -> p b n", b=2),
                                             ps[:, 3 * p:3 * p + 2, :], ACT.Silu).then_inc(proj_evac, 1)
                        split_piece(u + 3, (j + 3) % 2, (j + 3) % 4, i * 2 + (8 + (j + 3) // 2 + 1))
                act.wait_ge(proj_ready, UNITS)
                split_piece(27, 1, 3, 14)
                for p in range(2):
                    act.wait_ge(qk_out[p], 32 + 32 * UQK // 2)
                for vc in range(2):
                    for tt in range(KEYT):
                        n = KEYT * vc + tt
                        act.wait_ge(proj_ready, UNITS + n + 1)
                        if n >= 2:
                            act.wait_ge(v_out[n % 2], 32 * (n // 2))
                        nc.scalar.activation(out_hi[n % 2][:, 0:BANK].bitcast(F32R), ps[:, 3 * (n % 2), :],
                                             ACT.Copy).then_inc(v_hi_done, 1)
                    if vc == 0:
                        for g in range(28, 32):
                            split_piece(g, g % 2, g % 4, g // 2 + 1)

            @block.vector
            def _(dve):
                nc.vector.memset(note[:, 7:8], 0.0).then_inc(rope_done, 2)
                nc.vector.memset(note[:, 6:7], 0.0).then_inc(v_lo_done, 2)
                nc.vector.memset(low_note[:], 0.0).then_inc(out_lo_done, 1)
                dve.wait_ge(silu_done, 1)
                for q in range(2):
                    if q:
                        dve.wait_ge(mod_sums, 1)
                    for a in range(2):
                        nc.vector.memset(acc[:, a, :], 0.0).then_inc(mod_acc, 1)
                    with dve.Fori(0, KT // 2) as i:
                        for b in range(2):
                            dve.wait_ge(mod_in[b], i * 16 + 16 * (4 * q + 1))
                            for a in range(2):
                                dve.wait_ge(mod_acc, i * 4 + (18 * q + 2 + 2 * b + a - 1))
                                nc.vector.scalar_tensor_tensor(
                                    out=acc[:, a, :], in0=mod_tile[:, b, :],
                                    scalar=silu_c[:, ds(i * 2 + (a * KT + b), 1)], in1=acc[:, a, :],
                                    op0=ALU.mult, op1=ALU.add).then_inc(mod_acc, 1)
                dve.wait_ge(mod_sums, 2)
                for a in range(2):
                    nc.vector.tensor_tensor(mod0[:, 0, a, :], ps[:, 7, a * KT:(a + 1) * KT],
                                            vcol[:, V_MODB:V_MODB + KT], ALU.add).then_inc(mod_ready, 1)
                    nc.vector.scalar_tensor_tensor(out=mod0[:, 1, a, :], in0=ps[:, 7, (2 + a) * KT:(3 + a) * KT],
                                                   scalar=1.0, in1=vcol[:, V_MODB + KT:V_MODB + 2 * KT],
                                                   op0=ALU.add, op1=ALU.add).then_inc(mod_ready, 1)

                def low_piece(g, slot, wslot):
                    dve.wait_ge(w_hi_done, g + 1)
                    nc.vector.tensor_sub(w_lo[:, wslot, :], stage[:, slot, :],
                                         w_hi[:, wslot, :].bitcast(F32)).then_inc(w_lo_done, 1)

                low_piece(0, 0, 0)
                low_piece(1, 1, 1)
                for kt in range(KT):
                    dve.wait_ge(h_hi_done, kt + 1)
                    nc.vector.tensor_sub(h_lo[:, kt, :], work[:, kt, :],
                                         h_hi[:, kt, :].bitcast(F32)).then_inc(h_lo_done, 1)
                low_piece(2, 0, 2)
                dve.wait_ge(table_in, 32)
                for kind in range(2):
                    width = L if kind == 0 else LT
                    with dve.Fori(0, 2) as i:
                        for j in range(4):
                            u = i * 4 + (HEADS * kind + j)
                            p = j % 2
                            dve.wait_ge(proj_evac, u + 3)
                            dve.wait_ge(out_hi_done, u + 1)
                            dve.wait_ge(out_lo_done, u + 1)
                            nc.vector.memset(note[:, 5:6], 0.0)
                            nc.vector.stream_shuffle(turned[:, 0:L], straight[p][:, 0:L],
                                                     MASK_HALF_SWAP).then_inc(swapped, 1)
                            dve.wait_ge(swapped, u + 1)
                            nc.vector.tensor_mul(turned[:, 0:L], turned[:, 0:L], sin[:]).then_inc(sin_done, 1)
                            dve.wait_ge(sin_done, u + 1)
                            dve.wait_ge(cos_done, u + 1)
                            nc.vector.tensor_add(turned[:, 0:L], turned[:, 0:L],
                                                 straight[p][:, 0:L]).then_inc(rope_done, 1)
                            dve.wait_ge(out_hi_done, u + 2)
                            dve.wait_ge(rope_done, u + 3)
                            nc.vector.tensor_sub(out_lo[p][:, 0:width].bitcast(F32R), turned[:, 0:width],
                                                 out_hi[p][:, 0:width]).then_inc(out_lo_done, 1)
                            low_piece(u + 3, (j + 3) % 2, (j + 3) % 4)
                with dve.Fori(0, 2) as i:
                    for j in range(4):
                        u = i * 4 + (UQK + j)
                        low_piece(u + 3, (j + 3) % 2, (j + 3) % 4)
                        half = j // 2
                        for b in range(4):
                            step = 4 * j + b
                            pos = step + half
                            if step % 8 == 0:
                                dve.wait_ge(mod_sums, i * 2 + 2)
                                nc.vector.memset(acc[:, half, :], 0.0).then_inc(mod_acc, 1)
                            dve.wait_ge(mod_in[b % 2], i * 128 + 16 * (8 + 2 * j + b // 2 + 1))
                            dve.wait_ge(mod_acc, i * 18 + (MOD0 + pos + 1))
                            t = 4 * (j % 2) + b
                            nc.vector.scalar_tensor_tensor(
                                out=acc[:, half, :], in0=mod_tile[:, b % 2, :], scalar=silu_c[:, t:t + 1],
                                in1=acc[:, half, :], op0=ALU.mult, op1=ALU.add).then_inc(mod_acc, 1)
                    dve.wait_ge(mod_sums, i * 2 + 3)
                    g = keep.gate[:, ds(i, 1), :].rearrange("p a (b n) -> p (a b) n", b=2)
                    nc.vector.tensor_tensor(g, ps[:, 6:8, :], g, ALU.add).then_inc(gate_done, 1)
                    dve.wait_ge(mod_sums, i * 2 + 4)
                    nc.vector.tensor_tensor(keep.mod1[:, ds(i, 1), :].rearrange("p a n -> p (a n)"), ps[:, 7, 0:KT],
                                            vcol[:, ds(i * KT + (V_MODB + 3 * KT), KT)],
                                            ALU.add).then_inc(gate_done, 1)
                low_piece(27, 1, 3)
                dve.wait_ge(gate_done, 4)
                nc.vector.tensor_scalar_add(keep.mod1[:, 1, :], keep.mod1[:, 1, :], 1.0)
                for vc in range(2):
                    for tt in range(KEYT):
                        n = KEYT * vc + tt
                        dve.wait_ge(v_hi_done, n + 1)
                        nc.vector.tensor_sub(out_lo[n % 2][:, 0:BANK].bitcast(F32R), ps[:, 3 * (n % 2), :],
                                             out_hi[n % 2][:, 0:BANK]).then_inc(v_lo_done, 1)
                    if vc == 0:
                        for g in range(28, 32):
                            low_piece(g, g % 2, g % 4)

            @block.tensor
            def _(pe):
                pe.wait_ge(ones_done, 1)
                for q in range(2):
                    pe.wait_ge(mod_acc, 18 * (q + 1))
                    for a in range(2):
                        for j in range(KT):
                            c = (2 * q + a) * KT + j
                            last = nc.tensor.matmul(ps[:, 7, c:c + 1], acc[:, a, j * P:(j + 1) * P],
                                                    keep.ones[:, 0:1], start=True, stop=True)
                    last.then_inc(mod_sums, 1)

                def unit(u, j, context):
                    pe.wait_ge(w_lo_done, u + 1)
                    pe.wait_ge(proj_evac, u + 1)
                    p = j % 2
                    outs = [(3 * p + n, n * BANK, BANK) for n in range(HALVES)]
                    if context:
                        outs.append((3 * p + 2, L, LC))
                    for kt in range(KT):
                        for w, parts in ((w_hi, (h_hi, h_lo)), (w_lo, (h_hi,))):
                            for h in parts:
                                for bank, at, n in outs:
                                    last = nc.tensor.matmul(
                                        ps[:, bank, 0:n], w[:, j, kt * P:(kt + 1) * P], h[:, kt, at:at + n],
                                        start=(kt == 0 and w is w_hi and h is h_hi),
                                        stop=(kt == KT - 1 and w is w_lo))
                    last.then_inc(proj_ready, 1)

                pe.wait_ge(h_lo_done, KT)
                for kind in range(2):
                    with pe.Fori(0, 2) as i:
                        for j in range(4):
                            unit(i * 4 + (HEADS * kind + j), j, kind == 1)
                with pe.Fori(0, 2) as i:
                    for j in range(4):
                        unit(i * 4 + (UQK + j), j, False)
                        if j == 2:
                            pe.wait_ge(mod_acc, i * 18 + (MOD0 + 9))
                            for n in range(2):
                                last = nc.tensor.matmul(ps[:, 6 + n, :], keep.ones[:],
                                                        acc[:, 0, n * BANK:(n + 1) * BANK], start=True, stop=True)
                            last.then_inc(mod_sums, 1)
                    pe.wait_ge(mod_acc, i * 18 + (MOD0 + 18))
                    pe.wait_ge(gate_done, i * 2 + 1)
                    for n in range(KT):
                        last = nc.tensor.matmul(ps[:, 7, n:n + 1], acc[:, 1, n * P:(n + 1) * P],
                                                keep.ones[:, 0:1], start=True, stop=True)
                    last.then_inc(mod_sums, 1)
                with pe.Fori(0, 2) as vc:
                    for tt in range(KEYT):
                        if tt < 2:
                            pe.wait_ge(proj_evac, UNITS + 2)
                        pe.wait_ge(v_lo_done, vc * KEYT + (tt + 1))
                        for kt in range(KT):
                            if tt == 0 and kt % 2 == 0:
                                pe.wait_ge(w_lo_done, vc * 4 + (UNITS + kt // 2 + 1))
                            for h, parts in ((h_hi, (w_hi, w_lo)), (h_lo, (w_hi,))):
                                for w in parts:
                                    last = nc.tensor.matmul(
                                        ps[:, 3 * (tt % 2), :], h[:, kt, tt * P:(tt + 1) * P],
                                        w[:, kt // 2, (kt % 2) * BANK:(kt % 2 + 1) * BANK],
                                        start=(kt == 0 and h is h_hi and w is w_hi),
                                        stop=(kt == KT - 1 and h is h_lo))
                        last.then_inc(proj_ready, 1)


def attend(nc, io, keep):
    ROUNDS = [(0, 4), (4, 4), (8, 2)]
    BANK_T = [5, 6]
    BANK_SIDE, BANK_PV = 6, 7
    RMS_SHRINK = 2.0 ** -30
    GROUP = 4
    REST = LT - 2 * BANK
    PV_KEYS = [(0, 1), (2, 3, 4), (5, 6), (7, 8, 9)]
    with ExitStack() as stack:
        m = Memory(nc, stack, "at")
        q_a = m.sb("q_a", [P, 2, 2, L], F32R)
        q_b = m.sb("q_b", [P, 2, 2, L], F32R)
        k_s = m.sb("k_s", [P, 2, 2, LT], F32R)
        v_hi = m.sb("v_hi", [P, 2, KEYT, DV], F32R)
        v_lo = m.sb("v_lo", [P, 2, KEYT, DV], F32R)
        z_s = m.sb("z_s", [P, 2, BANK])
        prob0 = m.sb("prob0", [P, 4, LT])
        prob1 = m.sb("prob1", [P, 2, LT])
        a_hi = m.sb("a_hi", [P, 2, KEYT, GROUP * P], F32R)
        a_lo = m.sb("a_lo", [P, 2, KEYT, GROUP * P], F32R)
        square = m.sb("square", [P, BANK])
        gated = m.sb("gated", [P, BANK])
        normed = m.sb("normed", [P, BANK])
        o_hi = m.sb("o_hi", [P, BANK])
        rms = m.sb("rms", [P, GROUP])
        eps_sq = m.sb("eps_sq", [P, GROUP])
        sum0 = m.sb("sum0", [P, 4, GROUP])
        peak = m.sb("peak", [P, 2, 4])
        stat = m.sb("stat", [P, 2, 8])
        lam_in = m.sb("lam_in", [P, 4, DK])
        lam = m.sb("lam", [P, 6])
        note = m.sb("note", [P, 10])
        hold_out = m.sb("hold_out", [P, 1])
        mean_w = m.sb("mean_w", [P, 4])
        ps = m.psum("ps", [P, 8, BANK])

        lam_loaded, lam_step, lam_exp, lam_ready = (m.sem(n) for n in ("lam_loaded", "lam_step", "lam_exp", "lam_ready"))
        head_in = [m.sem("head_in0"), m.sem("head_in1")]
        v_in = [m.sem("v_in0"), m.sem("v_in1")]
        z_in = [m.sem("z_in0"), m.sem("z_in1")]
        s_ready = m.sem("s_ready")
        peak_done = m.sem("peak_done")
        max_done = [m.sem("max_done0"), m.sem("max_done1")]
        exp_done = [m.sem("exp_done0"), m.sem("exp_done1")]
        neg_done, scaled, diff_done = (m.sem(n) for n in ("neg_done", "scaled", "diff_done"))
        t_ready, t_hi_done, t_lo_done = m.sem("t_ready"), m.sem("t_hi_done"), m.sem("t_lo_done")
        pv_ready, sq_done, gated_done, mean_ready = (m.sem(n) for n in ("pv_ready", "sq_done", "gated_done", "mean_ready"))
        eps_done, var_done, rms_done, inv_rms_done, diag_done, spread_ready = (m.sem(n) for n in (
            "eps_done", "var_done", "rms_done", "inv_rms_done", "diag_done", "spread_ready"))
        normed_done, o_hi_done, o_lo_done, og_out = (m.sem(n) for n in ("normed_done", "o_hi_done", "o_lo_done", "og_out"))

        GROUPS = HEADS * QT // GROUP
        TILES = HEADS * QT
        IN_HEAD = 16 * 12
        IN_V = 16 * 2

        def run(eng, group):
            group(0, 0)
            group(1, 1)
            with eng.Fori(0, 3) as i:
                for b in range(4):
                    group(i * 4 + (b + 2), (b + 2) % 4)
            for g in range(14, GROUPS):
                group(g, g % 4)

        def softmaxed(g, c):
            return not (isinstance(g, int) and g * GROUP + c + 2 >= TILES)

        def early(g, n):
            return isinstance(g, int) and g < n

        with nc.Block() as block:
            @block.sync
            def _(sp):
                sp.dma_start(lam_in[:], io["lam"].partition_broadcast(P).rearrange("p a b n -> p (a b) n")
                             ).then_inc(lam_loaded, 16)

                def load_head(h, slot):
                    row = h * (2 * P)
                    for mp in range(2):
                        for part in range(2):
                            top = slice(part * DK, (part + 1) * DK)
                            other = slice((1 - part) * DK, (2 - part) * DK)
                            src = io["q_hl"][ds(row + (part * P + mp * DK), DK), :]
                            sp.dma_start(q_a[top, slot, mp, :].bitcast(F32), src).then_inc(head_in[slot], 16)
                            sp.dma_start(q_b[other, slot, mp, :].bitcast(F32), src).then_inc(head_in[slot], 16)
                            src = io["k_hl"][ds(row + (part * P + mp * DK), DK), :]
                            sp.dma_start(k_s[top, slot, mp, :].bitcast(F32), src).then_inc(head_in[slot], 16)

                def load_v(h, slot):
                    for part, v in ((0, v_hi), (1, v_lo)):
                        src = io["v_hl"][part].rearrange("t p n -> p t n")[:, :, ds(h * DV, DV)]
                        sp.dma_start(v[:, slot, :, :].bitcast(F32), src).then_inc(v_in[slot], 16)

                def load_z(row, half):
                    sp.dma_start(z_s[:, half, :], io["z_s"][ds(row, P), half * BANK:(half + 1) * BANK]
                                 ).then_inc(z_in[half], 16)

                def store(row, half, n):
                    sp.wait_ge(o_lo_done, n + 1)
                    for part, buf in ((0, o_hi), (1, normed)):
                        sp.dma_start(io["og_hl"][ds(row + part * D, P), half * BANK:(half + 1) * BANK],
                                     buf[:]).then_inc(og_out, 16)

                def group(g, n, head):
                    half = (g if isinstance(g, int) else g_mod[0]) % 2
                    heads_left = half == 0 and not (isinstance(g, int) and g == GROUPS - 2)
                    if heads_left:
                        sp.wait_ge(s_ready, (n + 2) * (3 * GROUP))
                        load_head(head + 2, 1 - g_mod[0] // 2)
                    sp.wait_ge(gated_done, n + 2)
                    load_z((head + 1) * P, half)
                    store(head * P, half, n)
                    if heads_left:
                        sp.wait_ge(pv_ready, n + 2)
                        load_v(head + 2, 1 - g_mod[0] // 2)

                g_mod = [None]
                load_head(0, 0)
                load_v(0, 0)
                load_z(0, 0)
                load_z(0, 1)
                load_head(1, 1)
                load_v(1, 1)
                with sp.Fori(0, 3) as i:
                    for b in range(4):
                        g_mod[0] = (b + 2) % 4
                        group(None, i * 4 + b, i * 2 + b // 2)
                for g in (14, 15):
                    group(g, g - 2, (g - 2) // 2)
                for n in (14, 15):
                    store(n // 2 * P, n % 2, n)
                sp.wait_ge(og_out, 32 + 32 * GROUPS)
                for half in range(2):
                    sp.wait_ge(z_in[half], 16 * HEADS)

            @block.tensor
            def _(pe):
                def products(nt, outs):
                    slot, tile = nt // QT, nt % QT
                    for bank, at, w, mp, key in outs:
                        for first, q in ((True, q_a), (False, q_b)):
                            last = nc.tensor.matmul(ps[:, bank, at:at + w], q[:, slot, mp, tile * P:(tile + 1) * P],
                                                    k_s[:, slot, mp, key:key + w], start=first, stop=not first)
                    last.then_inc(s_ready, 1)

                def scores_first(t, nt):
                    pe.wait_ge(exp_done[0], t + 1)
                    products(nt, [(0, 0, BANK, 0, 0), (1, 0, BANK, 0, BANK)])

                def scores_rest(t, nt):
                    pe.wait_ge(exp_done[1], t + 1)
                    products(nt, [(2, 0, REST, 0, 2 * BANK), (2, REST, REST, 1, 0)])
                    products(nt, [(3, 0, BANK, 1, REST), (4, 0, BANK, 1, REST + BANK)])

                def product_v(gm, keys):
                    slot, half = (gm - 1) % 4 // 2, (gm - 1) % 2
                    for k in keys:
                        for v, a in ((v_hi, a_hi), (v_hi, a_lo), (v_lo, a_hi)):
                            last = nc.tensor.matmul(ps[:, BANK_PV, :], v[:, slot, k, :], a[:, half, k, :],
                                                    start=(k == 0 and v is v_hi and a is a_hi),
                                                    stop=(k == KEYT - 1 and v is v_lo))
                        if k == KEYT - 1:
                            last.then_inc(pv_ready, 1)

                def mean(n):
                    pe.wait_ge(sq_done, n + 1)
                    for j in range(GROUP):
                        last = nc.tensor.matmul(ps[:, BANK_SIDE, j:j + 1], square[:, j * P:(j + 1) * P],
                                                mean_w[:, 0:1], start=True, stop=True)
                    last.then_inc(mean_ready, 1)

                def spread(n):
                    pe.wait_ge(diag_done, n + 1)
                    nc.tensor.matmul(ps[:, BANK_SIDE, :], keep.ones[:], square[:],
                                     start=True, stop=True).then_inc(spread_ready, 1)

                def group(g, gm):
                    for c in range(GROUP):
                        t = g * GROUP + c
                        pe.wait_ge(diff_done, t + 1)
                        transposes(g, c, 0)
                        transposes(g, c, 1)
                        if softmaxed(g, c):
                            scores_rest(t + 2, (gm * GROUP + c + 2) % (2 * QT))
                        transposes(g, c, 2)
                        if not early(g, 1):
                            if c == 0:
                                pe.wait_ge(gated_done, g)
                                if gm % 2 == 1:
                                    pe.wait_ge(v_in[gm // 2], v_loads(g))
                            product_v(gm, PV_KEYS[c])
                        if c == 0 and not early(g, 2):
                            pe.wait_ge(t_lo_done, g * 12 + 2)
                            mean(g - 2)
                        if c == 2 and not early(g, 2):
                            pe.wait_ge(t_lo_done, g * 12 + 8)
                            spread(g - 2)
                        if not (isinstance(g, int) and t + 3 >= TILES):
                            nt = (gm * GROUP + c + 3) % (2 * QT)
                            if nt % QT == 0:
                                pe.wait_ge(head_in[nt // QT], head_loads(g))
                            scores_first(t + 3, nt)

                def transposes(g, c, r):
                    at, n = ROUNDS[r]
                    if r < 2 and not (early(g, 1) and c == 0):
                        pe.wait_ge(t_lo_done, g * 12 + (3 * c + r - 1))
                    if r == 2:
                        pe.wait_ge(t_lo_done, g * 12 + (3 * c + 1))
                    if r == 0 and c == 1 and not early(g, 2):
                        pe.wait_ge(var_done, g - 1)
                    if r == 0 and c == 3 and not early(g, 2):
                        pe.wait_ge(normed_done, g)
                    for k in range(n):
                        last = nc.tensor.transpose(ps[:, BANK_T[(c + r) % 2], k * P:(k + 1) * P],
                                                   prob0[:, c, (at + k) * P:(at + k + 1) * P], keep.ident[:])
                    last.then_inc(t_ready, 1)

                def head_loads(g):
                    return IN_HEAD * ((g + 1) // 2 // 2 + 1) if isinstance(g, int) else head_count[0]

                def v_loads(g):
                    return IN_V * ((g - 1) // 4 + 1) if isinstance(g, int) else v_count[0]

                head_count, v_count = [None], [None]
                pe.wait_ge(head_in[0], IN_HEAD)
                pe.wait_ge(lam_step, 1)
                for t in range(2):
                    scores_first(t, t)
                    scores_rest(t, t)
                scores_first(2, 2)
                group(0, 0)
                group(1, 1)
                with pe.Fori(0, 3) as i:
                    head_count[0] = i * IN_HEAD + 2 * IN_HEAD
                    for b in range(4):
                        v_count[0] = i * IN_V + IN_V * (1 if b == 1 else 2)
                        group(i * 4 + (b + 2), (b + 2) % 4)
                for g in range(14, GROUPS):
                    group(g, g % 4)
                pe.wait_ge(gated_done, GROUPS)
                product_v(0, range(KEYT))
                pe.wait_ge(t_lo_done, 12 * GROUPS)
                mean(GROUPS - 2)
                pe.wait_ge(var_done, GROUPS - 1)
                spread(GROUPS - 2)
                pe.wait_ge(normed_done, GROUPS)
                mean(GROUPS - 1)
                pe.wait_ge(var_done, GROUPS)
                spread(GROUPS - 1)

            @block.gpsimd
            def _(pool):
                nc.gpsimd.memset(mean_w[:], 1.0 / DV).then_inc(lam_step, 1)

                def hold():
                    nc.gpsimd.tensor_add(hold_out[:], mean_w[:, 0:1], mean_w[:, 1:2])

                pool.wait_ge(lam_step, 1)

                def difference(t, p, p4):
                    pool.wait_ge(neg_done, t * 2 + 2)
                    hold()
                    nc.gpsimd.tensor_scalar(prob1[:, p, :], prob1[:, p, :], stat[:, p, 4:5], 1.0,
                                            ALU.mult, ALU.mult).then_inc(scaled, 1)
                    pool.wait_ge(scaled, t + 1)
                    nc.gpsimd.tensor_add(prob0[:, p4, :], prob0[:, p4, :], prob1[:, p, :]).then_inc(diff_done, 1)

                def diagonals(n):
                    pool.wait_ge(inv_rms_done, n + 1)
                    nc.gpsimd.tensor_tensor(square[:].rearrange("p (j q) -> p j q", j=GROUP),
                                            keep.ident[:].unsqueeze(1).broadcast_to([P, GROUP, P]),
                                            rms[:].unsqueeze(2).broadcast_to([P, GROUP, P]),
                                            ALU.mult).then_inc(diag_done, 1)

                def low_part(n):
                    pool.wait_ge(o_hi_done, n + 1)
                    nc.gpsimd.tensor_sub(normed[:].bitcast(F32R), normed[:], o_hi[:]).then_inc(o_lo_done, 1)

                difference(0, 0, 0)

                def group(g, gm):
                    for c in range(GROUP):
                        t = g * GROUP + c
                        if not (isinstance(g, int) and t + 1 >= TILES):
                            difference(t + 1, (c + 1) % 2, (c + 1) % 4)
                        if c == 1 and not early(g, 2):
                            diagonals(g - 2)
                        if c == 3 and not early(g, 2):
                            low_part(g - 2)

                run(pool, group)
                for n in (GROUPS - 2, GROUPS - 1):
                    diagonals(n)
                    low_part(n)

            @block.scalar
            def _(act):
                for n, s in enumerate((exp_done[0], exp_done[1])):
                    nc.scalar.activation(note[:, n:n + 1], keep.eps[:], ACT.Copy).then_inc(s, 1)
                nc.scalar.activation(note[:, 4:5], keep.eps[:], ACT.Copy).then_inc(og_out, 32)
                act.wait_ge(lam_step, 5)
                nc.scalar.activation(lam[:, 2:4], lam[:, 0:2], ACT.Exp).then_inc(lam_exp, 1)
                scores = ps[:, 0:5, :].rearrange("p b n -> p (b n)")

                def exponential0(t, p, t16, reused):
                    act.wait_ge(max_done[0], t + 1)
                    if reused is not None:
                        act.wait_ge(t_ready, reused)
                    nc.scalar.activation(prob0[:, t16 % 4, :], scores[:, 0:LT], ACT.Exp, bias=stat[:, p, 0:1],
                                         accum_out=sum0[:, t16 // 4, t16 % 4:t16 % 4 + 1]).then_inc(exp_done[0], 1)

                def exponential1(t, p):
                    act.wait_ge(max_done[1], t + 1)
                    if not (isinstance(t, int) and t < 2):
                        act.wait_ge(diff_done, t - 1)
                    nc.scalar.activation(prob1[:, p, :], scores[:, LT:2 * LT], ACT.Exp, bias=stat[:, p, 1:2],
                                         accum_out=stat[:, p, 2:3]).then_inc(exp_done[1], 1)

                def high(g, gm, c, r):
                    at, n = ROUNDS[r]
                    act.wait_ge(t_ready, g * 12 + (3 * c + r + 1))
                    nc.scalar.activation(a_hi[:, gm % 2, at:at + n, c * P:(c + 1) * P],
                                         ps[:, BANK_T[(c + r) % 2], 0:n * P].rearrange("p (k q) -> p k q", k=n),
                                         ACT.Copy).then_inc(t_hi_done, 1)

                def squares(n):
                    act.wait_ge(pv_ready, n + 1)
                    act.wait_ge(normed_done, n + 1)
                    nc.scalar.activation(square[:], ps[:, BANK_PV, :], ACT.Square).then_inc(sq_done, 1)

                def root(n):
                    act.wait_ge(var_done, n + 1)
                    nc.scalar.activation(rms[:], rms[:], ACT.Sqrt).then_inc(rms_done, 1)
                    nc.scalar.activation(note[:, 5:6], keep.eps[:], ACT.Exp)

                def high_part(n):
                    act.wait_ge(normed_done, n + 2)
                    act.wait_ge(og_out, n * 32 + 32)
                    nc.scalar.activation(o_hi[:].bitcast(F32R), normed[:], ACT.Copy).then_inc(o_hi_done, 1)

                for t in range(2):
                    exponential0(t, t, t, None)
                    exponential1(t, t)

                def group(g, gm):
                    for c in range(GROUP):
                        t = g * GROUP + c
                        if c == 0 and not early(g, 2):
                            squares(g - 2)
                        high(g, gm, c, 0)
                        high(g, gm, c, 1)
                        if c == 1 and not early(g, 2):
                            root(g - 2)
                        if softmaxed(g, c):
                            reused = None if early(g, 1) and c < 2 else g * 12 + 3 * (c - 1)
                            exponential0(t + 2, c % 2, (gm * GROUP + c + 2) % 16, reused)
                        high(g, gm, c, 2)
                        if softmaxed(g, c):
                            exponential1(t + 2, c % 2)
                        if c == 2 and not early(g, 2):
                            high_part(g - 2)

                run(act, group)
                for n in (GROUPS - 2, GROUPS - 1):
                    squares(n)
                    root(n)
                    high_part(n)

            @block.vector
            def _(dve):
                dve.wait_ge(lam_loaded, 16)
                dve.wait_ge(lam_step, 1)
                for n in range(2):
                    nc.vector.tensor_mul(lam_in[:, 2 * n, :], lam_in[:, 2 * n, :],
                                         lam_in[:, 2 * n + 1, :]).then_inc(lam_step, 1)
                dve.wait_ge(lam_step, 3)
                for n in range(2):
                    nc.vector.tensor_reduce(lam[:, n:n + 1], lam_in[:, 2 * n, :], AX.X, ALU.add).then_inc(lam_step, 1)
                dve.wait_ge(lam_exp, 1)
                nc.vector.tensor_sub(lam[:, 4:5], lam[:, 3:4], lam[:, 2:3]).then_inc(lam_ready, 1)
                dve.wait_ge(lam_ready, 1)
                nc.vector.tensor_scalar_add(lam[:, 5:6], lam[:, 4:5], -LAMBDA_INIT).then_inc(lam_ready, 1)
                dve.wait_ge(lam_ready, 2)

                def peak_of(t, p, n):
                    dve.wait_ge(s_ready, t * 3 + (n + 1))
                    view, out = ((ps[:, 0:2, :].rearrange("p b n -> p (b n)"), peak[:, p, 0:1]),
                                 (ps[:, 2, :].rearrange("p (a n) -> p a n", a=2), peak[:, p, 2:4]),
                                 (ps[:, 3:5, :].rearrange("p b n -> p (b n)"), peak[:, p, 1:2]))[n]
                    nc.vector.tensor_reduce(out, view, AX.X, ALU.max, negate=True).then_inc(peak_done, 1)

                def maximum(t, p, mp):
                    peak_of(t, p, 1 + mp)
                    dve.wait_ge(peak_done, t * 3 + (mp + 2))
                    nc.vector.tensor_tensor(stat[:, p, mp:mp + 1], peak[:, p, mp:mp + 1],
                                            peak[:, p, 2 + mp:3 + mp], ALU.min).then_inc(max_done[mp], 1)

                def weight(t, p, t16):
                    dve.wait_ge(exp_done[1], t + 2)
                    nc.vector.reciprocal(stat[:, p, 3:4], stat[:, p, 2:3]).then_inc(neg_done, 1)
                    dve.wait_ge(neg_done, t * 2 + 1)
                    nc.vector.scalar_tensor_tensor(out=stat[:, p, 4:5], in0=stat[:, p, 3:4], scalar=lam[:, 5:6],
                                                   in1=sum0[:, t16 // 4, t16 % 4:t16 % 4 + 1], op0=ALU.mult,
                                                   op1=ALU.mult).then_inc(neg_done, 1)

                def low(g, gm, c, r):
                    at, n = ROUNDS[r]
                    dve.wait_ge(t_hi_done, g * 12 + (3 * c + r + 1))
                    nc.vector.tensor_sub(a_lo[:, gm % 2, at:at + n, c * P:(c + 1) * P],
                                         ps[:, BANK_T[(c + r) % 2], 0:n * P].rearrange("p (k q) -> p k q", k=n),
                                         a_hi[:, gm % 2, at:at + n, c * P:(c + 1) * P].bitcast(F32)
                                         ).then_inc(t_lo_done, 1)

                def gate(n, half, loads):
                    dve.wait_ge(sq_done, n + 1)
                    dve.wait_ge(z_in[half], loads)
                    dve.wait_ge(normed_done, n + 1)
                    nc.vector.scalar_tensor_tensor(out=gated[:], in0=ps[:, BANK_PV, :], scalar=keep.subln[:],
                                                   in1=z_s[:, half, :], op0=ALU.mult,
                                                   op1=ALU.mult).then_inc(gated_done, 1)

                def eps_squares(n, gm):
                    nc.vector.scalar_tensor_tensor(out=eps_sq[:], in0=sum0[:, gm, :], scalar=EPS * RMS_SHRINK,
                                                   in1=sum0[:, gm, :], op0=ALU.mult, op1=ALU.mult).then_inc(eps_done, 1)

                def mean_squares(n):
                    dve.wait_ge(mean_ready, n + 1)
                    dve.wait_ge(eps_done, n + 1)
                    nc.vector.scalar_tensor_tensor(out=rms[:], in0=ps[:, BANK_SIDE, 0:GROUP], scalar=RMS_SHRINK,
                                                   in1=eps_sq[:], op0=ALU.mult, op1=ALU.add).then_inc(var_done, 1)

                def inverse_rms(n):
                    dve.wait_ge(rms_done, n + 1)
                    nc.vector.reciprocal(rms[:], rms[:]).then_inc(inv_rms_done, 1)

                def norm(n):
                    dve.wait_ge(spread_ready, n + 1)
                    dve.wait_ge(gated_done, n + 2)
                    dve.wait_ge(og_out, n * 32 + 32)
                    nc.vector.tensor_tensor(normed[:], gated[:], ps[:, BANK_SIDE, :],
                                            ALU.mult).then_inc(normed_done, 1)

                nc.vector.tensor_scalar_mul(keep.subln[:], keep.vcol[:, V_SUBG:V_SUBG + 1],
                                            (1.0 - LAMBDA_INIT) * RMS_SHRINK ** 0.5).then_inc(lam_ready, 1)
                nc.vector.memset(note[:, 6:7], 0.0).then_inc(gated_done, 1)
                nc.vector.memset(note[:, 7:8], 0.0).then_inc(normed_done, 1)
                dve.wait_ge(lam_ready, 3)
                peak_of(0, 0, 0)
                maximum(0, 0, 0)
                maximum(0, 0, 1)
                weight(0, 0, 0)
                peak_of(1, 1, 0)
                maximum(1, 1, 0)
                maximum(1, 1, 1)
                peak_of(2, 0, 0)

                z_loads = [None]

                def group(g, gm):
                    for c in range(GROUP):
                        t = g * GROUP + c
                        if not (isinstance(g, int) and t + 1 >= TILES):
                            weight(t + 1, (c + 1) % 2, (gm * GROUP + c + 1) % 16)
                        low(g, gm, c, 0)
                        if c == 0 and not early(g, 2):
                            gate(g - 2, gm % 2, 16 * ((g - 2) // 2 + 1) if isinstance(g, int) else z_loads[0][gm])
                        if softmaxed(g, c):
                            maximum(t + 2, c % 2, 0)
                            maximum(t + 2, c % 2, 1)
                        low(g, gm, c, 1)
                        low(g, gm, c, 2)
                        if c == 0 and not early(g, 2):
                            eps_squares(g - 2, (gm - 2) % 4)
                            mean_squares(g - 2)
                        if c == 2 and not early(g, 2):
                            norm(g - 2)
                        if not (isinstance(g, int) and t + 3 >= TILES):
                            peak_of(t + 3, (c + 1) % 2, 0)
                        if c == 1 and not early(g, 2):
                            inverse_rms(g - 2)

                group(0, 0)
                group(1, 1)
                with dve.Fori(0, 3) as i:
                    z_loads[0] = {(b + 2) % 4: i * 32 + 16 * (b // 2 + 1) for b in range(4)}
                    for b in range(4):
                        group(i * 4 + (b + 2), (b + 2) % 4)
                for g in range(14, GROUPS):
                    group(g, g % 4)
                for n in (GROUPS - 2, GROUPS - 1):
                    gate(n, n % 2, 16 * (n // 2 + 1))
                    eps_squares(n, n % 4)
                    mean_squares(n)
                    inverse_rms(n)
                    norm(n)


def output(nc, io, keep, layer, src, weights, residual, dst, nxt):
    with ExitStack() as stack:
        m = Memory(nc, stack, f"out{layer}")
        w_hi = m.sb("w_hi", [P, KT, D], F32R)
        w_lo = m.sb("w_lo", [P, KT, D], F32R)
        stage = m.sb("stage", [P, 2, D])
        s_hi = m.sb("s_hi", [P, 2, KT, P], F32R)
        s_lo = m.sb("s_lo", [P, 2, KT, P], F32R)
        res = m.sb("res", [P, 2, D])
        row = m.sb("row", [P, 2, D])
        done = m.sb("done", [P, 2, D])
        hf = m.sb("hf", [P, KT, P])
        ln_g = m.sb("ln_g", [P, D])
        ln_b = m.sb("ln_b", [P, D])
        stats = m.sb("stats", [P, 2, 2, 6])
        mv = m.sb("mv", [P, 2, 2])
        rstd = m.sb("rstd", [P, 2])
        note = m.sb("note", [P, 4])
        hold_out = m.sb("hold_out", [P, 1])
        ps = m.psum("ps", [P, 8, BANK])

        names = ("row_in", "w_hi_done", "w_lo_done", "proj_ready", "prod_done", "sum_done", "stats_done", "mv_done",
                 "std_done", "rstd_done", "norm_done", "weighted", "done_ready", "t_ready", "h_done", "h_hi_done",
                 "h_lo_done")
        (row_in, w_hi_done, w_lo_done, proj_ready, prod_done, sum_done, stats_done, mv_done, std_done, rstd_done,
         norm_done, weighted, done_ready, t_ready, h_done, h_hi_done, h_lo_done) = (m.sem(n) for n in names)
        stage_in = [m.sem("stage_in0"), m.sem("stage_in1")]
        src_in = [m.sem("src_in0"), m.sem("src_in1")]
        res_in = [m.sem("res_in0"), m.sem("res_in1")]
        done_out = [m.sem("done_out0"), m.sem("done_out1")]

        def run(eng, tile):
            tile(0, 0, 0)
            with eng.Fori(0, 3) as i:
                tile(i * 2 + 1, i, 1)
                tile(i * 2 + 2, i + 1, 0)
            tile(QT - 1, 3, 1)

        with nc.Block() as block:
            @block.sync
            def _(sp):
                def load_tile(n, p):
                    cols = ds(n * P, P)
                    for part, buf in ((0, s_hi), (1, s_lo)):
                        view = src[part * D:(part + 1) * D, :].rearrange("(k p) t -> p k t", p=P)
                        sp.dma_start(buf[:, p, :, :].bitcast(F32), view[:, :, cols]).then_inc(src_in[p], 16)
                    sp.dma_start(res[:, p, :], residual[ds(n * P, P), :]).then_inc(res_in[p], 16)

                load_tile(0, 0)
                for kt in range(KT):
                    if kt >= 2:
                        sp.wait_ge(w_lo_done, kt - 1)
                    sp.dma_start(stage[:, kt % 2, :], weights[kt * P:(kt + 1) * P, :]).then_inc(stage_in[kt % 2], 16)
                sp.dma_start(ln_g[:], io["ln_g"][layer:layer + 1, :].partition_broadcast(P)
                             .rearrange("p a n -> p (a n)")).then_inc(row_in, 16)
                sp.dma_start(ln_b[:], io["ln_b"][layer:layer + 1, :].partition_broadcast(P)
                             .rearrange("p a n -> p (a n)")).then_inc(row_in, 16)
                load_tile(1, 1)

                def tile(n, k, p):
                    if not (isinstance(n, int) and n == QT - 1):
                        sp.wait_ge(proj_ready, n + 1)
                        sp.wait_ge(sum_done, n + 1)
                        load_tile(n + 2, p)
                    sp.wait_ge(done_ready, n + 3)
                    sp.dma_start(dst[ds(n * P, P), :], done[:, p, :]).then_inc(done_out[p], 16)

                tile(0, 0, 0)
                with sp.Fori(0, 2) as i:
                    tile(i * 2 + 1, None, 1)
                    tile(i * 2 + 2, None, 0)
                tile(5, None, 1)
                for n in (6, 7):
                    sp.wait_ge(done_ready, n + 3)
                    sp.dma_start(dst[n * P:(n + 1) * P, :], done[:, n % 2, :]).then_inc(done_out[n % 2], 16)
                for p in range(2):
                    sp.wait_ge(done_out[p], 16 + 16 * QT // 2)

            @block.tensor
            def _(pe):
                def product(n, k, p):
                    pe.wait_ge(src_in[p], k * 32 + 32)
                    pe.wait_ge(prod_done, n + 1)
                    for kt in range(KT):
                        if isinstance(n, int) and n == 0:
                            pe.wait_ge(w_lo_done, kt + 1)
                        for s, parts in ((s_hi, (w_hi, w_lo)), (s_lo, (w_hi,))):
                            for w in parts:
                                for half in range(2):
                                    last = nc.tensor.matmul(
                                        ps[:, 2 * p + half, :], s[:, p, kt, :],
                                        w[:, kt, half * BANK:(half + 1) * BANK],
                                        start=(kt == 0 and s is s_hi and w is w_hi),
                                        stop=(kt == KT - 1 and s is s_lo))
                    last.then_inc(proj_ready, 1)

                def transposes(n, p):
                    pe.wait_ge(done_ready, n + 3)
                    pe.wait_ge(h_done, n + 1)
                    for kt in range(KT):
                        last = nc.tensor.transpose(ps[:, 4 + 2 * p + kt // 4, (kt % 4) * P:(kt % 4 + 1) * P],
                                                   done[:, p, kt * P:(kt + 1) * P], keep.ident[:])
                    last.then_inc(t_ready, 1)

                def tile(n, k, p):
                    product(n, k, p)
                    if nxt and not (isinstance(n, int) and n == 0):
                        transposes(n - 1, 1 - p)

                run(pe, tile)
                if nxt:
                    transposes(QT - 1, 1)

            @block.scalar
            def _(act):
                nc.scalar.activation(note[:, 0:1], keep.eps[:], ACT.Copy).then_inc(h_done, 2)
                nc.scalar.activation(note[:, 1:2], keep.eps[:], ACT.Copy).then_inc(t_ready, 2)
                for p in range(2):
                    nc.scalar.activation(done[:, p, 0:1], keep.eps[:], ACT.Copy).then_inc(done_out[p], 16)
                for kt in range(KT):
                    act.wait_ge(stage_in[kt % 2], 16 * (kt // 2 + 1))
                    nc.scalar.activation(w_hi[:, kt, :], stage[:, kt % 2, :], ACT.Copy).then_inc(w_hi_done, 1)

                def tile(n, k, p):
                    act.wait_ge(mv_done, n + 1)
                    nc.scalar.activation(rstd[:, p:p + 1], mv[:, p, 1:2], ACT.Sqrt,
                                         bias=keep.eps[:]).then_inc(std_done, 1)
                    if nxt and not (isinstance(n, int) and n == 0):
                        modulate(n - 1, 1 - p)

                def modulate(n, p):
                    act.wait_ge(t_ready, n + 3)
                    act.wait_ge(h_lo_done, n + 1)
                    for kt in range(KT):
                        last = nc.scalar.activation(
                            hf[:, kt, :], ps[:, 4 + 2 * p + kt // 4, (kt % 4) * P:(kt % 4 + 1) * P], ACT.Identity,
                            bias=keep.mod1[:, 0, kt:kt + 1], scale=keep.mod1[:, 1, kt:kt + 1])
                    last.then_inc(h_done, 1)

                run(act, tile)
                if nxt:
                    modulate(QT - 1, 1)

            @block.vector
            def _(dve):
                nc.vector.memset(stats[:, 0, 0, 0:1], 0.0).then_inc(prod_done, 2)
                nc.vector.memset(stats[:, 0, 0, 1:2], 0.0).then_inc(h_lo_done, 1)
                nc.vector.memset(stats[:, 0, 0, 2:3], 0.0).then_inc(done_ready, 2)
                for kt in range(KT):
                    dve.wait_ge(w_hi_done, kt + 1)
                    nc.vector.tensor_sub(w_lo[:, kt, :], stage[:, kt % 2, :],
                                         w_hi[:, kt, :].bitcast(F32)).then_inc(w_lo_done, 1)

                def tile(n, k, p):
                    dve.wait_ge(proj_ready, n + 1)
                    dve.wait_ge(done_ready, n + 1)
                    two = row[:, p, :].rearrange("p (b n) -> p b n", b=2)
                    gate = keep.gate[:, layer, :].rearrange("p (b n) -> p b n", b=2)
                    nc.vector.tensor_tensor(two, ps[:, 2 * p:2 * p + 2, :], gate, ALU.mult).then_inc(prod_done, 1)
                    dve.wait_ge(res_in[p], k * 16 + 16)
                    dve.wait_ge(prod_done, n + 3)
                    nc.vector.scalar_tensor_tensor(out=row[:, p, :], in0=res[:, p, :], scalar=ALPHA, in1=row[:, p, :],
                                                   op0=ALU.mult, op1=ALU.add).then_inc(sum_done, 1)
                    dve.wait_ge(sum_done, n + 1)
                    for half in range(2):
                        nc.vector.bn_stats(stats[:, p, half, :],
                                           row[:, p, half * BANK:(half + 1) * BANK]).then_inc(stats_done, 1)
                    dve.wait_ge(stats_done, n * 2 + 2)
                    nc.vector.memset(note[:, 3:4], 0.0)
                    nc.vector.bn_aggr(mv[:, p, :], stats[:, p, :, :].rearrange("p a b -> p (a b)")).then_inc(mv_done, 1)
                    dve.wait_ge(std_done, n + 1)
                    nc.vector.reciprocal(rstd[:, p:p + 1], rstd[:, p:p + 1]).then_inc(rstd_done, 1)
                    dve.wait_ge(rstd_done, n + 1)
                    nc.vector.tensor_scalar(row[:, p, :], row[:, p, :], mv[:, p, 0:1], rstd[:, p:p + 1],
                                            ALU.subtract, ALU.mult).then_inc(norm_done, 1)
                    if nxt and not (isinstance(n, int) and n == 0):
                        low(n - 1)

                def low(n):
                    dve.wait_ge(h_hi_done, n + 1)
                    nc.vector.tensor_sub(keep.h_lo[:, :, ds(n * P, P)], hf[:],
                                         keep.h_hi[:, :, ds(n * P, P)].bitcast(F32)).then_inc(h_lo_done, 1)

                run(dve, tile)
                if nxt:
                    low(QT - 1)

            @block.gpsimd
            def _(pool):
                pool.wait_ge(row_in, 32)

                def tile(n, k, p):
                    pool.wait_ge(norm_done, n + 1)
                    nc.gpsimd.tensor_mul(row[:, p, :], row[:, p, :], ln_g[:]).then_inc(weighted, 1)
                    pool.wait_ge(weighted, n + 1)
                    pool.wait_ge(done_out[p], k * 16 + 16)
                    if nxt:
                        pool.wait_ge(t_ready, n + 1)
                    nc.gpsimd.tensor_add(done[:, p, :], row[:, p, :], ln_b[:]).then_inc(done_ready, 1)
                    if nxt and not (isinstance(n, int) and n == 0):
                        high(n - 1)

                def high(n):
                    pool.wait_ge(h_done, n + 3)
                    nc.gpsimd.tensor_add(hold_out[:], ln_b[:, 0:1], ln_b[:, 1:2])
                    nc.gpsimd.tensor_copy(keep.h_hi[:, :, ds(n * P, P)], hf[:]).then_inc(h_hi_done, 1)

                run(pool, tile)
                if nxt:
                    high(QT - 1)


def conform(nc, io, keep):
    with ExitStack() as outer:
        mo = Memory(nc, outer, "cf")
        conv = mo.sb("conv", [P, KT, L])
        z_s = mo.sb("z_s", [P, KT, L])
        total = mo.sb("total", [P, L])
        mean_w = mo.sb("mean_w", [P, P])
        ps = mo.psum("ps", [P, 8, BANK])
        with ExitStack() as stack:
            m = Memory(nc, stack, "cg")
            w_hi = m.sb("w_hi", [P, 3, PIECE], F32R)
            w_lo = m.sb("w_lo", [P, 3, PIECE], F32R)
            stage = m.sb("stage", [P, 2, PIECE])
            padded = m.sb("padded", [P, 2, L + 2 * PAD])
            sig = m.sb("sig", [P, L])
            odd = m.sb("odd", [P, L])
            taps = m.sb("taps", [P, KT * CONF_KW])
            note = m.sb("note", [P, 4])
            (tap_in, w_hi_done, w_lo_done, g_ready, a_ready, z_ready, sig_done, glu_done, z_done, conv_step,
             total_done, pad_done) = (m.sem(n) for n in (
                 "tap_in", "w_hi_done", "w_lo_done", "g_ready", "a_ready", "z_ready", "sig_done", "glu_done",
                 "z_done", "conv_step", "total_done", "pad_done"))
            stage_in = [m.sem("stage_in0"), m.sem("stage_in1")]
            STEPS = CONF_KW + 1

            with nc.Block() as block:
                @block.sync
                def _(sp):
                    for g in range(2):
                        sp.dma_start(stage[:, g, :], io["conf_w"][g * P:(g + 1) * P, :]).then_inc(stage_in[g], 16)
                    sp.dma_start(taps[:], io["taps"]).then_inc(tap_in, 16)
                    with sp.Fori(0, 11) as i:
                        for b in range(2):
                            sp.wait_ge(w_lo_done, i * 2 + (b + 1))
                            sp.dma_start(stage[:, b, :],
                                         io["conf_w"][ds(i * (2 * P) + (2 + b) * P, P), :]).then_inc(stage_in[b], 16)

                @block.tensor
                def _(pe):
                    def part(c, kind, ready, free):
                        pe.wait_ge(w_lo_done, c * 3 + (kind + 1))
                        pe.wait_ge(free, c + 1)
                        for kt in range(KT):
                            for w, parts in ((w_hi, (keep.h_hi, keep.h_lo)), (w_lo, (keep.h_hi,))):
                                for h in parts:
                                    for half in range(2):
                                        last = nc.tensor.matmul(
                                            ps[:, 2 * kind + half, :], w[:, kind, kt * P:(kt + 1) * P],
                                            h[:, kt, half * BANK:(half + 1) * BANK],
                                            start=(kt == 0 and w is w_hi and h is keep.h_hi),
                                            stop=(kt == KT - 1 and w is w_lo))
                        last.then_inc(ready, 1)

                    with pe.Fori(0, KT) as c:
                        part(c, 0, g_ready, sig_done)
                        part(c, 1, a_ready, glu_done)
                        part(c, 2, z_ready, z_done)

                @block.scalar
                def _(act):
                    for n, s in enumerate((sig_done, z_done)):
                        nc.scalar.activation(note[:, n:n + 1], keep.eps[:], ACT.Copy).then_inc(s, 1)

                    def split(g, slot, kind, loads):
                        act.wait_ge(stage_in[slot], loads * 16)
                        nc.scalar.activation(w_hi[:, kind, :], stage[:, slot, :], ACT.Copy).then_inc(w_hi_done, 1)

                    def tile(c, n, following):
                        act.wait_ge(g_ready, c + 1)
                        act.wait_ge(glu_done, c + 1)
                        nc.scalar.activation(sig[:].rearrange("p (b n) -> p b n", b=2), ps[:, 0:2, :],
                                             ACT.Sigmoid).then_inc(sig_done, 1)
                        if following:
                            piece(c, n, 0)
                            act.wait_ge(a_ready, c + 1)
                            piece(c, n, 1)
                        act.wait_ge(z_ready, c + 1)
                        nc.scalar.activation(z_s[:, ds(c, 1), :].rearrange("p a (b n) -> p (a b) n", b=2),
                                             ps[:, 4:6, :], ACT.Silu).then_inc(z_done, 1)
                        if following:
                            piece(c, n, 2)

                    def piece(c, n, kind):
                        g = 3 * n + 3 + kind
                        i = (c - n) // 2 if isinstance(c, int) else half_c[0]
                        split(None, g % 2, kind, i * 3 + (g // 2 + 1))

                    half_c = [None]
                    for g in range(3):
                        split(g, g % 2, g, g // 2 + 1)
                    with act.Fori(0, 3) as i:
                        half_c[0] = i
                        tile(i * 2, 0, True)
                        tile(i * 2 + 1, 1, True)
                    tile(6, 0, True)
                    tile(7, 1, False)

                @block.gpsimd
                def _(pool):
                    nc.gpsimd.memset(mean_w[:], 1.0 / D)
                    nc.gpsimd.memset(total[:], 0.0).then_inc(total_done, 1)

                    def low(g, slot, kind):
                        pool.wait_ge(w_hi_done, g + 1)
                        nc.gpsimd.tensor_sub(w_lo[:, kind, :], stage[:, slot, :],
                                             w_hi[:, kind, :].bitcast(F32)).then_inc(w_lo_done, 1)

                    def add_total(c):
                        pool.wait_ge(conv_step, c * STEPS)
                        pool.wait_ge(total_done, c)
                        nc.gpsimd.tensor_add(total[:], total[:],
                                             conv[:, ds(c - 1, 1), :].rearrange("p a n -> p (a n)")
                                             ).then_inc(total_done, 1)

                    for g in range(3):
                        low(g, g % 2, g)

                    def tile(c, n):
                        for kind in range(3):
                            low(c * 3 + (3 + kind), (3 * n + 3 + kind) % 2, kind)
                        if not (isinstance(c, int) and c == 0):
                            add_total(c)

                    tile(0, 0)
                    with pool.Fori(0, 3) as i:
                        tile(i * 2 + 1, 1)
                        tile(i * 2 + 2, 0)
                    add_total(7)
                    add_total(8)

                @block.vector
                def _(dve):
                    nc.vector.memset(padded[:, :, 0:PAD], 0.0)
                    nc.vector.memset(padded[:, :, PAD + L:], 0.0).then_inc(pad_done, 1)
                    nc.vector.memset(odd[:, 0:1], 0.0).then_inc(glu_done, 1)
                    dve.wait_ge(tap_in, 16)
                    dve.wait_ge(pad_done, 1)

                    def tile(c, q):
                        dve.wait_ge(a_ready, c + 1)
                        dve.wait_ge(sig_done, c + 2)
                        nc.vector.tensor_tensor(padded[:, q, PAD:PAD + L].rearrange("p (b n) -> p b n", b=2),
                                                ps[:, 2:4, :], sig[:].rearrange("p (b n) -> p b n", b=2),
                                                ALU.mult).then_inc(glu_done, 1)
                        dve.wait_ge(glu_done, c + 2)
                        even = conv[:, ds(c, 1), :].rearrange("p a n -> p (a n)")

                        def tap(k):
                            return taps[:, ds(c * CONF_KW + k, 1)]

                        nc.vector.tensor_scalar(even, padded[:, q, 0:L], tap(0), keep.vcol[:, ds(c + V_DWB, 1)],
                                                ALU.mult, ALU.add).then_inc(conv_step, 1)
                        nc.vector.tensor_scalar(odd[:], padded[:, q, 1:1 + L], tap(1), None,
                                                ALU.mult).then_inc(conv_step, 1)
                        for k in range(2, CONF_KW):
                            dve.wait_ge(conv_step, c * STEPS + (k - 1))
                            into = even if k % 2 == 0 else odd[:]
                            nc.vector.scalar_tensor_tensor(out=into, in0=padded[:, q, k:k + L], scalar=tap(k),
                                                           in1=into, op0=ALU.mult, op1=ALU.add).then_inc(conv_step, 1)
                        dve.wait_ge(conv_step, c * STEPS + CONF_KW)
                        nc.vector.tensor_add(even, even, odd[:]).then_inc(conv_step, 1)
                        dve.wait_ge(conv_step, c * STEPS + STEPS)

                    with dve.Fori(0, KT // 2) as i:
                        tile(i * 2, 0)
                        tile(i * 2 + 1, 1)

        with ExitStack() as stack:
            m = Memory(nc, stack, "cn")
            square = m.sb("square", [P, 2, L])
            rstd = m.sb("rstd", [P, L])
            y_hi = m.sb("y_hi", [P, 2, L])
            y_lo = m.sb("y_lo", [P, 2, L])
            (mean_ready, centred, sq_done, sq_used, std_done, rstd_done, scaled, act_done, gated, y_hi_done,
             y_lo_done) = (m.sem(n) for n in ("mean_ready", "centred", "sq_done", "sq_used", "std_done", "rstd_done",
                                              "scaled", "act_done", "gated", "y_hi_done", "y_lo_done"))
            y_out = [m.sem("y_out0"), m.sem("y_out1")]

            with nc.Block() as block:
                @block.tensor
                def _(pe):
                    for half in range(2):
                        last = nc.tensor.matmul(ps[:, half, :], mean_w[:], total[:, half * BANK:(half + 1) * BANK],
                                                start=True, stop=True)
                    last.then_inc(mean_ready, 1)
                    for c in range(KT):
                        pe.wait_ge(sq_done, c + 1)
                        for half in range(2):
                            last = nc.tensor.matmul(ps[:, 2 + half, :], mean_w[:],
                                                    square[:, c % 2, half * BANK:(half + 1) * BANK],
                                                    start=c == 0, stop=c == KT - 1)
                        last.then_inc(sq_used, 1)

                @block.vector
                def _(dve):
                    dve.wait_ge(mean_ready, 1)
                    for c in range(KT):
                        two = conv[:, c, :].rearrange("p (b n) -> p b n", b=2)
                        nc.vector.tensor_tensor(two, two, ps[:, 0:2, :], ALU.subtract).then_inc(centred, 1)
                    dve.wait_ge(centred, KT)
                    dve.wait_ge(std_done, 1)
                    nc.vector.reciprocal(rstd[:], rstd[:]).then_inc(rstd_done, 1)
                    dve.wait_ge(rstd_done, 1)

                    def low(c):
                        dve.wait_ge(y_hi_done, c + 1)
                        nc.vector.tensor_sub(y_lo[:, c % 2, :].bitcast(F32R), conv[:, c, :],
                                             y_hi[:, c % 2, :]).then_inc(y_lo_done, 1)

                    for c in range(KT):
                        nc.vector.tensor_mul(conv[:, c, :], conv[:, c, :], rstd[:]).then_inc(scaled, 1)
                        if c >= 3:
                            low(c - 3)
                    for c in range(KT - 3, KT):
                        low(c)

                @block.scalar
                def _(act):
                    for c in range(KT):
                        act.wait_ge(centred, c + 1)
                        if c >= 2:
                            act.wait_ge(sq_used, c - 1)
                        nc.scalar.activation(square[:, c % 2, :], conv[:, c, :], ACT.Square).then_inc(sq_done, 1)
                    act.wait_ge(sq_used, KT)
                    nc.scalar.activation(rstd[:].rearrange("p (b n) -> p b n", b=2), ps[:, 2:4, :], ACT.Sqrt,
                                         bias=keep.eps[:]).then_inc(std_done, 1)

                    def high(c):
                        act.wait_ge(gated, c + 1)
                        if c >= 2:
                            act.wait_ge(y_out[c % 2], 32 * (c // 2))
                        nc.scalar.activation(y_hi[:, c % 2, :].bitcast(F32R), conv[:, c, :],
                                             ACT.Copy).then_inc(y_hi_done, 1)

                    for c in range(KT):
                        act.wait_ge(scaled, c + 1)
                        nc.scalar.activation(conv[:, c, :], conv[:, c, :], ACT.Silu,
                                             scale=keep.vcol[:, V_CLNG + c:V_CLNG + c + 1],
                                             bias=keep.vcol[:, V_CLNB + c:V_CLNB + c + 1]).then_inc(act_done, 1)
                        if c >= 2:
                            high(c - 2)
                    for c in range(KT - 2, KT):
                        high(c)

                @block.gpsimd
                def _(pool):
                    for c in range(KT):
                        pool.wait_ge(act_done, c + 1)
                        nc.gpsimd.tensor_mul(conv[:, c, :], conv[:, c, :], z_s[:, c, :]).then_inc(gated, 1)

                @block.sync
                def _(sp):
                    for c in range(KT):
                        sp.wait_ge(y_lo_done, c + 1)
                        for part, buf in ((0, y_hi), (1, y_lo)):
                            sp.dma_start(io["y_hl"][part * D + c * P:part * D + (c + 1) * P, :],
                                         buf[:, c % 2, :]).then_inc(y_out[c % 2], 16)
                    for p in range(2):
                        sp.wait_ge(y_out[p], 32 * KT // 2)


class Keep:
    pass


def build(nc, io, out):
    with ExitStack() as stack:
        m = Memory(nc, stack, "keep")
        keep = Keep()
        keep.vcol = m.sb("vcol", [P, V_N])
        keep.gate = m.sb("gate", [P, DEPTH, D])
        keep.mod1 = m.sb("mod1", [P, 2, KT])
        keep.ones = m.sb("ones", [P, P])
        keep.ident = m.sb("ident", [P, P])
        keep.eps = m.sb("eps", [P, 1])
        keep.subln = m.sb("subln", [P, 1])
        project(nc, io, keep)
        attend(nc, io, keep)
        keep_h = Memory(nc, stack, "h")
        keep.h_hi = keep_h.sb("hi", [P, KT, L], F32R)
        keep.h_lo = keep_h.sb("lo", [P, KT, L], F32R)
        output(nc, io, keep, 0, io["og_hl"], io["attn_w_out"], io["x"], io["x1"], True)
        conform(nc, io, keep)
        output(nc, io, keep, 1, io["y_hl"], io["conf_w_out"], io["x1"], out, False)


def rope_tables():
    import numpy as np
    half = DK // 2
    inv = (1.0 / (np.float32(10000.0) ** (np.arange(0, half, 2, dtype=np.float32) / half))).astype(np.float32)
    t = np.arange(L)
    ar = (t // 64).astype(np.float32)[:, None] * inv[None, :]
    ac = (t % 64).astype(np.float32)[:, None] * inv[None, :]
    ang = np.concatenate([ar, ar, ac, ac], axis=-1)
    sign = np.where(np.arange(DK) % half < half // 2, -1.0, 1.0).astype(np.float32)
    cos, sin = np.cos(ang), np.sin(ang) * sign
    both = np.concatenate([cos.T, sin.T], axis=1)
    return np.ascontiguousarray(np.concatenate([both, both], axis=0).astype(np.float32))


def kernel(x, c, ctx, c_ctx, mod_w, mod_b, ln_g, ln_b,
           attn_w_in, attn_w_out, attn_lambda_q1, attn_lambda_k1, attn_lambda_q2, attn_lambda_k2, attn_subln_g,
           conf_w_in, conf_dw_w, conf_dw_b, conf_ln_g, conf_ln_b, conf_w_out,
           sc_w_in, sc_conv_w, sc_w_out,
           pool_w_in, pool_w_group, pool_scale, pool_w_out):
    import numpy as np
    import concourse.bacc as bacc
    from concourse.bass_utils import run_bass_kernel_spmd

    a = lambda v: np.asarray(v)
    tokens = np.concatenate([a(x)[0], a(ctx)[0]], axis=0)
    cols = [a(c)[0], a(c_ctx), a(mod_b).reshape(-1), a(conf_dw_b)[0], a(conf_ln_g)[0], a(conf_ln_b)[0],
            a(attn_subln_g)[0]]
    vec = np.concatenate([v.reshape(-1, P) for v in cols], axis=0).T

    def pieces(w):
        n = w.shape[1] // P
        return w.reshape(KT, P, n, P).transpose(2, 1, 0, 3).reshape(n, P, PIECE)

    w_in = a(attn_w_in)[0]
    v_w = w_in[:, 2 * D:3 * D].reshape(4, 2, P, 2, BANK)
    v_w = v_w.transpose(3, 0, 2, 1, 4).reshape(8, P, PIECE)
    w_in = np.concatenate([pieces(w_in[:, :2 * D]), pieces(w_in[:, 3 * D:]), v_w], axis=0)
    conf = pieces(a(conf_w_in)[0]).reshape(3, KT, P, PIECE)
    conf = conf[[1, 0, 2]].transpose(1, 0, 2, 3).reshape(3 * KT * P, PIECE)
    taps = a(conf_dw_w)[0].reshape(CONF_KW, KT, P).transpose(2, 1, 0).reshape(P, KT * CONF_KW)
    arrays = {
        "x": a(x)[0], "x_t": tokens.T.reshape(KT, P, LT), "vec": vec, "mod_w": a(mod_w), "mod_b": a(mod_b),
        "ln_g": a(ln_g), "ln_b": a(ln_b), "w_in": w_in, "attn_w_out": a(attn_w_out)[0],
        "lam": np.stack([a(v)[0] for v in (attn_lambda_q1, attn_lambda_k1, attn_lambda_q2, attn_lambda_k2)])[None],
        "rope": rope_tables(), "conf_w": conf, "taps": taps, "conf_w_out": a(conf_w_out)[0],
    }
    arrays = {k: np.ascontiguousarray(v) for k, v in arrays.items()}
    nc = bacc.Bacc("TRN2", target_bir_lowering=False, num_devices=1)
    io = {k: nc.dram_tensor(f"in_{k}", v.shape, mybir.dt.from_np(v.dtype), kind="ExternalInput").ap()
          for k, v in arrays.items()}
    for name, shape in (("q_hl", (HEADS * 2 * P, L)), ("k_hl", (HEADS * 2 * P, LT)), ("v_hl", (2, KEYT, P, D)),
                        ("z_s", (D, L)), ("og_hl", (2 * D, L)), ("x1", (L, D)), ("y_hl", (2 * D, L))):
        io[name] = nc.dram_tensor(f"scratch_{name}", shape, F32, kind="Internal").ap()
    out = nc.dram_tensor("out", (L, D), F32, kind="ExternalOutput").ap()
    build(nc, io, out)
    r = run_bass_kernel_spmd(nc, [{f"in_{k}": v for k, v in arrays.items()}], core_ids=[0])
    return r.results[0]["out"].reshape(1, L, D)
```

```python
import math
from contextlib import ExitStack

import concourse.bass as bass
from concourse import mybir

F32 = mybir.dt.float32
F32R = mybir.dt.float32r
ALU = mybir.AluOpType
ACT = mybir.ActivationFunctionType
AX = mybir.AxisListType

P = 128
D = 1024
KT = D // P
L = 1024
LC = 256
LT = L + LC
HEADS = 8
DK = 64
DV = 128
BANK = 512
HALVES = L // BANK
QT = L // P
KEYT = LT // P
CONF_KW = 31
PAD = (CONF_KW - 1) // 2
DEPTH = 2
ALPHA = (2 * DEPTH) ** 0.25
LAMBDA_INIT = 0.8 - 0.6 * math.exp(-0.3 * 0)
EPS = 1e-5
PIECE = KT * P
MASK_HALF_SWAP = list(range(16, 32)) + list(range(16))

V_C, V_CCTX, V_MODB, V_DWB, V_CLNG, V_CLNB, V_SUBG = 0, 8, 16, 64, 72, 80, 88
V_N = 89


def ds(i, n):
    return bass.ds(i, n)


class Memory:

    def __init__(self, nc, stack, tag):
        self.nc, self.stack, self.tag = nc, stack, tag

    def sb(self, name, shape, dt=F32):
        return self.stack.enter_context(self.nc.sbuf_tensor(f"{self.tag}_{name}", shape, dt))

    def psum(self, name, shape):
        return self.stack.enter_context(self.nc.psum_tensor(f"{self.tag}_{name}", shape, F32))

    def sem(self, name):
        return self.stack.enter_context(self.nc.semaphore(f"{self.tag}_{name}"))


def project(nc, io, keep):
    UQK, UZ = 2 * HEADS, HEADS
    UNITS = UQK + UZ
    with ExitStack() as stack:
        m = Memory(nc, stack, "pj")
        work = m.sb("work", [P, KT, LT])
        h_hi = m.sb("h_hi", [P, KT, LT], F32R)
        h_lo = m.sb("h_lo", [P, KT, LT], F32R)
        w_hi = m.sb("w_hi", [P, 4, PIECE], F32R)
        w_lo = m.sb("w_lo", [P, 4, PIECE], F32R)
        stage = m.sb("stage", [P, 2, PIECE])
        mod_tile = m.sb("mod_tile", [P, 4, D])
        acc = m.sb("acc", [P, 2, D])
        cos = m.sb("cos", [P, L])
        sin = m.sb("sin", [P, L])
        silu_c = m.sb("silu_c", [P, 2 * KT])
        mod0 = m.sb("mod0", [P, 2, 2, KT])
        note = m.sb("note", [P, 10])
        low_note = m.sb("low_note", [P, 1])
        ps = m.psum("ps", [P, 8, BANK])

        straight = [work[:, 0, :], work[:, 1, :]]
        turned = work[:, 2, :]
        out_hi = [work[:, 3, :], work[:, 4, :]]
        out_lo = [work[:, 5, :], work[:, 6, :]]

        vec_in, table_in = m.sem("vec_in"), m.sem("table_in")
        x_in = [m.sem("x_in0"), m.sem("x_in1")]
        mod0_used = m.sem("mod0_used")
        mod_in = [m.sem(f"mod_in{n}") for n in range(4)]
        stage_in = [m.sem("stage_in0"), m.sem("stage_in1")]
        silu_done, ones_done = m.sem("silu_done"), m.sem("ones_done")
        mod_acc, mod_sums, mod_ready = m.sem("mod_acc"), m.sem("mod_sums"), m.sem("mod_ready")
        gate_done = m.sem("gate_done")
        h_mod, h_hi_done, h_lo_done = m.sem("h_mod"), m.sem("h_hi_done"), m.sem("h_lo_done")
        w_hi_done, w_lo_done = m.sem("w_hi_done"), m.sem("w_lo_done")
        proj_ready, proj_evac = m.sem("proj_ready"), m.sem("proj_evac")
        swapped, sin_done, cos_done = m.sem("swapped"), m.sem("sin_done"), m.sem("cos_done")
        rope_done, out_hi_done, out_lo_done = m.sem("rope_done"), m.sem("out_hi_done"), m.sem("out_lo_done")
        v_hi_done, v_lo_done = m.sem("v_hi_done"), m.sem("v_lo_done")
        qk_out = [m.sem("qk_out0"), m.sem("qk_out1")]
        z_out = [m.sem("z_out0"), m.sem("z_out1")]
        v_out = [m.sem("v_out0"), m.sem("v_out1")]

        MOD0 = 18
        vcol = keep.vcol
        mod_w = io["mod_w"].rearrange("l d n -> (l d) n")

        with nc.Block() as block:
            @block.sync
            def _(sp):
                sp.dma_start(vcol[:], io["vec"]).then_inc(vec_in, 16)

                def load_mod(slot, rows, cols):
                    sp.dma_start(mod_tile[:, slot, :], mod_w[rows, cols]).then_inc(mod_in[slot], 16)

                for n in range(2 * KT):
                    if n % 2 == 0:
                        if n >= 4:
                            sp.wait_ge(mod_acc, n)
                        load_mod(n % 4, slice(n // 2 * P, (n // 2 + 1) * P), slice(0, D))
                    else:
                        if n >= 4:
                            sp.wait_ge(mod0_used, (n - 3) // 2)
                        sp.dma_start(mod_tile[:, n % 4, :].rearrange("p (k n) -> p k n", k=KT),
                                     mod_w[0:D, D + n // 2 * P:D + (n // 2 + 1) * P]
                                     .rearrange("(k p) n -> p k n", p=P)).then_inc(mod_in[n % 4], 16)
                    if n == 7:
                        for g in range(2):
                            sp.dma_start(stage[:, g, :], io["w_in"][g]).then_inc(stage_in[g], 16)
                sp.dma_start(cos[:], io["rope"][:, 0:L]).then_inc(table_in, 16)
                sp.dma_start(sin[:], io["rope"][:, L:2 * L]).then_inc(table_in, 16)
                sp.wait_ge(w_lo_done, 1)
                sp.dma_start(stage[:, 0, :], io["w_in"][2]).then_inc(stage_in[0], 16)

                def load_piece(g, slot):
                    sp.wait_ge(w_lo_done, g - 1)
                    sp.dma_start(stage[:, slot, :], io["w_in"][ds(g, 1)].rearrange("a p n -> (a p) n")
                                 if not isinstance(g, int) else io["w_in"][g]).then_inc(stage_in[slot], 16)

                for kind, scratch, width in ((0, io["q_hl"], L), (1, io["k_hl"], LT)):
                    with sp.Fori(0, 2) as i:
                        for j in range(4):
                            u = i * 4 + (HEADS * kind + j)
                            load_piece(u + 3, (j + 3) % 2)
                            sp.wait_ge(out_lo_done, u + 2)
                            for part, buf in ((0, out_hi), (1, out_lo)):
                                sp.dma_start(scratch[ds((i * 4 + j) * (2 * P) + part * P, P), :],
                                             buf[j % 2][:, 0:width]).then_inc(qk_out[j % 2], 16)
                sp.wait_ge(mod0_used, KT)
                with sp.Fori(0, 2) as i:
                    for j in range(4):
                        u = i * 4 + (UQK + j)
                        load_piece(u + 3, (j + 3) % 2)
                        for b in range(4):
                            step = 4 * j + b
                            before = step - 3 if step < 4 else step - 3 + (1 if step < 12 else 2)
                            sp.wait_ge(mod_acc, i * 18 + (MOD0 + before))
                            t = 4 * (j % 2) + b
                            if j < 2:
                                load_mod(b, ds(i * D + t * P, P), slice(2 * D, 3 * D))
                            else:
                                load_mod(b, slice(D + t * P, D + (t + 1) * P), ds(i * D, D))
                load_piece(27, 1)
                for vc in range(2):
                    for tt in range(KEYT):
                        n = KEYT * vc + tt
                        if vc == 0 and tt in (1, 2):
                            load_piece(27 + tt, (27 + tt) % 2)
                        if vc == 1 and tt == 0:
                            load_piece(30, 0)
                            load_piece(31, 1)
                        sp.wait_ge(v_lo_done, n + 3)
                        for part, buf in ((0, out_hi), (1, out_lo)):
                            sp.dma_start(io["v_hl"][part, tt, :, vc * BANK:(vc + 1) * BANK],
                                         buf[n % 2][:, 0:BANK]).then_inc(v_out[n % 2], 16)
                for p in range(2):
                    sp.wait_ge(qk_out[p], 32 + 32 * UQK // 2)
                    sp.wait_ge(z_out[p], 16 + 16 * UZ // 2)
                    sp.wait_ge(v_out[p], 32 * KEYT)

            @block.gpsimd
            def _(pool):
                nc.gpsimd.memset(keep.ones[:], 1.0).then_inc(ones_done, 1)
                nc.gpsimd.memset(keep.eps[:], EPS)
                nc.gpsimd.memset(keep.ident[:], 0.0).then_inc(ones_done, 1)
                pool.wait_ge(ones_done, 2)
                nc.gpsimd.affine_select(out=keep.ident[:], in_=keep.ident[:], compare_op=ALU.not_equal, fill=1.0,
                                        base=0, pattern=[[-1, P]], channel_multiplier=1).then_inc(ones_done, 1)
                for kt in range(KT):
                    pool.wait_ge(x_in[kt // 4], 16 * 4)
                    pool.wait_ge(mod_ready, 4)
                    for a, cols in ((0, slice(0, L)), (1, slice(L, LT))):
                        nc.gpsimd.tensor_scalar(work[:, kt, cols], work[:, kt, cols], mod0[:, 1, a, kt:kt + 1],
                                                mod0[:, 0, a, kt:kt + 1], ALU.mult, ALU.add).then_inc(h_mod, 1)
                pool.wait_ge(table_in, 16 * (2 + DEPTH))
                with pool.Fori(0, 4) as i:
                    for j in range(4):
                        pool.wait_ge(swapped, i * 4 + (j + 1))
                        nc.gpsimd.tensor_mul(straight[j % 2][:, 0:L], straight[j % 2][:, 0:L],
                                             cos[:]).then_inc(cos_done, 1)

            @block.scalar
            def _(act):
                act.wait_ge(vec_in, 16)
                nc.scalar.activation(silu_c[:], vcol[:, 0:2 * KT], ACT.Silu).then_inc(silu_done, 1)
                nc.scalar.activation(note[:, 0:1], vcol[:, 0:1], ACT.Copy).then_inc(proj_evac, 2)
                nc.scalar.activation(note[:, 1:2], vcol[:, 0:1], ACT.Copy).then_inc(out_hi_done, 1)
                for p in range(2):
                    nc.scalar.activation(note[:, 2 + p:3 + p], vcol[:, 0:1], ACT.Copy).then_inc(qk_out[p], 32)
                    nc.scalar.activation(note[:, 8 + p:9 + p], vcol[:, 0:1], ACT.Copy).then_inc(z_out[p], 16)

                act.wait_ge(mod0_used, 6)
                for kt in range(KT):
                    act.dma_start(work[:, kt, :], io["x_t"][kt]).then_inc(x_in[kt // 4], 16)
                for n in range(DEPTH):
                    act.dma_start(keep.gate[:, n, :], io["mod_b"][n:n + 1, 2 * D:3 * D]
                                  .partition_broadcast(P).rearrange("p a n -> p (a n)")).then_inc(table_in, 16)

                def split_piece(g, slot, wslot, loads):
                    act.wait_ge(stage_in[slot], loads * 16)
                    nc.scalar.activation(w_hi[:, wslot, :], stage[:, slot, :], ACT.Copy).then_inc(w_hi_done, 1)

                split_piece(0, 0, 0, 1)
                split_piece(1, 1, 1, 1)
                for kt in range(KT):
                    act.wait_ge(h_mod, 2 * kt + 2)
                    nc.scalar.activation(h_hi[:, kt, :], work[:, kt, :], ACT.Copy).then_inc(h_hi_done, 1)
                split_piece(2, 0, 2, 2)
                act.wait_ge(h_lo_done, KT)
                for kind in range(2):
                    with act.Fori(0, 2) as i:
                        for j in range(4):
                            u = i * 4 + (HEADS * kind + j)
                            p = j % 2
                            act.wait_ge(proj_ready, u + 1)
                            act.wait_ge(rope_done, u + 1)
                            if kind == 1:
                                act.wait_ge(out_lo_done, u + 1)
                                nc.scalar.activation(turned[:, L:LT], ps[:, 3 * p + 2, 0:LC], ACT.Copy)
                            nc.scalar.activation(straight[p][:, 0:L].rearrange("p (b n) -> p b n", b=2),
                                                 ps[:, 3 * p:3 * p + 2, :], ACT.Copy,
                                                 scale=DK ** -0.5 if kind == 0 else 1.0).then_inc(proj_evac, 1)
                            act.wait_ge(rope_done, u + 3)
                            act.wait_ge(qk_out[p], i * 64 + 32 * (4 * kind + j // 2 + 1))
                            width = L if kind == 0 else LT
                            nc.scalar.activation(out_hi[p][:, 0:width].bitcast(F32R), turned[:, 0:width],
                                                 ACT.Copy).then_inc(out_hi_done, 1)
                            act.wait_ge(proj_ready, u + 1)
                            split_piece(u + 3, (j + 3) % 2, (j + 3) % 4, i * 2 + (4 * kind + (j + 3) // 2 + 1))
                act.wait_ge(rope_done, 2 + UQK)
                with act.Fori(0, 2) as i:
                    for j in range(4):
                        u = i * 4 + (UQK + j)
                        p = j % 2
                        act.wait_ge(proj_ready, u + 1)
                        act.wait_ge(z_out[p], i * 32 + 16 * (j // 2 + 1))
                        nc.scalar.activation(straight[p][:, 0:L].rearrange("p (b n) -> p b n", b=2),
                                             ps[:, 3 * p:3 * p + 2, :], ACT.Silu).then_inc(proj_evac, 1)
                        act.wait_ge(proj_evac, u + 3)
                        act.dma_start(io["z_s"][ds((i * 4 + j) * P, P), :],
                                      straight[p][:, 0:L]).then_inc(z_out[p], 16)
                        split_piece(u + 3, (j + 3) % 2, (j + 3) % 4, i * 2 + (8 + (j + 3) // 2 + 1))
                act.wait_ge(proj_ready, UNITS)
                split_piece(27, 1, 3, 14)
                for p in range(2):
                    act.wait_ge(qk_out[p], 32 + 32 * UQK // 2)
                for vc in range(2):
                    for tt in range(KEYT):
                        n = KEYT * vc + tt
                        act.wait_ge(proj_ready, UNITS + n + 1)
                        if n >= 2:
                            act.wait_ge(v_out[n % 2], 32 * (n // 2))
                        nc.scalar.activation(out_hi[n % 2][:, 0:BANK].bitcast(F32R), ps[:, 3 * (n % 2), :],
                                             ACT.Copy).then_inc(v_hi_done, 1)
                    if vc == 0:
                        for g in range(28, 32):
                            split_piece(g, g % 2, g % 4, g // 2 + 1)

            @block.vector
            def _(dve):
                nc.vector.memset(note[:, 7:8], 0.0).then_inc(rope_done, 2)
                nc.vector.memset(note[:, 6:7], 0.0).then_inc(v_lo_done, 2)
                nc.vector.memset(low_note[:], 0.0).then_inc(out_lo_done, 1)
                dve.wait_ge(silu_done, 1)
                for a in range(2):
                    nc.vector.memset(acc[:, a, :], 0.0).then_inc(mod_acc, 1)
                for t in range(KT):
                    dve.wait_ge(mod_in[2 * t % 4], 16 * (t // 2 + 1))
                    for a in range(2):
                        dve.wait_ge(mod_acc, 2 * t + a + 1)
                        nc.vector.scalar_tensor_tensor(out=acc[:, a, :], in0=mod_tile[:, 2 * t % 4, :],
                                                       scalar=silu_c[:, a * KT + t:a * KT + t + 1],
                                                       in1=acc[:, a, :], op0=ALU.mult, op1=ALU.add).then_inc(mod_acc, 1)
                dve.wait_ge(mod_sums, 2)
                sums = ps[:, 7, 0:4 * KT].rearrange("p (s k a) -> p s a k", s=2, a=2)
                for a in range(2):
                    nc.vector.tensor_tensor(mod0[:, 0, a, :], sums[:, 1, a, :], vcol[:, V_MODB:V_MODB + KT],
                                            ALU.add).then_inc(mod_ready, 1)
                    nc.vector.scalar_tensor_tensor(out=mod0[:, 1, a, :], in0=sums[:, 0, a, :], scalar=1.0,
                                                   in1=vcol[:, V_MODB + KT:V_MODB + 2 * KT],
                                                   op0=ALU.add, op1=ALU.add).then_inc(mod_ready, 1)

                def low_piece(g, slot, wslot):
                    dve.wait_ge(w_hi_done, g + 1)
                    nc.vector.tensor_sub(w_lo[:, wslot, :], stage[:, slot, :],
                                         w_hi[:, wslot, :].bitcast(F32)).then_inc(w_lo_done, 1)

                low_piece(0, 0, 0)
                low_piece(1, 1, 1)
                for kt in range(KT):
                    dve.wait_ge(h_hi_done, kt + 1)
                    nc.vector.tensor_sub(h_lo[:, kt, :], work[:, kt, :],
                                         h_hi[:, kt, :].bitcast(F32)).then_inc(h_lo_done, 1)
                low_piece(2, 0, 2)
                dve.wait_ge(table_in, 16 * (2 + DEPTH))
                for kind in range(2):
                    width = L if kind == 0 else LT
                    with dve.Fori(0, 2) as i:
                        for j in range(4):
                            u = i * 4 + (HEADS * kind + j)
                            p = j % 2
                            dve.wait_ge(proj_evac, u + 3)
                            dve.wait_ge(out_hi_done, u + 1)
                            dve.wait_ge(out_lo_done, u + 1)
                            nc.vector.memset(note[:, 5:6], 0.0)
                            nc.vector.stream_shuffle(turned[:, 0:L], straight[p][:, 0:L],
                                                     MASK_HALF_SWAP).then_inc(swapped, 1)
                            dve.wait_ge(swapped, u + 1)
                            nc.vector.tensor_mul(turned[:, 0:L], turned[:, 0:L], sin[:]).then_inc(sin_done, 1)
                            dve.wait_ge(sin_done, u + 1)
                            dve.wait_ge(cos_done, u + 1)
                            nc.vector.tensor_add(turned[:, 0:L], turned[:, 0:L],
                                                 straight[p][:, 0:L]).then_inc(rope_done, 1)
                            dve.wait_ge(out_hi_done, u + 2)
                            dve.wait_ge(rope_done, u + 3)
                            nc.vector.tensor_sub(out_lo[p][:, 0:width].bitcast(F32R), turned[:, 0:width],
                                                 out_hi[p][:, 0:width]).then_inc(out_lo_done, 1)
                            low_piece(u + 3, (j + 3) % 2, (j + 3) % 4)
                with dve.Fori(0, 2) as i:
                    for j in range(4):
                        u = i * 4 + (UQK + j)
                        half = j // 2
                        for b in range(4):
                            step = 4 * j + b
                            pos = step + half
                            if step % 8 == 0:
                                dve.wait_ge(mod_sums, i * 2 + 2)
                                nc.vector.memset(acc[:, half, :], 0.0).then_inc(mod_acc, 1)
                            dve.wait_ge(mod_in[b], i * 64 + 16 * (4 + j + 1))
                            dve.wait_ge(mod_acc, i * 18 + (MOD0 + pos + 1))
                            t = 4 * (j % 2) + b
                            nc.vector.scalar_tensor_tensor(
                                out=acc[:, half, :], in0=mod_tile[:, b, :], scalar=silu_c[:, t:t + 1],
                                in1=acc[:, half, :], op0=ALU.mult, op1=ALU.add).then_inc(mod_acc, 1)
                        low_piece(u + 3, (j + 3) % 2, (j + 3) % 4)
                    dve.wait_ge(mod_sums, i * 2 + 3)
                    g = keep.gate[:, ds(i, 1), :].rearrange("p a (b n) -> p (a b) n", b=2)
                    nc.vector.tensor_tensor(g, ps[:, 6:8, :], g, ALU.add).then_inc(gate_done, 1)
                    dve.wait_ge(mod_sums, i * 2 + 4)
                    nc.vector.tensor_tensor(keep.mod1[:, ds(i, 1), :].rearrange("p a n -> p (a n)"), ps[:, 7, 0:KT],
                                            vcol[:, ds(i * KT + (V_MODB + 3 * KT), KT)],
                                            ALU.add).then_inc(gate_done, 1)
                low_piece(27, 1, 3)
                dve.wait_ge(gate_done, 4)
                nc.vector.tensor_scalar_add(keep.mod1[:, 1, :], keep.mod1[:, 1, :], 1.0)
                for vc in range(2):
                    for tt in range(KEYT):
                        n = KEYT * vc + tt
                        dve.wait_ge(v_hi_done, n + 1)
                        nc.vector.tensor_sub(out_lo[n % 2][:, 0:BANK].bitcast(F32R), ps[:, 3 * (n % 2), :],
                                             out_hi[n % 2][:, 0:BANK]).then_inc(v_lo_done, 1)
                    if vc == 0:
                        for g in range(28, 32):
                            low_piece(g, g % 2, g % 4)

            @block.tensor
            def _(pe):
                pe.wait_ge(ones_done, 1)
                pe.wait_ge(silu_done, 1)
                both = silu_c[:].rearrange("p (a k) -> p k a", a=2)
                for n in range(KT):
                    slot = (2 * n + 1) % 4
                    pe.wait_ge(mod_in[slot], 16 * (n // 2 + 1))
                    for k in range(KT):
                        last = nc.tensor.matmul(ps[:, 7, 2 * n:2 * n + 2], mod_tile[:, slot, k * P:(k + 1) * P],
                                                both[:, k, :], start=k == 0, stop=k == KT - 1)
                    last.then_inc(mod0_used, 1)
                pe.wait_ge(mod_acc, MOD0)
                for k in range(KT):
                    for a in range(2):
                        at = 2 * (KT + k) + a
                        last = nc.tensor.matmul(ps[:, 7, at:at + 1], acc[:, a, k * P:(k + 1) * P],
                                                keep.ones[:, 0:1], start=True, stop=True)
                last.then_inc(mod_sums, 2)

                def unit(u, j, context):
                    pe.wait_ge(w_lo_done, u + 1)
                    pe.wait_ge(proj_evac, u + 1)
                    p = j % 2
                    outs = [(3 * p + n, n * BANK, BANK) for n in range(HALVES)]
                    if context:
                        outs.append((3 * p + 2, L, LC))
                    for kt in range(KT):
                        if j == 0 and not context:
                            pe.wait_ge(h_lo_done, kt + 1)
                        for w, parts in ((w_hi, (h_hi, h_lo)), (w_lo, (h_hi,))):
                            for h in parts:
                                for bank, at, n in outs:
                                    last = nc.tensor.matmul(
                                        ps[:, bank, 0:n], w[:, j, kt * P:(kt + 1) * P], h[:, kt, at:at + n],
                                        start=(kt == 0 and w is w_hi and h is h_hi),
                                        stop=(kt == KT - 1 and w is w_lo))
                    last.then_inc(proj_ready, 1)

                for kind in range(2):
                    with pe.Fori(0, 2) as i:
                        for j in range(4):
                            unit(i * 4 + (HEADS * kind + j), j, kind == 1)
                with pe.Fori(0, 2) as i:
                    for j in range(4):
                        unit(i * 4 + (UQK + j), j, False)
                        if j == 2:
                            pe.wait_ge(mod_acc, i * 18 + (MOD0 + 9))
                            for n in range(2):
                                last = nc.tensor.matmul(ps[:, 6 + n, :], keep.ones[:],
                                                        acc[:, 0, n * BANK:(n + 1) * BANK], start=True, stop=True)
                            last.then_inc(mod_sums, 1)
                    pe.wait_ge(mod_acc, i * 18 + (MOD0 + 18))
                    pe.wait_ge(gate_done, i * 2 + 1)
                    for n in range(KT):
                        last = nc.tensor.matmul(ps[:, 7, n:n + 1], acc[:, 1, n * P:(n + 1) * P],
                                                keep.ones[:, 0:1], start=True, stop=True)
                    last.then_inc(mod_sums, 1)
                with pe.Fori(0, 2) as vc:
                    for tt in range(KEYT):
                        if tt < 2:
                            pe.wait_ge(proj_evac, UNITS + 2)
                        pe.wait_ge(v_lo_done, vc * KEYT + (tt + 1))
                        for kt in range(KT):
                            if tt == 0 and kt % 2 == 0:
                                pe.wait_ge(w_lo_done, vc * 4 + (UNITS + kt // 2 + 1))
                            for h, parts in ((h_hi, (w_hi, w_lo)), (h_lo, (w_hi,))):
                                for w in parts:
                                    last = nc.tensor.matmul(
                                        ps[:, 3 * (tt % 2), :], h[:, kt, tt * P:(tt + 1) * P],
                                        w[:, kt // 2, (kt % 2) * BANK:(kt % 2 + 1) * BANK],
                                        start=(kt == 0 and h is h_hi and w is w_hi),
                                        stop=(kt == KT - 1 and h is h_lo))
                        last.then_inc(proj_ready, 1)


def attend(nc, io, keep):
    ROUNDS = [(0, 4), (4, 4), (8, 2)]
    BANK_T = [(5, 6, 5), (5, 6, 5), (6, 5, 6), (6, 5, 6)]
    BANK_MEAN, BANK_SPREAD, BANK_PV = 6, 5, 7
    RMS_SHRINK = 2.0 ** -30
    GROUP = 4
    REST = LT - 2 * BANK
    PV_KEYS = [(0, 1), (2, 3, 4), (5, 6), (7, 8, 9)]
    with ExitStack() as stack:
        m = Memory(nc, stack, "at")
        q_a = m.sb("q_a", [P, 2, 2, L], F32R)
        q_b = m.sb("q_b", [P, 2, 2, L], F32R)
        k_s = m.sb("k_s", [P, 2, 2, LT], F32R)
        v_hi = m.sb("v_hi", [P, 2, KEYT, DV], F32R)
        v_lo = m.sb("v_lo", [P, 2, KEYT, DV], F32R)
        z_s = m.sb("z_s", [P, 2, BANK])
        prob0 = m.sb("prob0", [P, 4, LT])
        prob1 = m.sb("prob1", [P, 2, LT])
        a_hi = m.sb("a_hi", [P, 2, KEYT, GROUP * P], F32R)
        a_lo = m.sb("a_lo", [P, 2, KEYT, GROUP * P], F32R)
        square = m.sb("square", [P, BANK])
        gated = m.sb("gated", [P, BANK])
        normed = m.sb("normed", [P, BANK])
        o_hi = m.sb("o_hi", [P, BANK])
        rms = m.sb("rms", [P, GROUP])
        eps_sq = m.sb("eps_sq", [P, GROUP])
        sum0 = m.sb("sum0", [P, 4, GROUP])
        peak = m.sb("peak", [P, 2, 4])
        stat = m.sb("stat", [P, 2, 8])
        lam_in = m.sb("lam_in", [P, 4, DK])
        lam = m.sb("lam", [P, 6])
        note = m.sb("note", [P, 10])
        hold_out = m.sb("hold_out", [P, 1])
        mean_w = m.sb("mean_w", [P, 4])
        ps = m.psum("ps", [P, 8, BANK])

        lam_loaded, lam_step, lam_exp, lam_ready = (m.sem(n) for n in ("lam_loaded", "lam_step", "lam_exp", "lam_ready"))
        head_in = [m.sem("head_in0"), m.sem("head_in1")]
        v_in = [m.sem("v_in0"), m.sem("v_in1")]
        z_in = [m.sem("z_in0"), m.sem("z_in1")]
        s_ready = m.sem("s_ready")
        peak_done = m.sem("peak_done")
        max_done = [m.sem("max_done0"), m.sem("max_done1")]
        exp_done = [m.sem("exp_done0"), m.sem("exp_done1")]
        neg_done, scaled, diff_done = (m.sem(n) for n in ("neg_done", "scaled", "diff_done"))
        t_ready, t_hi_done, t_lo_done = m.sem("t_ready"), m.sem("t_hi_done"), m.sem("t_lo_done")
        pv_ready, sq_done, gated_done, mean_ready = (m.sem(n) for n in ("pv_ready", "sq_done", "gated_done", "mean_ready"))
        eps_done, var_done, rms_done, inv_rms_done, diag_done, spread_ready = (m.sem(n) for n in (
            "eps_done", "var_done", "rms_done", "inv_rms_done", "diag_done", "spread_ready"))
        normed_done, o_hi_done, o_lo_done, og_out = (m.sem(n) for n in ("normed_done", "o_hi_done", "o_lo_done", "og_out"))

        GROUPS = HEADS * QT // GROUP
        TILES = HEADS * QT
        IN_HEAD = 16 * 12
        IN_V = 16 * 2

        def run(eng, group):
            group(0, 0)
            group(1, 1)
            with eng.Fori(0, 3) as i:
                for b in range(4):
                    group(i * 4 + (b + 2), (b + 2) % 4)
            for g in range(14, GROUPS):
                group(g, g % 4)

        def softmaxed(g, c):
            return not (isinstance(g, int) and g * GROUP + c + 2 >= TILES)

        def early(g, n):
            return isinstance(g, int) and g < n

        with nc.Block() as block:
            @block.sync
            def _(sp):
                sp.dma_start(lam_in[:], io["lam"].partition_broadcast(P).rearrange("p a b n -> p (a b) n")
                             ).then_inc(lam_loaded, 16)

                def load_head(h, slot):
                    row = h * (2 * P)
                    for mp in range(2):
                        for part in range(2):
                            top = slice(part * DK, (part + 1) * DK)
                            other = slice((1 - part) * DK, (2 - part) * DK)
                            src = io["q_hl"][ds(row + (part * P + mp * DK), DK), :]
                            sp.dma_start(q_a[top, slot, mp, :].bitcast(F32), src).then_inc(head_in[slot], 16)
                            sp.dma_start(q_b[other, slot, mp, :].bitcast(F32), src).then_inc(head_in[slot], 16)
                            src = io["k_hl"][ds(row + (part * P + mp * DK), DK), :]
                            sp.dma_start(k_s[top, slot, mp, :].bitcast(F32), src).then_inc(head_in[slot], 16)

                def load_v(h, slot):
                    for part, v in ((0, v_hi), (1, v_lo)):
                        src = io["v_hl"][part].rearrange("t p n -> p t n")[:, :, ds(h * DV, DV)]
                        sp.dma_start(v[:, slot, :, :].bitcast(F32), src).then_inc(v_in[slot], 16)

                def load_z(row, half):
                    sp.dma_start(z_s[:, half, :], io["z_s"][ds(row, P), half * BANK:(half + 1) * BANK]
                                 ).then_inc(z_in[half], 16)

                def store(row, half, n):
                    sp.wait_ge(o_lo_done, n + 1)
                    for part, buf in ((0, o_hi), (1, normed)):
                        sp.dma_start(io["og_hl"][ds(row + part * D, P), half * BANK:(half + 1) * BANK],
                                     buf[:]).then_inc(og_out, 16)

                def group(g, n, head):
                    half = (g if isinstance(g, int) else g_mod[0]) % 2
                    heads_left = half == 0 and not (isinstance(g, int) and g == GROUPS - 2)
                    if heads_left:
                        sp.wait_ge(s_ready, (n + 2) * (3 * GROUP))
                        load_head(head + 2, 1 - g_mod[0] // 2)
                    sp.wait_ge(gated_done, n + 2)
                    load_z((head + 1) * P, half)
                    store(head * P, half, n)
                    if heads_left:
                        sp.wait_ge(pv_ready, n + 2)
                        load_v(head + 2, 1 - g_mod[0] // 2)

                g_mod = [None]
                load_head(0, 0)
                load_v(0, 0)
                load_z(0, 0)
                load_z(0, 1)
                load_head(1, 1)
                load_v(1, 1)
                with sp.Fori(0, 3) as i:
                    for b in range(4):
                        g_mod[0] = (b + 2) % 4
                        group(None, i * 4 + b, i * 2 + b // 2)
                for g in (14, 15):
                    group(g, g - 2, (g - 2) // 2)
                for n in (14, 15):
                    store(n // 2 * P, n % 2, n)
                sp.wait_ge(og_out, 32 + 32 * GROUPS)
                for half in range(2):
                    sp.wait_ge(z_in[half], 16 * HEADS)

            @block.tensor
            def _(pe):
                def products(nt, outs):
                    slot, tile = nt // QT, nt % QT
                    for bank, at, w, mp, key in outs:
                        for first, q in ((True, q_a), (False, q_b)):
                            last = nc.tensor.matmul(ps[:, bank, at:at + w], q[:, slot, mp, tile * P:(tile + 1) * P],
                                                    k_s[:, slot, mp, key:key + w], start=first, stop=not first)
                    last.then_inc(s_ready, 1)

                def scores_first(t, nt):
                    pe.wait_ge(exp_done[0], t + 1)
                    products(nt, [(0, 0, BANK, 0, 0), (1, 0, BANK, 0, BANK)])

                def scores_rest(t, nt):
                    pe.wait_ge(exp_done[1], t + 1)
                    products(nt, [(2, 0, REST, 0, 2 * BANK), (2, REST, REST, 1, 0)])
                    products(nt, [(3, 0, BANK, 1, REST), (4, 0, BANK, 1, REST + BANK)])

                def product_v(gm, keys):
                    slot, half = (gm - 1) % 4 // 2, (gm - 1) % 2
                    for k in keys:
                        for v, a in ((v_hi, a_hi), (v_hi, a_lo), (v_lo, a_hi)):
                            last = nc.tensor.matmul(ps[:, BANK_PV, :], v[:, slot, k, :], a[:, half, k, :],
                                                    start=(k == 0 and v is v_hi and a is a_hi),
                                                    stop=(k == KEYT - 1 and v is v_lo))
                        if k == KEYT - 1:
                            last.then_inc(pv_ready, 1)

                def mean(n):
                    pe.wait_ge(sq_done, n + 1)
                    for j in range(GROUP):
                        last = nc.tensor.matmul(ps[:, BANK_MEAN, j:j + 1], square[:, j * P:(j + 1) * P],
                                                mean_w[:, 0:1], start=True, stop=True)
                    last.then_inc(mean_ready, 1)

                def spread(n):
                    pe.wait_ge(diag_done, n + 1)
                    nc.tensor.matmul(ps[:, BANK_SPREAD, :], keep.ones[:], square[:],
                                     start=True, stop=True).then_inc(spread_ready, 1)

                def group(g, gm):
                    for c in range(GROUP):
                        t = g * GROUP + c
                        pe.wait_ge(diff_done, t + 1)
                        transposes(g, c, 0)
                        transposes(g, c, 1)
                        if softmaxed(g, c):
                            scores_rest(t + 2, (gm * GROUP + c + 2) % (2 * QT))
                        transposes(g, c, 2)
                        if not early(g, 1):
                            if c == 0:
                                pe.wait_ge(gated_done, g)
                                if gm % 2 == 1:
                                    pe.wait_ge(v_in[gm // 2], v_loads(g))
                            product_v(gm, PV_KEYS[c])
                        if not (isinstance(g, int) and t + 3 >= TILES):
                            nt = (gm * GROUP + c + 3) % (2 * QT)
                            if nt % QT == 0:
                                pe.wait_ge(head_in[nt // QT], head_loads(g))
                            scores_first(t + 3, nt)
                        if c == 0 and not early(g, 2):
                            pe.wait_ge(t_lo_done, g * 12 + 2)
                            mean(g - 2)
                        if c == 2 and not early(g, 2):
                            pe.wait_ge(t_lo_done, g * 12 + 8)
                            spread(g - 2)

                def transposes(g, c, r):
                    at, n = ROUNDS[r]
                    if r < 2 and not (early(g, 1) and c == 0):
                        before = max(n for n in range(3) if BANK_T[c - 1][n] == BANK_T[c][r])
                        pe.wait_ge(t_lo_done, g * 12 + (3 * c - 2 + before))
                    if r == 2:
                        pe.wait_ge(t_lo_done, g * 12 + (3 * c + 1))
                    if r == 1 and c == 1 and not early(g, 2):
                        pe.wait_ge(var_done, g - 1)
                    if r == 1 and c == 3 and not early(g, 2):
                        pe.wait_ge(normed_done, g)
                    for k in range(n):
                        last = nc.tensor.transpose(ps[:, BANK_T[c][r], k * P:(k + 1) * P],
                                                   prob0[:, c, (at + k) * P:(at + k + 1) * P], keep.ident[:])
                    last.then_inc(t_ready, 1)

                def head_loads(g):
                    return IN_HEAD * ((g + 1) // 2 // 2 + 1) if isinstance(g, int) else head_count[0]

                def v_loads(g):
                    return IN_V * ((g - 1) // 4 + 1) if isinstance(g, int) else v_count[0]

                head_count, v_count = [None], [None]
                pe.wait_ge(head_in[0], IN_HEAD)
                pe.wait_ge(lam_step, 1)
                for t in range(2):
                    scores_first(t, t)
                    scores_rest(t, t)
                scores_first(2, 2)
                group(0, 0)
                group(1, 1)
                with pe.Fori(0, 3) as i:
                    head_count[0] = i * IN_HEAD + 2 * IN_HEAD
                    for b in range(4):
                        v_count[0] = i * IN_V + IN_V * (1 if b == 1 else 2)
                        group(i * 4 + (b + 2), (b + 2) % 4)
                for g in range(14, GROUPS):
                    group(g, g % 4)
                pe.wait_ge(gated_done, GROUPS)
                product_v(0, range(KEYT))
                pe.wait_ge(t_lo_done, 12 * GROUPS)
                mean(GROUPS - 2)
                pe.wait_ge(var_done, GROUPS - 1)
                spread(GROUPS - 2)
                pe.wait_ge(normed_done, GROUPS)
                mean(GROUPS - 1)
                pe.wait_ge(var_done, GROUPS)
                spread(GROUPS - 1)

            @block.gpsimd
            def _(pool):
                nc.gpsimd.memset(mean_w[:], 1.0 / DV).then_inc(lam_step, 1)

                def hold():
                    nc.gpsimd.tensor_add(hold_out[:], mean_w[:, 0:1], mean_w[:, 1:2])

                pool.wait_ge(lam_step, 1)

                def difference(t, p, p4):
                    pool.wait_ge(neg_done, t * 2 + 2)
                    hold()
                    nc.gpsimd.tensor_scalar(prob1[:, p, :], prob1[:, p, :], stat[:, p, 4:5], 1.0,
                                            ALU.mult, ALU.mult).then_inc(scaled, 1)
                    pool.wait_ge(scaled, t + 1)
                    nc.gpsimd.tensor_add(prob0[:, p4, :], prob0[:, p4, :], prob1[:, p, :]).then_inc(diff_done, 1)

                def diagonals(n):
                    pool.wait_ge(inv_rms_done, n + 1)
                    nc.gpsimd.tensor_tensor(square[:].rearrange("p (j q) -> p j q", j=GROUP),
                                            keep.ident[:].unsqueeze(1).broadcast_to([P, GROUP, P]),
                                            rms[:].unsqueeze(2).broadcast_to([P, GROUP, P]),
                                            ALU.mult).then_inc(diag_done, 1)

                def low_part(n):
                    pool.wait_ge(o_hi_done, n + 1)
                    nc.gpsimd.tensor_sub(normed[:].bitcast(F32R), normed[:], o_hi[:]).then_inc(o_lo_done, 1)

                difference(0, 0, 0)

                def group(g, gm):
                    for c in range(GROUP):
                        t = g * GROUP + c
                        if not (isinstance(g, int) and t + 1 >= TILES):
                            difference(t + 1, (c + 1) % 2, (c + 1) % 4)
                        if c == 1 and not early(g, 2):
                            diagonals(g - 2)
                        if c == 3 and not early(g, 2):
                            low_part(g - 2)

                run(pool, group)
                for n in (GROUPS - 2, GROUPS - 1):
                    diagonals(n)
                    low_part(n)

            @block.scalar
            def _(act):
                for n, s in enumerate((exp_done[0], exp_done[1])):
                    nc.scalar.activation(note[:, n:n + 1], keep.eps[:], ACT.Copy).then_inc(s, 1)
                nc.scalar.activation(note[:, 4:5], keep.eps[:], ACT.Copy).then_inc(og_out, 32)
                act.wait_ge(lam_step, 5)
                nc.scalar.activation(lam[:, 2:4], lam[:, 0:2], ACT.Exp).then_inc(lam_exp, 1)
                scores = ps[:, 0:5, :].rearrange("p b n -> p (b n)")

                def exponential0(t, p, t16, reused):
                    act.wait_ge(max_done[0], t + 1)
                    if reused is not None:
                        act.wait_ge(t_ready, reused)
                    nc.scalar.activation(prob0[:, t16 % 4, :], scores[:, 0:LT], ACT.Exp, bias=stat[:, p, 0:1],
                                         accum_out=sum0[:, t16 // 4, t16 % 4:t16 % 4 + 1]).then_inc(exp_done[0], 1)

                def exponential1(t, p):
                    act.wait_ge(max_done[1], t + 1)
                    if not (isinstance(t, int) and t < 2):
                        act.wait_ge(diff_done, t - 1)
                    nc.scalar.activation(prob1[:, p, :], scores[:, LT:2 * LT], ACT.Exp, bias=stat[:, p, 1:2],
                                         accum_out=stat[:, p, 2:3]).then_inc(exp_done[1], 1)

                def high(g, gm, c, r):
                    at, n = ROUNDS[r]
                    act.wait_ge(t_ready, g * 12 + (3 * c + r + 1))
                    nc.scalar.activation(a_hi[:, gm % 2, at:at + n, c * P:(c + 1) * P],
                                         ps[:, BANK_T[c][r], 0:n * P].rearrange("p (k q) -> p k q", k=n),
                                         ACT.Copy).then_inc(t_hi_done, 1)

                def squares(n):
                    act.wait_ge(pv_ready, n + 1)
                    act.wait_ge(normed_done, n + 1)
                    nc.scalar.activation(square[:], ps[:, BANK_PV, :], ACT.Square).then_inc(sq_done, 1)

                def root(n):
                    act.wait_ge(var_done, n + 1)
                    nc.scalar.activation(rms[:], rms[:], ACT.Sqrt).then_inc(rms_done, 1)
                    nc.scalar.activation(note[:, 5:6], keep.eps[:], ACT.Exp)

                def high_part(n):
                    act.wait_ge(normed_done, n + 2)
                    act.wait_ge(og_out, n * 32 + 32)
                    nc.scalar.activation(o_hi[:].bitcast(F32R), normed[:], ACT.Copy).then_inc(o_hi_done, 1)

                for t in range(2):
                    exponential0(t, t, t, None)
                    exponential1(t, t)

                def group(g, gm):
                    for c in range(GROUP):
                        t = g * GROUP + c
                        if c == 0 and not early(g, 2):
                            squares(g - 2)
                        high(g, gm, c, 0)
                        high(g, gm, c, 1)
                        if c == 1 and not early(g, 2):
                            root(g - 2)
                        if softmaxed(g, c):
                            reused = None if early(g, 1) and c < 2 else g * 12 + 3 * (c - 1)
                            exponential0(t + 2, c % 2, (gm * GROUP + c + 2) % 16, reused)
                        high(g, gm, c, 2)
                        if softmaxed(g, c):
                            exponential1(t + 2, c % 2)
                        if c == 2 and not early(g, 2):
                            high_part(g - 2)

                run(act, group)
                for n in (GROUPS - 2, GROUPS - 1):
                    squares(n)
                    root(n)
                    high_part(n)

            @block.vector
            def _(dve):
                dve.wait_ge(lam_loaded, 16)
                dve.wait_ge(lam_step, 1)
                for n in range(2):
                    nc.vector.tensor_mul(lam_in[:, 2 * n, :], lam_in[:, 2 * n, :],
                                         lam_in[:, 2 * n + 1, :]).then_inc(lam_step, 1)
                dve.wait_ge(lam_step, 3)
                for n in range(2):
                    nc.vector.tensor_reduce(lam[:, n:n + 1], lam_in[:, 2 * n, :], AX.X, ALU.add).then_inc(lam_step, 1)
                dve.wait_ge(lam_exp, 1)
                nc.vector.tensor_sub(lam[:, 4:5], lam[:, 3:4], lam[:, 2:3]).then_inc(lam_ready, 1)
                dve.wait_ge(lam_ready, 1)
                nc.vector.tensor_scalar_add(lam[:, 5:6], lam[:, 4:5], -LAMBDA_INIT).then_inc(lam_ready, 1)
                dve.wait_ge(lam_ready, 2)

                def peak_of(t, p, n):
                    dve.wait_ge(s_ready, t * 3 + (n + 1))
                    view, out = ((ps[:, 0:2, :].rearrange("p b n -> p (b n)"), peak[:, p, 0:1]),
                                 (ps[:, 2, :].rearrange("p (a n) -> p a n", a=2), peak[:, p, 2:4]),
                                 (ps[:, 3:5, :].rearrange("p b n -> p (b n)"), peak[:, p, 1:2]))[n]
                    nc.vector.tensor_reduce(out, view, AX.X, ALU.max, negate=True).then_inc(peak_done, 1)

                def maximum(t, p, mp):
                    peak_of(t, p, 1 + mp)
                    dve.wait_ge(peak_done, t * 3 + (mp + 2))
                    nc.vector.tensor_tensor(stat[:, p, mp:mp + 1], peak[:, p, mp:mp + 1],
                                            peak[:, p, 2 + mp:3 + mp], ALU.min).then_inc(max_done[mp], 1)

                def weight(t, p, t16):
                    dve.wait_ge(exp_done[1], t + 2)
                    nc.vector.reciprocal(stat[:, p, 3:4], stat[:, p, 2:3]).then_inc(neg_done, 1)
                    dve.wait_ge(neg_done, t * 2 + 1)
                    nc.vector.scalar_tensor_tensor(out=stat[:, p, 4:5], in0=stat[:, p, 3:4], scalar=lam[:, 5:6],
                                                   in1=sum0[:, t16 // 4, t16 % 4:t16 % 4 + 1], op0=ALU.mult,
                                                   op1=ALU.mult).then_inc(neg_done, 1)

                def low(g, gm, c, r):
                    at, n = ROUNDS[r]
                    dve.wait_ge(t_hi_done, g * 12 + (3 * c + r + 1))
                    nc.vector.tensor_sub(a_lo[:, gm % 2, at:at + n, c * P:(c + 1) * P],
                                         ps[:, BANK_T[c][r], 0:n * P].rearrange("p (k q) -> p k q", k=n),
                                         a_hi[:, gm % 2, at:at + n, c * P:(c + 1) * P].bitcast(F32)
                                         ).then_inc(t_lo_done, 1)

                def gate(n, half, loads):
                    dve.wait_ge(sq_done, n + 1)
                    dve.wait_ge(z_in[half], loads)
                    dve.wait_ge(normed_done, n + 1)
                    nc.vector.scalar_tensor_tensor(out=gated[:], in0=ps[:, BANK_PV, :], scalar=keep.subln[:],
                                                   in1=z_s[:, half, :], op0=ALU.mult,
                                                   op1=ALU.mult).then_inc(gated_done, 1)

                def eps_squares(n, gm):
                    nc.vector.scalar_tensor_tensor(out=eps_sq[:], in0=sum0[:, gm, :], scalar=EPS * RMS_SHRINK,
                                                   in1=sum0[:, gm, :], op0=ALU.mult, op1=ALU.mult).then_inc(eps_done, 1)

                def mean_squares(n):
                    dve.wait_ge(mean_ready, n + 1)
                    dve.wait_ge(eps_done, n + 1)
                    nc.vector.scalar_tensor_tensor(out=rms[:], in0=ps[:, BANK_MEAN, 0:GROUP], scalar=RMS_SHRINK,
                                                   in1=eps_sq[:], op0=ALU.mult, op1=ALU.add).then_inc(var_done, 1)

                def inverse_rms(n):
                    dve.wait_ge(rms_done, n + 1)
                    nc.vector.reciprocal(rms[:], rms[:]).then_inc(inv_rms_done, 1)

                def norm(n):
                    dve.wait_ge(spread_ready, n + 1)
                    dve.wait_ge(gated_done, n + 2)
                    dve.wait_ge(og_out, n * 32 + 32)
                    nc.vector.tensor_tensor(normed[:], gated[:], ps[:, BANK_SPREAD, :],
                                            ALU.mult).then_inc(normed_done, 1)

                nc.vector.tensor_scalar_mul(keep.subln[:], keep.vcol[:, V_SUBG:V_SUBG + 1],
                                            (1.0 - LAMBDA_INIT) * RMS_SHRINK ** 0.5).then_inc(lam_ready, 1)
                nc.vector.memset(note[:, 6:7], 0.0).then_inc(gated_done, 1)
                nc.vector.memset(note[:, 7:8], 0.0).then_inc(normed_done, 1)
                dve.wait_ge(lam_ready, 3)
                peak_of(0, 0, 0)
                maximum(0, 0, 0)
                maximum(0, 0, 1)
                weight(0, 0, 0)
                peak_of(1, 1, 0)
                maximum(1, 1, 0)
                maximum(1, 1, 1)
                peak_of(2, 0, 0)

                z_loads = [None]

                def group(g, gm):
                    for c in range(GROUP):
                        t = g * GROUP + c
                        if not (isinstance(g, int) and t + 1 >= TILES):
                            weight(t + 1, (c + 1) % 2, (gm * GROUP + c + 1) % 16)
                        low(g, gm, c, 0)
                        if c == 0 and not early(g, 2):
                            gate(g - 2, gm % 2, 16 * ((g - 2) // 2 + 1) if isinstance(g, int) else z_loads[0][gm])
                        if softmaxed(g, c):
                            maximum(t + 2, c % 2, 0)
                            maximum(t + 2, c % 2, 1)
                        low(g, gm, c, 1)
                        low(g, gm, c, 2)
                        if not (isinstance(g, int) and t + 3 >= TILES):
                            peak_of(t + 3, (c + 1) % 2, 0)
                        if c == 0 and not early(g, 2):
                            eps_squares(g - 2, (gm - 2) % 4)
                            mean_squares(g - 2)
                        if c == 2 and not early(g, 2):
                            norm(g - 2)
                        if c == 1 and not early(g, 2):
                            inverse_rms(g - 2)

                group(0, 0)
                group(1, 1)
                with dve.Fori(0, 3) as i:
                    z_loads[0] = {(b + 2) % 4: i * 32 + 16 * (b // 2 + 1) for b in range(4)}
                    for b in range(4):
                        group(i * 4 + (b + 2), (b + 2) % 4)
                for g in range(14, GROUPS):
                    group(g, g % 4)
                for n in (GROUPS - 2, GROUPS - 1):
                    gate(n, n % 2, 16 * (n // 2 + 1))
                    eps_squares(n, n % 4)
                    mean_squares(n)
                    inverse_rms(n)
                    norm(n)


def output(nc, io, keep, layer, src, weights, residual, dst, nxt):
    with ExitStack() as stack:
        m = Memory(nc, stack, f"out{layer}")
        split_here = keep.w_out is None
        if split_here:
            w_hi = m.sb("w_hi", [P, KT, D], F32R)
            w_lo = m.sb("w_lo", [P, KT, D], F32R)
            stage = m.sb("stage", [P, 4, D])
        else:
            w_hi, w_lo = keep.w_out
        s_hi = m.sb("s_hi", [P, 2, KT, P], F32R)
        s_lo = m.sb("s_lo", [P, 2, KT, P], F32R)
        res = m.sb("res", [P, 2, D])
        row = m.sb("row", [P, 2, D])
        done = m.sb("done", [P, 2, D])
        hf = m.sb("hf", [P, KT, P])
        ln_g = m.sb("ln_g", [P, D])
        ln_b = m.sb("ln_b", [P, D])
        stats = m.sb("stats", [P, 2, 2, 6])
        mv = m.sb("mv", [P, 2, 2])
        rstd = m.sb("rstd", [P, 2])
        note = m.sb("note", [P, 4])
        ps = m.psum("ps", [P, 8, BANK])

        row_in, proj_ready, prod_done, sum_done, stats_done, mv_done, std_done, rstd_done, centred, done_ready = (
            m.sem(n) for n in ("row_in", "proj_ready", "prod_done", "sum_done", "stats_done", "mv_done", "std_done",
                               "rstd_done", "centred", "done_ready"))
        if split_here:
            w_hi_done, w_lo_done = m.sem("w_hi_done"), m.sem("w_lo_done")
            stage_in = [m.sem(f"stage_in{n}") for n in range(4)]
        if nxt:
            t_ready, h_done, h_hi_done, h_lo_done = (m.sem(n) for n in ("t_ready", "h_done", "h_hi_done", "h_lo_done"))
        src_in = [m.sem("src_in0"), m.sem("src_in1")]
        res_in = [m.sem("res_in0"), m.sem("res_in1")]
        done_out = [m.sem("done_out0"), m.sem("done_out1")]

        def run(eng, tile):
            tile(0, 0, 0)
            with eng.Fori(0, 3) as i:
                tile(i * 2 + 1, i, 1)
                tile(i * 2 + 2, i + 1, 0)
            tile(QT - 1, 3, 1)

        with nc.Block() as block:
            @block.sync
            def _(sp):
                def load_tile(n, p):
                    cols = ds(n * P, P)
                    for part, buf in ((0, s_hi), (1, s_lo)):
                        view = src[part * D:(part + 1) * D, :].rearrange("(k p) t -> p k t", p=P)
                        sp.dma_start(buf[:, p, :, :].bitcast(F32), view[:, :, cols]).then_inc(src_in[p], 16)
                    sp.dma_start(res[:, p, :], residual[ds(n * P, P), :]).then_inc(res_in[p], 16)

                if not split_here:
                    load_tile(0, 0)
                for kt in range(KT if split_here else 0):
                    if kt >= 4:
                        sp.wait_ge(w_lo_done, kt - 3)
                    sp.dma_start(stage[:, kt % 4, :], weights[kt * P:(kt + 1) * P, :]).then_inc(stage_in[kt % 4], 16)
                    if kt == 1:
                        load_tile(0, 0)
                load_tile(1, 1)
                sp.dma_start(ln_g[:], io["ln_g"][layer:layer + 1, :].partition_broadcast(P)
                             .rearrange("p a n -> p (a n)")).then_inc(row_in, 16)
                sp.dma_start(ln_b[:], io["ln_b"][layer:layer + 1, :].partition_broadcast(P)
                             .rearrange("p a n -> p (a n)")).then_inc(row_in, 16)

                def tile(n, k, p):
                    if not (isinstance(n, int) and n == QT - 1):
                        sp.wait_ge(proj_ready, n + 1)
                        sp.wait_ge(sum_done, n + 1)
                        load_tile(n + 2, p)
                    sp.wait_ge(done_ready, n + 3)
                    sp.dma_start(dst[ds(n * P, P), :], done[:, p, :]).then_inc(done_out[p], 16)

                tile(0, 0, 0)
                with sp.Fori(0, 2) as i:
                    tile(i * 2 + 1, None, 1)
                    tile(i * 2 + 2, None, 0)
                tile(5, None, 1)
                for n in (6, 7):
                    sp.wait_ge(done_ready, n + 3)
                    sp.dma_start(dst[n * P:(n + 1) * P, :], done[:, n % 2, :]).then_inc(done_out[n % 2], 16)
                for p in range(2):
                    sp.wait_ge(done_out[p], 16 + 16 * QT // 2)

            @block.tensor
            def _(pe):
                def product(n, k, p):
                    pe.wait_ge(src_in[p], k * 32 + 32)
                    pe.wait_ge(prod_done, n + 1)
                    for kt in range(KT):
                        if split_here and isinstance(n, int) and n == 0:
                            pe.wait_ge(w_lo_done, kt + 1)
                        for s, parts in ((s_hi, (w_hi, w_lo)), (s_lo, (w_hi,))):
                            for w in parts:
                                for half in range(2):
                                    last = nc.tensor.matmul(
                                        ps[:, 2 * p + half, :], s[:, p, kt, :],
                                        w[:, kt, half * BANK:(half + 1) * BANK],
                                        start=(kt == 0 and s is s_hi and w is w_hi),
                                        stop=(kt == KT - 1 and s is s_lo))
                    last.then_inc(proj_ready, 1)

                def transposes(n, p):
                    pe.wait_ge(done_ready, n + 3)
                    pe.wait_ge(h_done, n + 1)
                    for kt in range(KT):
                        last = nc.tensor.transpose(ps[:, 4 + 2 * p + kt // 4, (kt % 4) * P:(kt % 4 + 1) * P],
                                                   done[:, p, kt * P:(kt + 1) * P], keep.ident[:])
                    last.then_inc(t_ready, 1)

                def tile(n, k, p):
                    product(n, k, p)
                    if nxt and not (isinstance(n, int) and n == 0):
                        transposes(n - 1, 1 - p)

                run(pe, tile)
                if nxt:
                    transposes(QT - 1, 1)

            @block.scalar
            def _(act):
                if nxt:
                    nc.scalar.activation(note[:, 0:1], keep.eps[:], ACT.Copy).then_inc(h_done, 2)
                    nc.scalar.activation(note[:, 1:2], keep.eps[:], ACT.Copy).then_inc(t_ready, 2)
                for p in range(2):
                    nc.scalar.activation(done[:, p, 0:1], keep.eps[:], ACT.Copy).then_inc(done_out[p], 16)
                for kt in range(KT if split_here else 0):
                    act.wait_ge(stage_in[kt % 4], 16 * (kt // 4 + 1))
                    nc.scalar.activation(w_hi[:, kt, :], stage[:, kt % 4, :], ACT.Copy).then_inc(w_hi_done, 1)

                def tile(n, k, p):
                    act.wait_ge(mv_done, n + 1)
                    nc.scalar.activation(rstd[:, p:p + 1], mv[:, p, 1:2], ACT.Sqrt,
                                         bias=keep.eps[:]).then_inc(std_done, 1)
                    if nxt and not (isinstance(n, int) and n == 0):
                        modulate(n - 1, 1 - p)

                def modulate(n, p):
                    act.wait_ge(t_ready, n + 3)
                    act.wait_ge(h_lo_done, n + 1)
                    for kt in range(KT):
                        last = nc.scalar.activation(
                            hf[:, kt, :], ps[:, 4 + 2 * p + kt // 4, (kt % 4) * P:(kt % 4 + 1) * P], ACT.Identity,
                            bias=keep.mod1[:, 0, kt:kt + 1], scale=keep.mod1[:, 1, kt:kt + 1])
                    last.then_inc(h_done, 1)
                    act.wait_ge(h_done, n + 3)
                    nc.scalar.activation(keep.h_hi[:, :, ds(n * P, P)], hf[:], ACT.Copy).then_inc(h_hi_done, 1)

                run(act, tile)
                if nxt:
                    modulate(QT - 1, 1)

            @block.vector
            def _(dve):
                nc.vector.memset(stats[:, 0, 0, 0:1], 0.0).then_inc(prod_done, 2)
                if nxt:
                    nc.vector.memset(stats[:, 0, 0, 1:2], 0.0).then_inc(h_lo_done, 1)
                nc.vector.memset(stats[:, 0, 0, 2:3], 0.0).then_inc(done_ready, 2)
                for kt in range(KT if split_here else 0):
                    dve.wait_ge(w_hi_done, kt + 1)
                    nc.vector.tensor_sub(w_lo[:, kt, :], stage[:, kt % 4, :],
                                         w_hi[:, kt, :].bitcast(F32)).then_inc(w_lo_done, 1)

                def tile(n, k, p):
                    dve.wait_ge(proj_ready, n + 1)
                    dve.wait_ge(done_ready, n + 1)
                    two = row[:, p, :].rearrange("p (b n) -> p b n", b=2)
                    gate = keep.gate[:, layer, :].rearrange("p (b n) -> p b n", b=2)
                    nc.vector.tensor_tensor(two, ps[:, 2 * p:2 * p + 2, :], gate, ALU.mult).then_inc(prod_done, 1)
                    dve.wait_ge(res_in[p], k * 16 + 16)
                    dve.wait_ge(prod_done, n + 3)
                    nc.vector.scalar_tensor_tensor(out=row[:, p, :], in0=res[:, p, :], scalar=ALPHA, in1=row[:, p, :],
                                                   op0=ALU.mult, op1=ALU.add).then_inc(sum_done, 1)
                    dve.wait_ge(sum_done, n + 1)
                    for half in range(2):
                        nc.vector.bn_stats(stats[:, p, half, :],
                                           row[:, p, half * BANK:(half + 1) * BANK]).then_inc(stats_done, 1)
                    dve.wait_ge(stats_done, n * 2 + 2)
                    nc.vector.memset(note[:, 3:4], 0.0)
                    nc.vector.bn_aggr(mv[:, p, :], stats[:, p, :, :].rearrange("p a b -> p (a b)")).then_inc(mv_done, 1)
                    if isinstance(n, int) and n == 0:
                        dve.wait_ge(row_in, 32)
                    dve.wait_ge(mv_done, n + 1)
                    nc.vector.scalar_tensor_tensor(out=row[:, p, :], in0=row[:, p, :], scalar=mv[:, p, 0:1],
                                                   in1=ln_g[:], op0=ALU.subtract, op1=ALU.mult).then_inc(centred, 1)
                    dve.wait_ge(std_done, n + 1)
                    nc.vector.reciprocal(rstd[:, p:p + 1], rstd[:, p:p + 1]).then_inc(rstd_done, 1)
                    dve.wait_ge(rstd_done, n + 1)
                    dve.wait_ge(centred, n + 1)
                    dve.wait_ge(done_out[p], k * 16 + 16)
                    if nxt:
                        dve.wait_ge(t_ready, n + 1)
                    nc.vector.scalar_tensor_tensor(out=done[:, p, :], in0=row[:, p, :], scalar=rstd[:, p:p + 1],
                                                   in1=ln_b[:], op0=ALU.mult, op1=ALU.add).then_inc(done_ready, 1)
                    if nxt and not (isinstance(n, int) and n == 0):
                        low(n - 1)

                def low(n):
                    dve.wait_ge(h_hi_done, n + 1)
                    nc.vector.tensor_sub(keep.h_lo[:, :, ds(n * P, P)], hf[:],
                                         keep.h_hi[:, :, ds(n * P, P)].bitcast(F32)).then_inc(h_lo_done, 1)

                run(dve, tile)
                if nxt:
                    low(QT - 1)


def conform(nc, io, keep):
    with ExitStack() as outer:
        mo = Memory(nc, outer, "cf")
        conv = mo.sb("conv", [P, KT, L])
        z_s = mo.sb("z_s", [P, KT, L])
        total = mo.sb("total", [P, L])
        mean_w = mo.sb("mean_w", [P, P])
        ps = mo.psum("ps", [P, 8, BANK])
        with ExitStack() as stack:
            m = Memory(nc, stack, "cg")
            w_hi = m.sb("w_hi", [P, 3, PIECE], F32R)
            w_lo = m.sb("w_lo", [P, 3, PIECE], F32R)
            stage = m.sb("stage", [P, 2, PIECE])
            padded = m.sb("padded", [P, 2, L + 2 * PAD])
            sig = m.sb("sig", [P, L])
            odd = m.sb("odd", [P, L])
            prod = m.sb("prod", [P, 2, L])
            extra = m.sb("extra", [P, L])
            hold_out = m.sb("hold_out", [P, 1])
            taps = m.sb("taps", [P, KT * CONF_KW])
            note = m.sb("note", [P, 4])
            (tap_in, w_hi_done, w_lo_done, g_ready, a_ready, z_ready, sig_done, glu_done, z_done, conv_step,
             total_done, pad_done, prod_done, add_done, extra_done) = (m.sem(n) for n in (
                 "tap_in", "w_hi_done", "w_lo_done", "g_ready", "a_ready", "z_ready", "sig_done", "glu_done",
                 "z_done", "conv_step", "total_done", "pad_done", "prod_done", "add_done", "extra_done"))
            stage_in = [m.sem("stage_in0"), m.sem("stage_in1")]
            TAPS_D = 24
            TAPS_A = CONF_KW - TAPS_D
            ADDS = TAPS_A - 1
            STEPS = TAPS_D + 1

            with nc.Block() as block:
                @block.sync
                def _(sp):
                    for g in range(2):
                        sp.dma_start(stage[:, g, :], io["conf_w"][g * P:(g + 1) * P, :]).then_inc(stage_in[g], 16)
                    sp.dma_start(taps[:], io["taps"]).then_inc(tap_in, 16)
                    with sp.Fori(0, 11) as i:
                        for b in range(2):
                            sp.wait_ge(w_lo_done, i * 2 + (b + 1))
                            sp.dma_start(stage[:, b, :],
                                         io["conf_w"][ds(i * (2 * P) + (2 + b) * P, P), :]).then_inc(stage_in[b], 16)

                @block.tensor
                def _(pe):
                    def part(c, kind, ready, free):
                        pe.wait_ge(w_lo_done, c * 3 + (kind + 1))
                        pe.wait_ge(free, c + 1)
                        for kt in range(KT):
                            for w, parts in ((w_hi, (keep.h_hi, keep.h_lo)), (w_lo, (keep.h_hi,))):
                                for h in parts:
                                    for half in range(2):
                                        last = nc.tensor.matmul(
                                            ps[:, 2 * kind + half, :], w[:, kind, kt * P:(kt + 1) * P],
                                            h[:, kt, half * BANK:(half + 1) * BANK],
                                            start=(kt == 0 and w is w_hi and h is keep.h_hi),
                                            stop=(kt == KT - 1 and w is w_lo))
                        last.then_inc(ready, 1)

                    with pe.Fori(0, KT) as c:
                        part(c, 0, g_ready, sig_done)
                        part(c, 1, a_ready, glu_done)
                        part(c, 2, z_ready, z_done)

                @block.scalar
                def _(act):
                    for n, s in enumerate((sig_done, z_done)):
                        nc.scalar.activation(note[:, n:n + 1], keep.eps[:], ACT.Copy).then_inc(s, 1)

                    def split(g, slot, kind, loads):
                        act.wait_ge(stage_in[slot], loads * 16)
                        nc.scalar.activation(w_hi[:, kind, :], stage[:, slot, :], ACT.Copy).then_inc(w_hi_done, 1)

                    def tile(c, n, following):
                        act.wait_ge(g_ready, c + 1)
                        act.wait_ge(glu_done, c + 1)
                        nc.scalar.activation(sig[:].rearrange("p (b n) -> p b n", b=2), ps[:, 0:2, :],
                                             ACT.Sigmoid).then_inc(sig_done, 1)
                        if following:
                            piece(c, n, 0)
                            act.wait_ge(a_ready, c + 1)
                            piece(c, n, 1)
                        act.wait_ge(glu_done, c + 2)
                        for k in range(TAPS_A):
                            act.wait_ge(add_done, c * ADDS + (1 + (max(1, k - 2) if k >= 2 else 0)))
                            nc.scalar.activation(prod[:, k % 2, :], padded[:, n, TAPS_D + k:TAPS_D + k + L], ACT.Copy,
                                                 scale=taps[:, ds(c * CONF_KW + (TAPS_D + k), 1)]
                                                 ).then_inc(prod_done, 1)
                        act.wait_ge(z_ready, c + 1)
                        nc.scalar.activation(z_s[:, ds(c, 1), :].rearrange("p a (b n) -> p (a b) n", b=2),
                                             ps[:, 4:6, :], ACT.Silu).then_inc(z_done, 1)
                        if following:
                            piece(c, n, 2)

                    def piece(c, n, kind):
                        g = 3 * n + 3 + kind
                        i = (c - n) // 2 if isinstance(c, int) else half_c[0]
                        split(None, g % 2, kind, i * 3 + (g // 2 + 1))

                    half_c = [None]
                    nc.scalar.activation(prod[:, 0, 0:1], keep.eps[:], ACT.Copy).then_inc(prod_done, 2 * TAPS_A)
                    act.wait_ge(prod_done, 2 * TAPS_A)
                    act.wait_ge(tap_in, 16)
                    for g in range(3):
                        split(g, g % 2, g, g // 2 + 1)
                    with act.Fori(0, 3) as i:
                        half_c[0] = i
                        tile(i * 2, 0, True)
                        tile(i * 2 + 1, 1, True)
                    tile(6, 0, True)
                    tile(7, 1, False)

                @block.gpsimd
                def _(pool):
                    nc.gpsimd.memset(mean_w[:], 1.0 / D)
                    nc.gpsimd.memset(total[:], 0.0).then_inc(total_done, 1)
                    pool.wait_ge(total_done, 1)
                    nc.gpsimd.memset(extra[:, 0:1], 0.0).then_inc(add_done, 1)

                    def low(g, slot, kind):
                        pool.wait_ge(w_hi_done, g + 1)
                        nc.gpsimd.tensor_sub(w_lo[:, kind, :], stage[:, slot, :],
                                             w_hi[:, kind, :].bitcast(F32)).then_inc(w_lo_done, 1)

                    def hold():
                        nc.gpsimd.tensor_add(hold_out[:], mean_w[:, 0:1], mean_w[:, 1:2])

                    def add_total(c):
                        pool.wait_ge(conv_step, c * STEPS)
                        pool.wait_ge(add_done, c * ADDS + 1)
                        hold()
                        last = conv[:, ds(c - 1, 1), :].rearrange("p a n -> p (a n)")
                        nc.gpsimd.tensor_add(last, last, extra[:]).then_inc(extra_done, 1)
                        pool.wait_ge(extra_done, c)
                        pool.wait_ge(total_done, c)
                        hold()
                        nc.gpsimd.tensor_add(total[:], total[:],
                                             conv[:, ds(c - 1, 1), :].rearrange("p a n -> p (a n)")
                                             ).then_inc(total_done, 1)

                    for g in range(3):
                        low(g, g % 2, g)

                    def add_products(c):
                        for j in range(ADDS):
                            pool.wait_ge(prod_done, c * TAPS_A + (2 * TAPS_A + j + 2))
                            if j == 0:
                                if not (isinstance(c, int) and c == 0):
                                    pool.wait_ge(extra_done, c)
                                nc.gpsimd.tensor_add(extra[:], prod[:, 0, :], prod[:, 1, :]).then_inc(add_done, 1)
                            else:
                                pool.wait_ge(add_done, c * ADDS + (1 + j))
                                nc.gpsimd.tensor_add(extra[:], extra[:], prod[:, (j + 1) % 2, :]).then_inc(add_done, 1)

                    def tile(c, n):
                        for kind in range(2):
                            low(c * 3 + (3 + kind), (3 * n + 3 + kind) % 2, kind)
                        if not (isinstance(c, int) and c == 0):
                            add_total(c)
                        add_products(c)
                        low(c * 3 + 5, (3 * n + 5) % 2, 2)

                    tile(0, 0)
                    with pool.Fori(0, 3) as i:
                        tile(i * 2 + 1, 1)
                        tile(i * 2 + 2, 0)
                    add_total(7)
                    add_products(7)
                    add_total(8)

                @block.vector
                def _(dve):
                    nc.vector.memset(padded[:, :, 0:PAD], 0.0)
                    nc.vector.memset(padded[:, :, PAD + L:], 0.0).then_inc(pad_done, 1)
                    nc.vector.memset(odd[:, 0:1], 0.0).then_inc(glu_done, 1)
                    dve.wait_ge(tap_in, 16)
                    dve.wait_ge(pad_done, 1)

                    def tile(c, q):
                        dve.wait_ge(prod_done, c * TAPS_A + TAPS_A)
                        dve.wait_ge(a_ready, c + 1)
                        dve.wait_ge(sig_done, c + 2)
                        nc.vector.tensor_tensor(padded[:, q, PAD:PAD + L].rearrange("p (b n) -> p b n", b=2),
                                                ps[:, 2:4, :], sig[:].rearrange("p (b n) -> p b n", b=2),
                                                ALU.mult).then_inc(glu_done, 1)
                        dve.wait_ge(glu_done, c + 2)
                        even = conv[:, ds(c, 1), :].rearrange("p a n -> p (a n)")

                        def tap(k):
                            return taps[:, ds(c * CONF_KW + k, 1)]

                        nc.vector.tensor_scalar(even, padded[:, q, 0:L], tap(0), keep.vcol[:, ds(c + V_DWB, 1)],
                                                ALU.mult, ALU.add).then_inc(conv_step, 1)
                        nc.vector.tensor_scalar(odd[:], padded[:, q, 1:1 + L], tap(1), None,
                                                ALU.mult).then_inc(conv_step, 1)
                        for k in range(2, TAPS_D):
                            dve.wait_ge(conv_step, c * STEPS + (k - 1))
                            into = even if k % 2 == 0 else odd[:]
                            nc.vector.scalar_tensor_tensor(out=into, in0=padded[:, q, k:k + L], scalar=tap(k),
                                                           in1=into, op0=ALU.mult, op1=ALU.add).then_inc(conv_step, 1)
                        dve.wait_ge(conv_step, c * STEPS + TAPS_D)
                        nc.vector.tensor_add(even, even, odd[:]).then_inc(conv_step, 1)
                        dve.wait_ge(conv_step, c * STEPS + STEPS)

                    with dve.Fori(0, KT // 2) as i:
                        tile(i * 2, 0)
                        tile(i * 2 + 1, 1)

        with ExitStack() as stack:
            keep.w_out = w_hi, w_lo = keep.h_hi, keep.h_lo
            m = Memory(nc, stack, "cn")
            stage = m.sb("stage", [P, 4, D])
            square = m.sb("square", [P, 2, L])
            rstd = m.sb("rstd", [P, L])
            y_hi = m.sb("y_hi", [P, 2, L])
            y_lo = m.sb("y_lo", [P, 2, L])
            (mean_ready, centred, sq_done, sq_used, std_done, rstd_done, scaled, act_done, gated, y_hi_done,
             y_lo_done) = (m.sem(n) for n in ("mean_ready", "centred", "sq_done", "sq_used", "std_done", "rstd_done",
                                              "scaled", "act_done", "gated", "y_hi_done", "y_lo_done"))
            y_out = [m.sem("y_out0"), m.sem("y_out1")]
            stage_in = [m.sem(f"stage_in{n}") for n in range(4)]
            w_hi_done, w_lo_done = m.sem("w_hi_done"), m.sem("w_lo_done")

            with nc.Block() as block:
                @block.tensor
                def _(pe):
                    for half in range(2):
                        last = nc.tensor.matmul(ps[:, half, :], mean_w[:], total[:, half * BANK:(half + 1) * BANK],
                                                start=True, stop=True)
                    last.then_inc(mean_ready, 1)
                    for c in range(KT):
                        pe.wait_ge(sq_done, c + 1)
                        for half in range(2):
                            last = nc.tensor.matmul(ps[:, 2 + half, :], mean_w[:],
                                                    square[:, c % 2, half * BANK:(half + 1) * BANK],
                                                    start=c == 0, stop=c == KT - 1)
                        last.then_inc(sq_used, 1)

                @block.vector
                def _(dve):
                    dve.wait_ge(mean_ready, 1)
                    for c in range(KT):
                        two = conv[:, c, :].rearrange("p (b n) -> p b n", b=2)
                        nc.vector.tensor_tensor(two, two, ps[:, 0:2, :], ALU.subtract).then_inc(centred, 1)
                    for kt in range(KT):
                        dve.wait_ge(w_hi_done, kt + 1)
                        nc.vector.tensor_sub(w_lo[:, kt, :], stage[:, kt % 4, :],
                                             w_hi[:, kt, :].bitcast(F32)).then_inc(w_lo_done, 1)
                    dve.wait_ge(centred, KT)
                    dve.wait_ge(std_done, 1)
                    nc.vector.reciprocal(rstd[:], rstd[:]).then_inc(rstd_done, 1)
                    dve.wait_ge(rstd_done, 1)

                    def low(c):
                        dve.wait_ge(y_hi_done, c + 1)
                        nc.vector.tensor_sub(y_lo[:, c % 2, :].bitcast(F32R), conv[:, c, :],
                                             y_hi[:, c % 2, :]).then_inc(y_lo_done, 1)

                    for c in range(KT):
                        nc.vector.tensor_mul(conv[:, c, :], conv[:, c, :], rstd[:]).then_inc(scaled, 1)
                        if c >= 3:
                            low(c - 3)
                    for c in range(KT - 3, KT):
                        low(c)

                @block.scalar
                def _(act):
                    for c in range(KT):
                        act.wait_ge(centred, c + 1)
                        if c >= 2:
                            act.wait_ge(sq_used, c - 1)
                        nc.scalar.activation(square[:, c % 2, :], conv[:, c, :], ACT.Square).then_inc(sq_done, 1)
                        act.wait_ge(stage_in[c % 4], 16 * (c // 4 + 1))
                        nc.scalar.activation(w_hi[:, c, :], stage[:, c % 4, :], ACT.Copy).then_inc(w_hi_done, 1)
                    act.wait_ge(sq_used, KT)
                    nc.scalar.activation(rstd[:].rearrange("p (b n) -> p b n", b=2), ps[:, 2:4, :], ACT.Sqrt,
                                         bias=keep.eps[:]).then_inc(std_done, 1)

                    def high(c):
                        act.wait_ge(gated, c + 1)
                        if c >= 2:
                            act.wait_ge(y_out[c % 2], 32 * (c // 2))
                        nc.scalar.activation(y_hi[:, c % 2, :].bitcast(F32R), conv[:, c, :],
                                             ACT.Copy).then_inc(y_hi_done, 1)

                    for c in range(KT):
                        act.wait_ge(scaled, c + 1)
                        nc.scalar.activation(conv[:, c, :], conv[:, c, :], ACT.Silu,
                                             scale=keep.vcol[:, V_CLNG + c:V_CLNG + c + 1],
                                             bias=keep.vcol[:, V_CLNB + c:V_CLNB + c + 1]).then_inc(act_done, 1)
                        if c >= 2:
                            high(c - 2)
                    for c in range(KT - 2, KT):
                        high(c)

                @block.gpsimd
                def _(pool):
                    for c in range(KT):
                        pool.wait_ge(act_done, c + 1)
                        nc.gpsimd.tensor_mul(conv[:, c, :], conv[:, c, :], z_s[:, c, :]).then_inc(gated, 1)

                @block.sync
                def _(sp):
                    for kt in range(KT):
                        if kt >= 4:
                            sp.wait_ge(w_lo_done, kt - 3)
                        sp.dma_start(stage[:, kt % 4, :],
                                     io["conf_w_out"][kt * P:(kt + 1) * P, :]).then_inc(stage_in[kt % 4], 16)
                    for c in range(KT):
                        sp.wait_ge(y_lo_done, c + 1)
                        for part, buf in ((0, y_hi), (1, y_lo)):
                            sp.dma_start(io["y_hl"][part * D + c * P:part * D + (c + 1) * P, :],
                                         buf[:, c % 2, :]).then_inc(y_out[c % 2], 16)
                    for p in range(2):
                        sp.wait_ge(y_out[p], 32 * KT // 2)


class Keep:
    pass


def build(nc, io, out):
    with ExitStack() as stack:
        m = Memory(nc, stack, "keep")
        keep = Keep()
        keep.vcol = m.sb("vcol", [P, V_N])
        keep.gate = m.sb("gate", [P, DEPTH, D])
        keep.mod1 = m.sb("mod1", [P, 2, KT])
        keep.ones = m.sb("ones", [P, P])
        keep.ident = m.sb("ident", [P, P])
        keep.eps = m.sb("eps", [P, 1])
        keep.subln = m.sb("subln", [P, 1])
        project(nc, io, keep)
        attend(nc, io, keep)
        keep_h = Memory(nc, stack, "h")
        keep.h_hi = keep_h.sb("hi", [P, KT, L], F32R)
        keep.h_lo = keep_h.sb("lo", [P, KT, L], F32R)
        keep.w_out = None
        output(nc, io, keep, 0, io["og_hl"], io["attn_w_out"], io["x"], io["x1"], True)
        conform(nc, io, keep)
        output(nc, io, keep, 1, io["y_hl"], io["conf_w_out"], io["x1"], out, False)


def rope_tables():
    import numpy as np
    half = DK // 2
    inv = (1.0 / (np.float32(10000.0) ** (np.arange(0, half, 2, dtype=np.float32) / half))).astype(np.float32)
    t = np.arange(L)
    ar = (t // 64).astype(np.float32)[:, None] * inv[None, :]
    ac = (t % 64).astype(np.float32)[:, None] * inv[None, :]
    ang = np.concatenate([ar, ar, ac, ac], axis=-1)
    sign = np.where(np.arange(DK) % half < half // 2, -1.0, 1.0).astype(np.float32)
    cos, sin = np.cos(ang), np.sin(ang) * sign
    both = np.concatenate([cos.T, sin.T], axis=1)
    return np.ascontiguousarray(np.concatenate([both, both], axis=0).astype(np.float32))


def kernel(x, c, ctx, c_ctx, mod_w, mod_b, ln_g, ln_b,
           attn_w_in, attn_w_out, attn_lambda_q1, attn_lambda_k1, attn_lambda_q2, attn_lambda_k2, attn_subln_g,
           conf_w_in, conf_dw_w, conf_dw_b, conf_ln_g, conf_ln_b, conf_w_out,
           sc_w_in, sc_conv_w, sc_w_out,
           pool_w_in, pool_w_group, pool_scale, pool_w_out):
    import numpy as np
    import concourse.bacc as bacc
    from concourse.bass_utils import run_bass_kernel_spmd

    a = lambda v: np.asarray(v)
    tokens = np.concatenate([a(x)[0], a(ctx)[0]], axis=0)
    cols = [a(c)[0], a(c_ctx), a(mod_b).reshape(-1), a(conf_dw_b)[0], a(conf_ln_g)[0], a(conf_ln_b)[0],
            a(attn_subln_g)[0]]
    vec = np.concatenate([v.reshape(-1, P) for v in cols], axis=0).T

    def pieces(w):
        n = w.shape[1] // P
        return w.reshape(KT, P, n, P).transpose(2, 1, 0, 3).reshape(n, P, PIECE)

    w_in = a(attn_w_in)[0]
    v_w = w_in[:, 2 * D:3 * D].reshape(4, 2, P, 2, BANK)
    v_w = v_w.transpose(3, 0, 2, 1, 4).reshape(8, P, PIECE)
    w_in = np.concatenate([pieces(w_in[:, :2 * D]), pieces(w_in[:, 3 * D:]), v_w], axis=0)
    conf = pieces(a(conf_w_in)[0]).reshape(3, KT, P, PIECE)
    conf = conf[[1, 0, 2]].transpose(1, 0, 2, 3).reshape(3 * KT * P, PIECE)
    taps = a(conf_dw_w)[0].reshape(CONF_KW, KT, P).transpose(2, 1, 0).reshape(P, KT * CONF_KW)
    arrays = {
        "x": a(x)[0], "x_t": tokens.T.reshape(KT, P, LT), "vec": vec, "mod_w": a(mod_w), "mod_b": a(mod_b),
        "ln_g": a(ln_g), "ln_b": a(ln_b), "w_in": w_in, "attn_w_out": a(attn_w_out)[0],
        "lam": np.stack([a(v)[0] for v in (attn_lambda_q1, attn_lambda_k1, attn_lambda_q2, attn_lambda_k2)])[None],
        "rope": rope_tables(), "conf_w": conf, "taps": taps, "conf_w_out": a(conf_w_out)[0],
    }
    arrays = {k: np.ascontiguousarray(v) for k, v in arrays.items()}
    nc = bacc.Bacc("TRN2", target_bir_lowering=False, num_devices=1)
    io = {k: nc.dram_tensor(f"in_{k}", v.shape, mybir.dt.from_np(v.dtype), kind="ExternalInput").ap()
          for k, v in arrays.items()}
    for name, shape in (("q_hl", (HEADS * 2 * P, L)), ("k_hl", (HEADS * 2 * P, LT)), ("v_hl", (2, KEYT, P, D)),
                        ("z_s", (D, L)), ("og_hl", (2 * D, L)), ("x1", (L, D)), ("y_hl", (2 * D, L))):
        io[name] = nc.dram_tensor(f"scratch_{name}", shape, F32, kind="Internal").ap()
    out = nc.dram_tensor("out", (L, D), F32, kind="ExternalOutput").ap()
    build(nc, io, out)
    r = run_bass_kernel_spmd(nc, [{f"in_{k}": v for k, v in arrays.items()}], core_ids=[0])
    return r.results[0]["out"].reshape(1, L, D)
```
